# Optimizing a Trainium2 kernel written in Bass

```python
import jax, jax.numpy as jnp
from jax import lax
import numpy as np
import math

D_MODEL = 1024
BATCH = 1
SEQ = 1024
DEPTH = 1

HEAD_DIM = 64
A_HEADS = 8
B_HEADS = 8
IDX_HEADS = 8
IDX_DIM = 64
DILATED_PATTERNS = ((128, 1), (512, 4), (2048, 16))
TOPK_MAX = 256
D_A = A_HEADS * HEAD_DIM
D_B = B_HEADS * HEAD_DIM
D_FF = ((8 * D_MODEL + 767) // 768) * 256
ROPE_THETA = 10000.0
RMS_EPS = 1e-6
BLOCK = 128
ATTN_SCALE = HEAD_DIM ** -0.5
IDX_SCALE = (IDX_DIM ** -0.5) * (IDX_HEADS ** -0.5)
IN_SPLITS = (D_A, D_A, D_A, D_B, HEAD_DIM, HEAD_DIM, IDX_HEADS * IDX_DIM, IDX_DIM, IDX_HEADS, D_MODEL, D_MODEL)
IN_OFFSETS = tuple(int(o) for o in np.cumsum(IN_SPLITS)[:-1])
D_IN = int(sum(IN_SPLITS))


def rmsnorm(x, g):
    x32 = x.astype(jnp.float32)
    y = x32 * lax.rsqrt(jnp.mean(x32 * x32, axis=-1, keepdims=True) + RMS_EPS)
    return (y * g.astype(jnp.float32)).astype(x.dtype)

def rope(z, pos):
    half = z.shape[-1] // 2
    inv_freq = ROPE_THETA ** (-jnp.arange(half, dtype=jnp.float32) / half)
    ang = pos.astype(jnp.float32)[:, None] * inv_freq[None, :]
    cos = jnp.cos(ang)[None, :, None, :]
    sin = jnp.sin(ang)[None, :, None, :]
    z32 = z.astype(jnp.float32)
    z1, z2 = z32[..., :half], z32[..., half:]
    return jnp.concatenate([z1 * cos - z2 * sin, z2 * cos + z1 * sin], axis=-1).astype(z.dtype)

def dilated_window_attention(q, k, v, window, dilation):
    B, T, H, hd = q.shape
    steps = window // dilation
    seg = dilation * BLOCK
    t_pad = -(-T // seg) * seg
    m_len = t_pad // dilation
    nb = m_len // BLOCK

    def to_blocks(z):
        z = jnp.pad(z, ((0, 0), (0, t_pad - T), (0, 0), (0, 0)))
        z = z.reshape(B, m_len, dilation, H, hd).transpose(0, 2, 3, 1, 4)
        return z.reshape(B, dilation, H, nb, BLOCK, hd)

    qb, kb, vb = to_blocks(q), to_blocks(k), to_blocks(v)

    def with_prev(z):
        prev = jnp.pad(z[:, :, :, :-1], ((0, 0), (0, 0), (0, 0), (1, 0), (0, 0), (0, 0)))
        return jnp.concatenate([prev, z], axis=4)

    k2, v2 = with_prev(kb), with_prev(vb)
    s = jnp.einsum('brhnqd,brhnkd->brhnqk', qb, k2).astype(jnp.float32) * ATTN_SCALE
    qi = jnp.arange(BLOCK)[:, None]
    kj = jnp.arange(2 * BLOCK)[None, :]
    dist = qi + BLOCK - kj
    band = (dist >= 0) & (dist <= steps)
    has_prev = (jnp.arange(nb)[:, None, None] > 0) | (kj >= BLOCK)[None]
    mask = band[None] & has_prev
    s = jnp.where(mask, s, -jnp.inf)
    m = jnp.max(s, axis=-1, keepdims=True)
    p = jnp.exp(s - m)
    den = jnp.sum(p, axis=-1, keepdims=True)
    o = jnp.einsum('brhnqk,brhnkd->brhnqd', p.astype(v.dtype), v2).astype(jnp.float32) / den
    lse = (m + jnp.log(den))[..., 0]
    o = o.reshape(B, dilation, H, m_len, hd).transpose(0, 3, 1, 2, 4).reshape(B, t_pad, H, hd)[:, :T]
    lse = lse.reshape(B, dilation, H, m_len).transpose(0, 3, 1, 2).reshape(B, t_pad, H)[:, :T]
    return o, lse

def dilated_mixture(q, k, v):
    outs, lses = [], []
    for window, dilation in DILATED_PATTERNS:
        o, l = dilated_window_attention(q, k, v, window, dilation)
        outs.append(o)
        lses.append(l)
    w = jax.nn.softmax(jnp.stack(lses, axis=0), axis=0)
    return jnp.sum(w[..., None] * jnp.stack(outs, axis=0), axis=0)

def indexed_sparse_attention(q, k, v, qi, ki, wi):
    B, T, H, hd = q.shape
    topk = min(TOPK_MAX, T // 4)
    nb = T // BLOCK
    key_pos = jnp.arange(T)

    def blocks(z):
        return jnp.moveaxis(z.reshape((B, nb, BLOCK) + z.shape[2:]), 1, 0)

    def one_block(args):
        q_blk, qi_blk, wi_blk, start = args
        q_pos = start + jnp.arange(BLOCK)
        causal = key_pos[None, :] <= q_pos[:, None]
        dots = jnp.einsum('bqhd,bsd->bqhs', qi_blk, ki).astype(jnp.float32)
        score = jnp.einsum('bqh,bqhs->bqs', wi_blk.astype(jnp.float32), jax.nn.relu(dots)) * IDX_SCALE
        score = jnp.where(causal[None], score, -jnp.inf)
        _, sel = lax.top_k(score, topk)
        valid = sel <= q_pos[None, :, None]
        k_sel = jax.vmap(lambda kk, ii: kk[ii])(k, sel)
        v_sel = jax.vmap(lambda vv, ii: vv[ii])(v, sel)
        s = jnp.einsum('bqhd,bqkd->bhqk', q_blk, k_sel).astype(jnp.float32) * ATTN_SCALE
        s = jnp.where(valid[:, None], s, -jnp.inf)
        p = jax.nn.softmax(s, axis=-1)
        return jnp.einsum('bhqk,bqkd->bqhd', p.astype(v.dtype), v_sel)

    starts = jnp.arange(nb, dtype=jnp.int32) * BLOCK
    out = lax.map(one_block, (blocks(q), blocks(qi), blocks(wi), starts))
    return jnp.moveaxis(out, 0, 1).reshape(B, T, H, hd)

def first_inputs(seed: int = 0) -> dict:
    key = jax.random.key(seed)
    ks = jax.random.split(key, 12)
    f32 = jnp.float32

    def dense(k, shape, fan_in):
        return jax.random.normal(k, shape, f32) * fan_in ** -0.5

    def gain(k, shape):
        return 1.0 + 0.02 * jax.random.normal(k, shape, f32)

    return {
        'x': jax.random.normal(ks[0], (BATCH, SEQ, D_MODEL), f32),
        'norm_mix': gain(ks[1], (DEPTH, D_MODEL)),
        'w_in': dense(ks[2], (DEPTH, D_MODEL, D_IN), D_MODEL),
        'w_up_a': dense(ks[3], (DEPTH, D_A, D_MODEL), D_A),
        'w_up_b': dense(ks[4], (DEPTH, D_B, D_MODEL), D_B),
        'w_out': dense(ks[5], (DEPTH, D_MODEL, D_MODEL), D_MODEL),
        'norm_ffn': gain(ks[6], (DEPTH, D_MODEL)),
        'w_gate': dense(ks[7], (DEPTH, D_MODEL, D_FF), D_MODEL),
        'w_up': dense(ks[8], (DEPTH, D_MODEL, D_FF), D_MODEL),
        'w_down': dense(ks[9], (DEPTH, D_FF, D_MODEL), D_FF),
        'norm_final': gain(ks[10], (D_MODEL,)),
    }

def first_block(x, norm_mix, w_in, w_up_a, w_up_b, w_out, norm_ffn, w_gate, w_up, w_down, norm_final):
    B, T, _ = x.shape
    pos = jnp.arange(T, dtype=jnp.int32)
    for layer in range(DEPTH):
        h = rmsnorm(x, norm_mix[layer])
        proj = h @ w_in[layer]
        qa, ka, va, qb, kb, vb, qi, ki, wi, ga, gb = jnp.split(proj, IN_OFFSETS, axis=-1)
        qa = rope(qa.reshape(B, T, A_HEADS, HEAD_DIM), pos)
        ka = rope(ka.reshape(B, T, A_HEADS, HEAD_DIM), pos)
        va = va.reshape(B, T, A_HEADS, HEAD_DIM)
        y_a = dilated_mixture(qa, ka, va).astype(x.dtype).reshape(B, T, D_A)
        qb = rope(qb.reshape(B, T, B_HEADS, HEAD_DIM), pos)
        kb = rope(kb[:, :, None], pos)[:, :, 0]
        qi = rope(qi.reshape(B, T, IDX_HEADS, IDX_DIM), pos)
        ki = rope(ki[:, :, None], pos)[:, :, 0]
        y_b = indexed_sparse_attention(qb, kb, vb, qi, ki, wi).reshape(B, T, D_B)
        merged = jax.nn.sigmoid(ga) * (y_a @ w_up_a[layer]) + jax.nn.sigmoid(gb) * (y_b @ w_up_b[layer])
        x = x + merged @ w_out[layer]
        h = rmsnorm(x, norm_ffn[layer])
        x = x + (jax.nn.silu(h @ w_gate[layer]) * (h @ w_up[layer])) @ w_down[layer]
    return rmsnorm(x, norm_final)


MLA_HEADS = 4
MLA_NOPE = 128
MLA_ROPE = 64
MLA_V = 128
Q_LORA = D_MODEL // 4
KV_LORA = D_MODEL // 8
MLA_QK = MLA_NOPE + MLA_ROPE
MLA_WIDTH = MLA_HEADS * MLA_V

DIFF_HEADS = 4
DIFF_D = 64
DIFF_V = 2 * DIFF_D
DIFF_QK_WIDTH = DIFF_HEADS * 2 * DIFF_D
DIFF_WIDTH = DIFF_HEADS * DIFF_V

MIX_WIDTH = MLA_WIDTH + DIFF_WIDTH
IN_WIDTH = Q_LORA + KV_LORA + MLA_ROPE + 2 * DIFF_QK_WIDTH + DIFF_WIDTH
SPLITS = (Q_LORA, Q_LORA + KV_LORA, Q_LORA + KV_LORA + MLA_ROPE,
          Q_LORA + KV_LORA + MLA_ROPE + DIFF_QK_WIDTH,
          Q_LORA + KV_LORA + MLA_ROPE + 2 * DIFF_QK_WIDTH)

D_FF_2 = 4 * D_MODEL
N_BUCKETS = 32
MAX_DISTANCE = 128
EPS = 1e-6
Q_BLOCK = 128


def _rmsnorm(x, w):
    x32 = x.astype(jnp.float32)
    y = x32 * lax.rsqrt(jnp.mean(x32 * x32, axis=-1, keepdims=True) + EPS)
    return (y * w.astype(jnp.float32)).astype(x.dtype)

def _rotate_half(x):
    x1, x2 = jnp.split(x, 2, axis=-1)
    return jnp.concatenate([-x2, x1], axis=-1)

def _rope_tables(seq, dtype):
    inv = ROPE_THETA ** (-jnp.arange(0, MLA_ROPE, 2, dtype=jnp.float32) / MLA_ROPE)
    ang = jnp.arange(seq, dtype=jnp.float32)[:, None] * inv[None, :]
    ang = jnp.concatenate([ang, ang], axis=-1)
    return jnp.cos(ang).astype(dtype), jnp.sin(ang).astype(dtype)

def _t5_bucket(rel):
    half = N_BUCKETS // 2
    ret = jnp.where(rel > 0, half, 0)
    n = jnp.abs(rel)
    max_exact = half // 2
    large = max_exact + (jnp.log(jnp.maximum(n, 1).astype(jnp.float32) / max_exact)
                         / math.log(MAX_DISTANCE / max_exact)
                         * (half - max_exact)).astype(jnp.int32)
    large = jnp.minimum(large, half - 1)
    return ret + jnp.where(n < max_exact, n, large)

def _query_blocks(q):
    b, s = q.shape[:2]
    qb = q.reshape((b, s // Q_BLOCK, Q_BLOCK) + q.shape[2:])
    return jnp.moveaxis(qb, 1, 0)

def _merge_blocks(o):
    o = jnp.moveaxis(o, 0, 1)
    return o.reshape((o.shape[0], o.shape[1] * o.shape[2]) + o.shape[3:])

def _mla_attention(q, k, v):
    scale = MLA_QK ** -0.5

    def one(qblk):
        s = jnp.einsum('bqhd,bkhd->bhqk', qblk, k).astype(jnp.float32) * scale
        p = jax.nn.softmax(s, axis=-1).astype(v.dtype)
        return jnp.einsum('bhqk,bkhd->bqhd', p, v)

    return _merge_blocks(lax.map(one, _query_blocks(q)))

def _diff_attention(q, k, v, rel_bias, lam):
    seq = q.shape[1]
    scale = DIFF_D ** -0.5
    kpos = jnp.arange(seq, dtype=jnp.int32)
    starts = jnp.arange(seq // Q_BLOCK, dtype=jnp.int32) * Q_BLOCK
    table = rel_bias.astype(jnp.float32)

    def one(args):
        qblk, start = args
        qpos = start + jnp.arange(Q_BLOCK, dtype=jnp.int32)
        bucket = _t5_bucket(kpos[None, :] - qpos[:, None])
        bias = jnp.moveaxis(table[bucket], -1, 0)
        s = jnp.einsum('bqhmd,bkhmd->bmhqk', qblk, k).astype(jnp.float32) * scale + bias
        p = jax.nn.softmax(s, axis=-1)
        a = p[:, 0] - lam * p[:, 1]
        return jnp.einsum('bhqk,bkhd->bqhd', a.astype(v.dtype), v)

    return _merge_blocks(lax.map(one, (_query_blocks(q), starts)))

def second_inputs(seed: int = 0) -> dict:
    key = jax.random.key(seed)
    ks = jax.random.split(key, 24)
    f32 = jnp.float32

    def w(k, shape, fan_in):
        return jax.random.normal(k, shape, f32) * fan_in ** -0.5

    def gain(k, shape):
        return 1.0 + 0.02 * jax.random.normal(k, shape, f32)

    L = DEPTH
    return {
        "x": jax.random.normal(ks[0], (BATCH, SEQ, D_MODEL), f32),
        "attn_norm_w": gain(ks[1], (L, D_MODEL)),
        "w_in": w(ks[2], (L, D_MODEL, IN_WIDTH), D_MODEL),
        "q_a_norm_w": gain(ks[3], (L, Q_LORA)),
        "w_uq": w(ks[4], (L, Q_LORA, MLA_HEADS * MLA_QK), Q_LORA),
        "kv_a_norm_w": gain(ks[5], (L, KV_LORA)),
        "w_ukv": w(ks[6], (L, KV_LORA, MLA_HEADS * (MLA_NOPE + MLA_V)), KV_LORA),
        "mla_q_norm_w": gain(ks[7], (L, MLA_QK)),
        "mla_k_norm_w": gain(ks[8], (L, MLA_QK)),
        "diff_q_norm_w": gain(ks[9], (L, DIFF_D)),
        "diff_k_norm_w": gain(ks[10], (L, DIFF_D)),
        "lambda_q1": 0.1 * jax.random.normal(ks[11], (L, DIFF_D), f32),
        "lambda_k1": 0.1 * jax.random.normal(ks[12], (L, DIFF_D), f32),
        "lambda_q2": 0.1 * jax.random.normal(ks[13], (L, DIFF_D), f32),
        "lambda_k2": 0.1 * jax.random.normal(ks[14], (L, DIFF_D), f32),
        "diff_out_norm_w": gain(ks[15], (L, DIFF_V)),
        "w_out": w(ks[16], (L, MIX_WIDTH, D_MODEL), MIX_WIDTH),
        "mlp_norm_w": gain(ks[17], (L, D_MODEL)),
        "w_up": w(ks[18], (L, D_MODEL, D_FF_2), D_MODEL),
        "w_down": w(ks[19], (L, D_FF_2, D_MODEL), D_FF_2),
        "rel_bias": 0.5 * jax.random.normal(ks[20], (N_BUCKETS, DIFF_HEADS), f32),
    }

def second_block(x, attn_norm_w, w_in, q_a_norm_w, w_uq, kv_a_norm_w, w_ukv,
              mla_q_norm_w, mla_k_norm_w, diff_q_norm_w, diff_k_norm_w,
              lambda_q1, lambda_k1, lambda_q2, lambda_k2, diff_out_norm_w,
              w_out, mlp_norm_w, w_up, w_down, rel_bias):
    b, s, _ = x.shape
    cos, sin = _rope_tables(s, x.dtype)
    for layer in range(DEPTH):
        lam_init = 0.8 - 0.6 * math.exp(-0.3 * layer)

        h = _rmsnorm(x, attn_norm_w[layer])
        proj = h @ w_in[layer]
        c_q, c_kv, k_rope, dq, dk, dv = jnp.split(proj, SPLITS, axis=-1)

        q = (_rmsnorm(c_q, q_a_norm_w[layer]) @ w_uq[layer]).reshape(b, s, MLA_HEADS, MLA_QK)
        q_nope, q_rope = q[..., :MLA_NOPE], q[..., MLA_NOPE:]
        q_rope = q_rope * cos[:, None, :] + _rotate_half(q_rope) * sin[:, None, :]
        kv = (_rmsnorm(c_kv, kv_a_norm_w[layer]) @ w_ukv[layer]).reshape(b, s, MLA_HEADS, MLA_NOPE + MLA_V)
        k_nope, v_mla = kv[..., :MLA_NOPE], kv[..., MLA_NOPE:]
        k_rope = k_rope * cos + _rotate_half(k_rope) * sin
        k_rope = jnp.broadcast_to(k_rope[:, :, None, :], (b, s, MLA_HEADS, MLA_ROPE))
        q_m = _rmsnorm(jnp.concatenate([q_nope, q_rope], axis=-1), mla_q_norm_w[layer])
        k_m = _rmsnorm(jnp.concatenate([k_nope, k_rope], axis=-1), mla_k_norm_w[layer])
        o_mla = _mla_attention(q_m, k_m, v_mla).reshape(b, s, MLA_WIDTH)

        dq = _rmsnorm(dq.reshape(b, s, DIFF_HEADS, 2, DIFF_D), diff_q_norm_w[layer])
        dk = _rmsnorm(dk.reshape(b, s, DIFF_HEADS, 2, DIFF_D), diff_k_norm_w[layer])
        dv = dv.reshape(b, s, DIFF_HEADS, DIFF_V)
        lam = (jnp.exp(jnp.sum(lambda_q1[layer].astype(jnp.float32) * lambda_k1[layer].astype(jnp.float32)))
               - jnp.exp(jnp.sum(lambda_q2[layer].astype(jnp.float32) * lambda_k2[layer].astype(jnp.float32)))
               + lam_init)
        o_d = _diff_attention(dq, dk, dv, rel_bias, lam)
        o_diff = (_rmsnorm(o_d, diff_out_norm_w[layer]) * (1.0 - lam_init)).reshape(b, s, DIFF_WIDTH)

        x = x + jnp.concatenate([o_mla, o_diff], axis=-1) @ w_out[layer]

        h = _rmsnorm(x, mlp_norm_w[layer])
        x = x + jnp.square(jax.nn.relu(h @ w_up[layer])) @ w_down[layer]
    return x


def setup_inputs(seed=0):
    out = dict(first_inputs(seed))
    for name, value in second_inputs(seed + 1).items():
        if name != "x":
            out[name + "_2"] = value
    return out


def reference(
    x, norm_mix, w_in, w_up_a, w_up_b, w_out, norm_ffn, w_gate, w_up, w_down, norm_final,
    attn_norm_w_2, w_in_2, q_a_norm_w_2, w_uq_2, kv_a_norm_w_2, w_ukv_2, mla_q_norm_w_2,
    mla_k_norm_w_2, diff_q_norm_w_2, diff_k_norm_w_2, lambda_q1_2, lambda_k1_2, lambda_q2_2,
    lambda_k2_2, diff_out_norm_w_2, w_out_2, mlp_norm_w_2, w_up_2, w_down_2, rel_bias_2,
):
    x = first_block(
        x, norm_mix, w_in, w_up_a, w_up_b, w_out, norm_ffn, w_gate, w_up, w_down, norm_final,
    )
    return second_block(
        x, attn_norm_w_2, w_in_2, q_a_norm_w_2, w_uq_2, kv_a_norm_w_2, w_ukv_2, mla_q_norm_w_2,
        mla_k_norm_w_2, diff_q_norm_w_2, diff_k_norm_w_2, lambda_q1_2, lambda_k1_2, lambda_q2_2,
        lambda_k2_2, diff_out_norm_w_2, w_out_2, mlp_norm_w_2, w_up_2, w_down_2, rel_bias_2,
    )


_drawn_inputs = setup_inputs


def setup_inputs(seed=0):
    import zlib

    import numpy as np

    out = dict(_drawn_inputs(seed))
    spreads = {}
    factors = {'norm_mix': 4.861,
     'norm_ffn': 2.951,
     'attn_norm_w_2': 2.816,
     'q_a_norm_w_2': 8.0,
     'kv_a_norm_w_2': 8.0,
     'mla_q_norm_w_2': 8.0,
     'mla_k_norm_w_2': 8.0,
     'diff_q_norm_w_2': 5.674,
     'diff_k_norm_w_2': 6.226,
     'diff_out_norm_w_2': 41.178,
     'mlp_norm_w_2': 9.195}
    for name, (base, spread) in spreads.items():
        noise = np.random.default_rng([zlib.crc32(name.encode()), seed]).standard_normal(out[name].shape)
        drawn = base * np.exp(spread * noise) if base else spread * noise
        out[name] = __import__('jax').numpy.asarray(drawn.astype(out[name].dtype))
    for name, factor in factors.items():
        out[name] = (out[name] * factor).astype(out[name].dtype)
    return out
```

```python
from contextlib import ExitStack
import math

import numpy as np

import concourse.bass as bass
from concourse import mybir

F32 = mybir.dt.float32
F32R = mybir.dt.float32r
ACT = mybir.ActivationFunctionType
ALU = mybir.AluOpType
AX = mybir.AxisListType

P = 128
T = 1024
D = 1024
QT = T // P
DC = D // P
HALF = 512
CH = P * DC
HD = 64
TOPK = 256
D_FF = 2816
D_FF2 = 4096
EPS = 1e-6
ATTN_SCALE = HD ** -0.5
IDX_SCALE = (HD ** -0.5) * (8 ** -0.5)
MLA_QK = 192
MLA_SCALE = MLA_QK ** -0.5
LAM_INIT = 0.8 - 0.6 * math.exp(0.0)
MASKED = -1e30
UNREACHABLE = -3e38
TAKEN = -3.4e38
SPAN = 1920

QA, KA, VA, QB, KB, VB, QI, KI, WI, GA, GB = 0, 512, 1024, 1536, 2048, 2112, 2176, 2688, 2752, 2760, 3784
CQ, CKV, KR, DQ, DK, DV = 0, 256, 384, 448, 960, 1472

GAINS = {"mix": (0, 8), "ffn": (8, 8), "final": (16, 8), "attn2": (24, 8), "mlp2": (32, 8), "q_a": (40, 2),
         "kv_a": (42, 1), "mq_n": (43, 1), "mq_r": (44, 1), "mk_n": (45, 1), "mk_r": (46, 1), "dq": (47, 1),
         "dk": (48, 1), "dout": (49, 1)}


def shape_constants():
    f = np.float32
    half = HD // 2
    inv = np.power(f(10000.0), (-np.arange(half, dtype=f) / f(half)).astype(f)).astype(f)
    ang = (np.arange(T, dtype=f)[:, None] * inv[None, :]).astype(f)
    cos, sin = np.cos(ang).astype(f).T, np.sin(ang).astype(f).T
    cos_t = np.concatenate([cos, cos, cos, cos], 0)
    sin_t = np.concatenate([sin, -sin, sin, -sin], 0)
    dist = np.arange(P)[:, None] + 896 - np.arange(T)[None, :]
    count = ((dist <= 128).astype(int) + ((dist % 4 == 0) & (dist <= 512)) + (dist % 16 == 0)) * (dist >= 0)
    abias = np.where(count > 0, np.log(np.maximum(count, 1)) / ATTN_SCALE, MASKED).astype(f)
    causal = np.where(np.arange(P)[None, :] > np.arange(P)[:, None], UNREACHABLE, 0.0).astype(f)
    rel = np.arange(2 * T) - (T - 1)
    n = np.abs(rel)
    large = 8 + (np.log(np.maximum(n, 1).astype(f) / f(8)) / f(math.log(128 / 8)) * f(8)).astype(np.int32)
    bucket = np.where(rel > 0, 16, 0) + np.where(n < 8, n, np.minimum(large, 15))
    onehot = (bucket[None, :] == np.arange(32)[:, None]).astype(f)
    blocks = np.kron(np.eye(2), np.ones((64, 64))).astype(f)
    return {"cos_t": cos_t, "sin_t": sin_t, "abias": abias, "causal": causal, "onehot": onehot,
            "ident": np.eye(P, dtype=f), "blocks": blocks}


class Signal:

    def __init__(self, sem, known):
        self.sem, self.known, self.count = sem, known, 0

    def mark(self, *key, by=1):
        self.count += by
        self.known[key] = self.count
        return self.sem, by

    def at(self, *key):
        return self.sem, self.known.get(key, 1) if self.known is not None else 1

    def loop(self, *key, total):
        self.known[key] = self.count
        self.count += total
        return self.count - total

    def base(self, *key):
        return self.known.get(key, 0)


def emit(nc, known, a):
    ctx = ExitStack()
    with ctx:
        _emit(nc, ctx, known, a)


def _emit(nc, ctx, known, a):
    base0 = (nc.sbuf_base + 63) // 64 * 64

    def at(name, offset, shape, dt=F32):
        return nc.alloc_sbuf_tensor_at(name, shape, dt, offset=base0 + offset)

    K = 1024
    G1, G2, WB, M0, X0, R0 = 0, 64 * K, 128 * K, 152 * K, 152 * K + 7424, 184 * K + 7424
    g1h, g1l = at("g1_hi", G1, [P, DC, T], F32R), at("g1_lo", G1 + 32 * K, [P, DC, T], F32R)
    g2h, g2l = at("g2_hi", G2, [P, DC, T], F32R), at("g2_lo", G2 + 32 * K, [P, DC, T], F32R)
    w_raw = [at(f"w_raw{s}", WB + 4 * K * s, [P, CH]) for s in range(2)]
    w_hi = [at(f"w_hi{s}", WB + 8 * K + 4 * K * s, [P, CH], F32R) for s in range(2)]
    w_lo = [at(f"w_lo{s}", WB + 16 * K + 4 * K * s, [P, CH], F32R) for s in range(2)]
    r_rep = at("r_rep", M0, [P, T])
    ident = at("ident_sb", M0 + 4096, [P, P])
    ones = at("ones_sb", M0 + 4608, [P, P])
    blocks = at("blocks_sb", M0 + 5120, [P, P])
    causal = at("causal_sb", M0 + 5632, [P, P])
    gains = at("gains", M0 + 6144, [P, 50])
    eps_c = at("eps_c", M0 + 6400, [P, 1])
    lam_v = at("lam_v", M0 + 6464, [HD, 8])
    lam_e = at("lam_e", M0 + 6528, [P, 4])
    mn = at("mn", M0 + 6592, [P, 8])
    sm = at("sm", M0 + 6656, [P, 8])
    rc = at("rc", M0 + 6720, [P, 8])
    m8 = at("m8", M0 + 6784, [P, 8])
    wiT = at("wiT", M0 + 6848, [P, QT, 8])
    tab = at("tab", M0 + 7104, [32, 4])
    xres = at("x_res", X0, [P, DC, T])
    ya = at("y_a", X0, [P, 4, T])
    yb = at("y_b", X0 + 16 * K, [P, 4, T])
    cosr, sinr = at("cos_r", R0, [P, T]), at("sin_r", R0 + 4 * K, [P, T])
    rot1, rot2 = at("rot1", R0 + 8 * K, [P, T]), at("rot2", R0 + 12 * K, [P, T])
    qab = [at(f"qa{s}", G2 + 4 * K * s, [P, T]) for s in range(2)]
    kab = [at(f"ka{s}", G2 + 8 * K + 4 * K * s, [P, T]) for s in range(2)]
    vab = [at(f"va{s}", G2 + 16 * K + 4 * K * s, [P, QT, P]) for s in range(2)]
    kib = at("ki_b", G2 + 8 * K, [P, T])
    qbb = [at(f"qb{c}", G2 + 4 * K * c, [P, T]) for c in range(4)]
    kbb = at("kb_b", G2 + 16 * K, [P, T])
    vbb = at("vb_b", G2 + 20 * K, [P, QT, HD])
    prob = [at(f"prob{s}", G2 + 24 * K + 8 * K * s, [P, 2, T]) for s in range(2)]
    rel = [at(f"rel{s}", G2 + 24 * K + 4 * K * s, [P, T]) for s in range(2)]
    wif = at("wi_f", G2 + 32 * K, [P, T])
    pt = [at(f"pt{s}", G2 + 40 * K + 2 * K * s, [P, HALF]) for s in range(3)]
    acc_at = [sum(P * (j + 1) for j in range(i)) for i in range(QT + 1)]
    acc = at("idx_acc", G2 + 46 * K, [P, acc_at[QT]])
    xt = [at(f"xt{s}", G2 + 4 * K * s, [P, QT, P]) for s in range(2)]
    xs = [at(f"xs{s}", G2 + 8 * K + 4 * K * s, [P, T]) for s in range(2)]
    gst = [at(f"gst{s}", X0 + 16 * K + 4 * K * s, [P, T]) for s in range(2)]
    abias = at("abias_sb", X0 + 24 * K, [P, T])
    vf = at("v_f", X0 + 28 * K, [P, T])
    oh = at("onehot_sb", G1, [32, 2 * T])
    brow = [at(f"brow{s}", G1 + 8 * K + 8 * K * s, [P, 2 * T]) for s in range(2)]
    tabr = at("tabr", G1 + 24 * K, [32, P])
    sgab = [at("sg_a", R0 + 8 * K, [P, T]), at("sg_b", R0 + 12 * K, [P, T])]
    ta, tb = at("t_a", R0, [P, T]), at("t_b", R0 + 4 * K, [P, T])
    NB = {"x": X0, "r": R0, "y": X0 + 16 * K}
    nb = {k: {"sq": [at(f"sq_{k}{s}", o + 4 * K * s, [P, T]) for s in range(2)],
              "ss": at(f"ss_{k}", o + 8 * K, [P, T]), "rt": at(f"rt_{k}", o + 12 * K, [P, T])} for k, o in NB.items()}
    tg, tsil, tact = at("t_g", R0, [P, T]), at("t_silu", R0 + 4 * K, [P, T]), at("t_act", R0 + 8 * K, [P, T])
    dprob = [[at(f"dprob{s}{m}", G1 + 16 * K * s + 8 * K * m, [P, 2, T]) for m in range(2)] for s in range(2)]
    dqb = [at(f"dq{s}", G1 + 32 * K + 4 * K * s, [P, T]) for s in range(2)]
    dkb = [at(f"dk{s}", G1 + 40 * K + 4 * K * s, [P, T]) for s in range(2)]
    dvb = [at(f"dv{s}", G1 + 48 * K + 4 * K * s, [P, QT, P]) for s in range(2)]
    dpt = [at(f"dpt{s}", G1 + 56 * K + 2 * K * s, [P, HALF]) for s in range(3)]
    dbias = [at(f"dbias{s}", R0 + 7680 * s, [P, SPAN]) for s in range(2)]
    yd, ym = at("y_d", X0, [P, 4, T]), at("y_m", X0 + 16 * K, [P, 4, T])
    dvf = at("dv_f", X0 + 28 * K, [P, T])
    mprob = [at(f"mprob{s}", G1 + 8 * K * s, [P, 2, T]) for s in range(2)]
    rkv = at("r_kv", G1, [P, T])
    sqr = [at(f"sqr{s}", G1 + 4 * K + 4 * K * s, [P, T]) for s in range(3)]
    cqf = [at(f"cqf{s}", G1 + 16 * K + 4 * K * s, [P, T]) for s in range(3)]
    krb = at("kr_b", G1 + 28 * K, [P, T])
    clh = at("cl_hi", G1 + 32 * K, [P, 3, T], F32R)
    cll = at("cl_lo", G1 + 44 * K, [P, 3, T], F32R)
    mqn = [at(f"mqn{h}", G2 + 4 * K * h, [P, T]) for h in range(4)]
    mkn = [at(f"mkn{h}", G2 + 16 * K + 4 * K * h, [P, T]) for h in range(4)]
    mqr = [at(f"mqr{p}", G2 + 32 * K + 4 * K * p, [P, T]) for p in range(2)]
    mkr = [at(f"mkr{p}", G2 + 40 * K + 4 * K * p, [P, T]) for p in range(2)]
    mvb = [at(f"mv{h}", G2 + 48 * K + 4 * K * h, [P, QT, P]) for h in range(4)]
    sqn = [at(f"sqn{s}", X0 + 16 * K + 4 * K * s, [P, T]) for s in range(2)]
    mrt = at("mrt", X0 + 24 * K, [P, T])
    mvf = at("mv_f", X0 + 28 * K, [P, T])
    sskv = at("ss_kv", G1 + 60 * K, [P, T])
    krz = at("kr_z", G1 + 56 * K, [P, T])
    yst = [at(f"yst{s}", R0 + 4 * K * s, [P, QT, P]) for s in range(2)]

    big = [ctx.enter_context(nc.psum_tensor(f"big{s}", [P, T], F32)) for s in range(2)]
    tbank = [ctx.enter_context(nc.psum_tensor(f"tbank{s}", [P, HALF], F32)) for s in range(2)]
    obank = [ctx.enter_context(nc.psum_tensor(f"obank{s}", [P, HALF], F32)) for s in range(2)]

    def dram(name, shape):
        return nc.dram_tensor(name, shape, F32, kind="Internal").ap()

    x_spill = dram("x_spill", [DC, P, T])
    g_spill = dram("g_spill", [2 * DC, P, T])
    b_spill = dram("b_spill", [4, P * 2 * T])

    def sig(name):
        return Signal(ctx.enter_context(nc.semaphore(name)), known.setdefault(name, {}))

    w_in_dma = [sig(f"w_loaded{s}") for s in range(2)]
    s_whi, s_wlo = sig("w_hi_done"), sig("w_lo_done")
    s_big = sig("big_done")
    s_rel = sig("big_released")
    s_arel = sig("big_read_act")
    s_tb, s_te = sig("tbank_done"), sig("tbank_read")
    s_o, s_oe = sig("obank_done"), sig("obank_read")
    s_cst = [sig(f"const{n}") for n in range(4)]
    s_xl = [sig(f"x_loaded{s}") for s in range(2)]
    s_sp = [sig(f"spilled{s}") for s in range(2)]
    s_bsp = [sig(f"bias_spilled{s}") for s in range(2)]
    s_bl = [sig(f"bias_loaded{s}") for s in range(2)]
    s_gsp = [sig(f"gate_spilled{s}") for s in range(2)]
    s_gl = [sig(f"gate_loaded{s}") for s in range(2)]
    s_dup = sig("key_duplicated")
    s_tabl = sig("tables_loaded")
    s_out = [sig(f"out_stored{s}") for s in range(2)]
    s_nh, s_sq = sig("norm_hi"), sig("norm_square")
    s_nl = sig("norm_lo")
    s_ss = sig("squares_summed")
    s_rt, s_r = sig("root_done"), sig("r_ready")
    s_dv = sig("dve_step")
    s_rot = sig("rope_added")
    s_tab = sig("tables_scaled")
    s_relu, s_acc = sig("relu_done"), sig("acc_done")
    s_tk = sig("topk_step")
    s_sc, s_ex, s_nrm = sig("scores_shifted"), sig("exp_done"), sig("probs_ready")
    s_gt, s_sg = sig("gate_scaled"), sig("gate_done")
    s_mg, s_mgh, s_mgl = sig("merged"), sig("merged_hi"), sig("merged_lo")
    s_yh, s_yl = sig("y_hi"), sig("y_lo")
    s_mm, s_msq = sig("max_prepared"), sig("head_squares")
    s_hn = sig("head_normed")
    s_ptu = sig("pt_used")
    s_xres, s_fin = sig("x_reloaded"), sig("lambda_ready")

    w_in, w_in2 = a["w_in"][0], a["w_in_2"][0]

    def cols(w, c0, n=P, k0=0, kn=None):
        kn = w.shape[0] if kn is None else kn
        return w[k0:k0 + kn, c0:c0 + n].rearrange("(k p) m -> p k m", p=P)

    def raw(s, k, m, o=0):
        return w_raw[s][:, o:o + k * m].rearrange("p (k m) -> p k m", k=k)

    chunks = []

    def std(name, w, c0, k0=0, kn=None):
        kn_ = w.shape[0] if kn is None else kn
        chunks.append((name, lambda s: [(raw(s, kn_ // P, P), cols(w, c0, P, k0, kn_))]))

    def mixed(name, w, parts):
        chunks.append((name, lambda s: [(raw(s, DC, P)[:, :, m0:m0 + n], cols(w, c0, n)) for m0, c0, n in parts]))

    std("qi0", w_in, QI)
    std("qi1", w_in, QI + P)
    mixed("kiwi", w_in, [(0, KI, HD), (HD, WI, 8)])
    std("qi2", w_in, QI + 2 * P)
    std("qi3", w_in, QI + 3 * P)
    for c in range(4):
        std(f"va{c}", w_in, VA + P * c)
        std(f"qa{c}", w_in, QA + P * c)
        std(f"ka{c}", w_in, KA + P * c)
    for j in range(DC):
        std(f"ga{j}", w_in, GA + P * j)
    for j in range(DC):
        std(f"gb{j}", w_in, GB + P * j)
    mixed("kbvb", w_in, [(0, KB, HD), (HD, VB, HD)])
    for c in range(4):
        std(f"qb{c}", w_in, QB + P * c)
    for j in range(DC):
        chunks.append((f"up{j}", lambda s, j=j: [(raw(s, 4, P), cols(a["w_up_a"][0], P * j)),
                                                 (raw(s, 4, P, 4 * P), cols(a["w_up_b"][0], P * j))]))
    for j in range(DC):
        std(f"out{j}", a["w_out"][0], P * j)
    groups1 = [(0, 8), (8, 8), (16, 6)]
    groups2 = [(8 * n, 8) for n in range(4)]
    for n, (f0, fn) in enumerate(groups1):
        for f in range(fn):
            std(f"gate{f0 + f}", a["w_gate"][0], P * (f0 + f))
            std(f"upf{f0 + f}", a["w_up"][0], P * (f0 + f))
        for j in range(DC):
            std(f"down{n}_{j}", a["w_down"][0], P * j, P * f0, P * fn)
    for h in range(4):
        std(f"dv{h}", w_in2, DV + P * h)
        std(f"dq{h}", w_in2, DQ + P * h)
        std(f"dk{h}", w_in2, DK + P * h)
    std("cq0", w_in2, CQ)
    std("cq1", w_in2, CQ + P)
    std("ckv", w_in2, CKV)
    mixed("kr", w_in2, [(0, KR, HD), (HD, KR, HD)])
    uq = a["w_uq_2"][0]
    ukv = a["w_ukv_2"][0]
    chunks.append(("uqr", lambda s: [(raw(s, 2, 4 * HD)[:, :, HD * h:HD * h + HD], cols(uq, MLA_QK * h + P, HD))
                                     for h in range(4)]))
    for h in range(4):
        chunks.append((f"mh{h}", lambda s, h=h: [(raw(s, 2, P), cols(uq, MLA_QK * h)),
                                                 (raw(s, 2, P, 2 * P), ukv[:, 2 * P * h:2 * P * h + 2 * P].rearrange("p (k m) -> p k m", k=2))]))
    for j in range(DC):
        std(f"out2_{j}", a["w_out_2"][0], P * j)
    for n, (f0, fn) in enumerate(groups2):
        for f in range(fn):
            std(f"up2_{f0 + f}", a["w_up_2"][0], P * (f0 + f))
        for j in range(DC):
            std(f"down2_{n}_{j}", a["w_down_2"][0], P * j, P * f0, P * fn)
    W = {name: w for w, (name, _) in enumerate(chunks)}
    NW = len(chunks)

    S = []
    add = lambda *x: S.append(x)
    for h in range(4):
        add("biasrow", h)
    add("lam")
    for j in range(DC):
        add("xin", j)
    add("rope", "qi0")
    add("ss", "mix")
    add("tables", "b1")
    add("rope", "qi1")
    add("kiwi")
    add("wi_t")
    add("idx", 0)
    add("rope", "qi2")
    add("idx", 1)
    add("rope", "qi3")
    add("idx", 2)
    add("lin", "va0")
    add("idx", 3)
    add("fill")
    rounds = [(i, r) for i in range(2, QT) for r in range(TOPK // 8)]
    cost = lambda i: 2 * (P * (i + 1) / 960.0 + 0.07)
    left = list(rounds)

    def topk(us):
        n0 = len(rounds) - len(left)
        t = 0.0
        while left and t + cost(left[0][0]) / 2 < us:
            t += cost(left.pop(0)[0])
        n1 = len(rounds) - len(left)
        if n1 > n0:
            add("topk", n0, n1)

    a_steps = {c: [("a", c, g, hh) for g in range(4) for hh in range(2)] for c in range(4)}
    b_steps = {c: [("b", c, g, hh) for g in range(4) for hh in range(2)] for c in range(4)}

    def pipeline(steps, filler, rest=0.0):
        for n, s in enumerate(steps):
            add("sc", s)
            if n:
                add("pv", steps[n - 1])
            if rest:
                topk(rest)
        filler()
        add("pv", steps[-1])

    add("rope", "qa0")
    add("v_t", "va0")
    add("rope", "ka0")
    topk(8.0)

    def a_proj(c):
        def go():
            add("lin", f"va{c}")
            topk(8.0)
            add("rope", f"qa{c}")
            add("v_t", f"va{c}")
            topk(4.0)
            add("rope", f"ka{c}")
            topk(4.0)
        return go

    def gates(j0, j1):
        def go():
            for j in range(j0, j1):
                add("gate", j)
                topk(8.5)
        return go

    for c in range(3):
        pipeline(a_steps[c], a_proj(c + 1), 0.8)
    pipeline(a_steps[3], gates(0, 2), 0.8)
    gates(2, 16)()
    add("kbvb")
    add("vb_t")
    topk(4.0)
    for c in range(4):
        add("rope", f"qb{c}")
        topk(1e9 if c == 3 else 4.0)
    add("mask")
    for c in range(4):
        pipeline(b_steps[c], lambda: None)
    add("ysplit")
    for j in range(DC):
        add("up", j)
    for j in range(DC):
        add("out", j)
    add("ss", "ffn")
    add("mlp1")
    add("ss", "final")
    for j in range(DC):
        add("x1", j)
    d_steps = {h: [("d", h, g, 0) for g in range(4)] for h in range(4)}
    m_steps = {h: [("m", h, g, 0) for g in range(4)] for h in range(4)}

    def d_proj(h):
        def go():
            add("lin", f"dv{h}")
            if h == 0:
                add("ss", "attn2")
            add("lin", f"dq{h}")
            add("v_t", f"dv{h}")
            add("lin", f"dk{h}")
            add("dnorm", "dq", h)
            add("dnorm", "dk", h)
        return go

    d_proj(0)()
    for h in range(4):
        pipeline(d_steps[h], d_proj(h + 1) if h < 3 else (lambda: None))
    for h in range(4):
        add("donorm", h)
    add("lin", "cq0")
    add("tables", "b2")
    add("lin", "cq1")
    add("lin", "ckv")
    add("krope")
    add("ss", "q_a")
    add("ss", "kv_a")
    add("uqr")
    for h in range(4):
        add("mh", h)
        add("v_t", f"mv{h}")
    mnorms = [(q, h) for h in range(4) for q in "qk"]
    add("mn1", *mnorms[0])
    for n, m in enumerate(mnorms):
        if n + 1 < 8:
            add("mn1", *mnorms[n + 1])
        add("mn2", *m)
    for h in range(4):
        pipeline(m_steps[h], lambda: None)
    add("y2split")
    for j in range(DC):
        add("out2", j)
    add("ss", "mlp2")
    add("mlp2")
    for j in range(DC):
        add("yout", j)

    def step_of(s):
        kind, c, g, hh = s
        o = HD * hh
        tiles = (2 * g, 2 * g + 1)
        if kind == "a":
            return dict(tiles=tiles, causal=True, maps=[[(qab[c % 2][o:o + HD, :], kab[c % 2][o:o + HD, :])]],
                        v=lambda kt: vab[c % 2][:, kt, o:o + HD], o0=o, m=HD, prob=[prob], pt=pt, scale=ATTN_SCALE,
                        bias=lambda i: abias[:, 896 - P * i:T], y=ya[:, c, :], first=hh == 0, last=hh == 1)
        if kind == "b":
            return dict(tiles=tiles, causal=True, maps=[[(qbb[c][o:o + HD, :], kbb[o:o + HD, :])]],
                        v=lambda kt: vbb[:, kt, :], o0=o, m=HD, prob=[prob], pt=pt, scale=ATTN_SCALE,
                        bias=lambda i: acc[:, acc_at[i]:acc_at[i + 1]], y=yb[:, c, :], first=hh == 0, last=hh == 1)
        if kind == "d":
            return dict(tiles=tiles, causal=False,
                        maps=[[(dqb[c % 2][HD * m:HD * m + HD, :], dkb[c % 2][HD * m:HD * m + HD, :])] for m in range(2)],
                        v=lambda kt: dvb[c % 2][:, kt, :], o0=0, m=P, prob=[[dprob[0][0], dprob[1][0]], [dprob[0][1], dprob[1][1]]],
                        pt=dpt, scale=HD ** -0.5, bias=lambda i: dbias[c % 2][:, 896 - P * i:896 - P * i + T],
                        y=yd[:, c, :], first=True, last=True)
        r = HD * (c % 2)
        return dict(tiles=tiles, causal=False,
                    maps=[[(mqn[c][:, :], mkn[c][:, :]), (mqr[c // 2][r:r + HD, :], mkr[c // 2][r:r + HD, :])]],
                    v=lambda kt: mvb[c][:, kt, :], o0=0, m=P, prob=[mprob], pt=[dpt[0], dpt[1], dpt[2]], scale=MLA_SCALE,
                    bias=None, y=ym[:, c, :], first=True, last=True)

    steps = [x[1] for x in S if x[0] == "sc"]
    nstep = {s: n for n, s in enumerate(steps)}

    def keys(st, i):
        return P * (i + 1) if st["causal"] else T

    def tgroups(st):
        i0, i1 = st["tiles"]
        last = i1 if st["causal"] else QT - 1
        out = []
        for k0 in range(0, last + 1, 2):
            if st["causal"] and k0 + 1 == i1:
                out.append([(k0, 0, 2 * P, 0), (k0 + 1, 2 * P, P, P)])
            else:
                out.append([(k0, 0, 2 * P, 0), (k0 + 1, 2 * P, 2 * P, 0)])
        return out

    def rope_dest(name):
        kind = name[:2]
        if kind == "qi":
            c = int(name[2])
            return qab[c % 2], ([("big", ("idx", c - 2, 1, QT - 1))] if c >= 2 else [])
        if kind in ("qa", "ka"):
            c = int(name[2])
            buf = (qab if kind == "qa" else kab)[c % 2]
            if c >= 2:
                return buf, [("big", ("sc",) + a_steps[c - 2][-1] + (1, 0))]
            if kind == "ka":
                return buf, [("big", ("idx", 3, 1, QT - 1))]
            return buf, [("big", ("idx", 2 + c % 2, 1, QT - 1))]
        if kind == "qb":
            return qbb[int(name[2])], [("o", ("o",) + a_steps[3][-1])]
        if name == "kr":
            return krb, []
        raise KeyError(name)

    lin_dest = {f"va{c}": vf for c in range(4)} | {f"dv{h}": dvf for h in range(4)}
    lin_dest |= {f"dq{h}": dqb[h % 2] for h in range(4)} | {f"dk{h}": dkb[h % 2] for h in range(4)}
    lin_dest |= {"cq0": cqf[0], "cq1": cqf[1], "ckv": cqf[2]}

    def nb_of(key):
        if key in ("q_a", "kv_a"):
            return nb["y"]
        return nb["x" if key == "mix" else "r"]

    def ss_of(key):
        return sskv if key == "kv_a" else nb_of(key)["ss"]

    def root_of(key):
        return nb_of(key)["rt"]

    def r_of(key):
        return rkv if key == "kv_a" else r_rep

    def load_bias(sp, h):
        sp.wait_ge(*s_bsp[h % 2].at(h))
        rows = b_spill[h][127:127 + P * (2 * T - 1)].rearrange("(p m) -> p m", p=P)
        sp.dma_start(dbias[h % 2][:, :], rows[:, 0:SPAN]).then_inc(*s_bl[h % 2].mark(h, by=16))

    pair = {}

    block = ctx.enter_context(nc.Block())

    @block.tensor
    def _(pe):
        jobs = []
        tn, on, pn = [0], [0], [0]

        def take(key, by):
            n = len(jobs)
            if n >= 2:
                last, reader = jobs[n - 2]
                pe.wait_ge(*reader.at(*last))
            jobs.append((key, by))
            pair[key] = n % 2
            return big[n % 2]

        def passes(out, m, slot, terms):
            total = len(terms)
            for n, (col, hi, lo, ready) in enumerate(terms):
                if ready is not None:
                    pe.wait_ge(*ready)
                for q, (w, x) in enumerate(((w_hi, hi), (w_hi, lo), (w_lo, hi))):
                    for h in range(2):
                        ins = pe.matmul(out[0:m, HALF * h:HALF * h + HALF], w[slot][:, col:col + m],
                                        x[:, HALF * h:HALF * h + HALF], start=(n == 0 and q == 0),
                                        stop=(n == total - 1 and q == 2))
            return ins

        def weight_job(name, key, m, terms, by=s_rel, end=True):
            w = W[name]
            pe.wait_ge(s_wlo.sem, w + 1)
            out = take(key, by)
            passes(out, m, w % 2, terms).then_inc(*s_big.mark(*key))
            if end:
                s_big.known[("w", w)] = s_big.count

        def chunk_terms(xh, xl, n=DC, k0=0, ready=None, col=0):
            return [(col + P * k, xh[:, k0 + k, :], xl[:, k0 + k, :], ready(k) if ready else None) for k in range(n)]

        def full_product(key, by, terms):
            out = take(key, by)
            for h in range(2):
                for n, (w, x) in enumerate(terms):
                    ins = pe.matmul(out[:, HALF * h:HALF * h + HALF], w, x[:, HALF * h:HALF * h + HALF],
                                    start=n == 0, stop=n == len(terms) - 1)
            ins.then_inc(*s_big.mark(*key))

        def to_tokens(name, src, r0, m, ready, per_bank):
            pe.wait_ge(*ready)
            for b in range(QT // per_bank):
                if tn[0] >= 2:
                    pe.wait_ge(s_te.sem, tn[0] - 1)
                for q in range(per_bank):
                    i = per_bank * b + q
                    ins = pe.transpose(tbank[tn[0] % 2][:, m * q:m * q + m], src[r0:r0 + m, P * i:P * i + P],
                                       ident[r0:r0 + m, r0:r0 + m])
                ins.then_inc(*s_tb.mark("t", name, b))
                tn[0] += 1

        pe.wait_ge(*s_cst[0].at())
        pe.wait_ge(*s_mm.at("ones"))
        seen = set()

        def once(tag, *waits):
            if tag not in seen:
                seen.add(tag)
                for w in waits:
                    pe.wait_ge(*w)

        for stage, *x in S:
            if stage == "biasrow":
                h, = x
                pe.wait_ge(*s_mm.at("tabr", h))
                for q in range(2):
                    out = take(("br", h, q), s_rel)
                    for b in range(2):
                        ins = pe.matmul(out[:, HALF * b:HALF * b + HALF], tabr[:, :],
                                        oh[:, T * q + HALF * b:T * q + HALF * b + HALF], start=True, stop=True)
                    ins.then_inc(*s_big.mark("br", h, q))
            elif stage == "lam":
                pe.wait_ge(*s_mm.at("lamp"))
                out = take(("lam",), s_arel)
                pe.matmul(out[:, 0:2], ones[0:HD, :], lam_v[:, 4:6], start=True, stop=True).then_inc(*s_big.mark("lam"))
            elif stage == "xin":
                j, = x
                pe.wait_ge(*s_xl[j % 2].at("xin", j))
                out = take(("xin", j), s_rel)
                for i in range(QT):
                    ins = pe.transpose(out[:, P * i:P * i + P], xt[j % 2][:, i, :], ident[:, :])
                ins.then_inc(*s_big.mark("xin", j))
            elif stage == "ss":
                key, = x
                n = {"q_a": 2, "kv_a": 1}.get(key, DC)
                pe.wait_ge(*s_ss.at(key, n - 1))
                full_product(("ss", key), s_arel, [(ones[:, :], ss_of(key)[:, :])])
            elif stage in ("rope", "lin"):
                name, = x
                norm = "mix" if W[name] < W["up0"] else "attn2"
                gh, gl = (g1h, g1l) if norm == "mix" else (g2h, g2l)
                first = name in ("qi0", "dv0")
                weight_job(name, (name,), P, chunk_terms(gh, gl, ready=(lambda k: s_nl.at(norm, k)) if first else None))
            elif stage in ("kiwi", "kbvb"):
                weight_job(stage, (stage,), HD + 8 if stage == "kiwi" else P, chunk_terms(g1h, g1l))
            elif stage == "krope":
                weight_job("kr", ("kr",), P, chunk_terms(g2h, g2l))
            elif stage == "wi_t":
                to_tokens("wi", wif, HD, 8, s_rel.at("kiwi"), 8)
            elif stage == "vb_t":
                to_tokens("vb", vf, HD, HD, s_rel.at("kbvb"), 8)
            elif stage == "v_t":
                name, = x
                src = vf if name[0] == "v" else (dvf if name[0] == "d" else mvf)
                ready = s_rel.at("mh", int(name[2]), "v") if name[0] == "m" else s_rel.at(name)
                to_tokens(name, src, 0, P, ready, 4)
            elif stage == "idx":
                c, = x
                pe.wait_ge(*s_rot.at(f"qi{c}"))
                pe.wait_ge(*s_dup.at("kiwi"))
                for hh in range(2):
                    for i in range(2, QT):
                        key = ("idx", c, hh, i)
                        out = take(key, s_arel)
                        n1 = P * (i + 1)
                        o = HD * hh
                        for n0 in range(0, n1, HALF):
                            ne = min(n0 + HALF, n1)
                            ins = pe.matmul(out[:, n0:ne], qab[c % 2][o:o + HD, P * i:P * i + P], kib[o:o + HD, n0:ne],
                                            start=True, stop=True)
                        ins.then_inc(*s_big.mark(*key))
            elif stage == "gate":
                j, = x
                name = f"ga{j}" if j < DC else f"gb{j - DC}"
                weight_job(name, (name,), P, chunk_terms(g1h, g1l))
            elif stage == "sc":
                s, = x
                st = step_of(s)
                kind, c = s[0], s[1]
                once(("q", kind, c), *{
                    "a": lambda: (s_rot.at(f"qa{c}"), s_rot.at(f"ka{c}")),
                    "b": lambda: (s_rot.at(f"qb{c}"), s_dup.at("kbvb")),
                    "d": lambda: (s_hn.at("dq", c), s_hn.at("dk", c)),
                    "m": lambda: (s_hn.at("mq", c), s_hn.at("mk", c)),
                }[kind]())
                for ti, i in enumerate(st["tiles"]):
                    for m, parts in enumerate(st["maps"]):
                        key = ("sc",) + s + (ti, m)
                        out = take(key, s_rel)
                        n1 = keys(st, i)
                        for n0 in range(0, n1, HALF):
                            ne = min(n0 + HALF, n1)
                            for q, (qa, ka) in enumerate(parts):
                                ins = pe.matmul(out[:, n0:ne], qa[:, P * i:P * i + P], ka[:, n0:ne], start=q == 0,
                                                stop=q == len(parts) - 1)
                        ins.then_inc(*s_big.mark(*key))
            elif stage == "pv":
                s, = x
                st = step_of(s)
                kind, c = s[0], s[1]
                once(("v", kind, c), s_te.at("t", {"a": f"va{c}", "b": "vb", "d": f"dv{c}", "m": f"mv{c}"}[kind],
                                             0 if kind == "b" else 1))
                groups = tgroups(st)
                n = nstep[s]
                last_kt = groups[-1][-1][0]

                def transposed(t):
                    if t == 0:
                        for ti in range(2):
                            pe.wait_ge(*s_nrm.at(s, ti))
                    if tn[0] >= 2:
                        pe.wait_ge(s_te.sem, tn[0] - 1)
                    for kt, c0, cn, q0 in groups[t]:
                        for ti in range(q0 // P, 2):
                            o = c0 + P * ti - q0
                            ins = pe.transpose(tbank[tn[0] % 2][:, o:o + P], st["prob"][0][n % 2][:, ti, P * kt:P * kt + P],
                                               ident[:, :])
                    ins.then_inc(*s_tb.mark(s, t))
                    tn[0] += 1

                def product(t):
                    if t == 0 and st["first"] and on[0] >= 2:
                        pe.wait_ge(s_oe.sem, on[0] - 1)
                    pe.wait_ge(*s_te.at(s, t))
                    for kt, c0, cn, q0 in groups[t]:
                        ins = pe.matmul(obank[on[0] % 2][st["o0"]:st["o0"] + st["m"], q0:q0 + cn], st["v"](kt),
                                        st["pt"][pn[0] % 3][:, c0:c0 + cn], start=kt == 0, stop=kt == last_kt)
                    ins.then_inc(*s_ptu.mark(s, t))
                    pn[0] += 1

                for t in range(len(groups)):
                    transposed(t)
                    if t:
                        product(t - 1)
                product(len(groups) - 1)
                s_ptu.known[("end", s)] = s_ptu.count
                if st["last"]:
                    on[0] += 1
            elif stage == "up":
                j, = x
                for half, part in enumerate("ab"):
                    weight_job(f"up{j}", ("up", j, part), P,
                               chunk_terms(g2h, g2l, 4, 4 * half, (lambda k: s_yl.at(4 * half + k)) if j == 0 else None,
                                           HALF * half), end=part == "b")
            elif stage == "out":
                j, = x
                weight_job(f"out{j}", ("out", j), P,
                           chunk_terms(g1h, g1l, ready=(lambda k: s_mgl.at("m", k)) if j == 0 else None))
            elif stage == "out2":
                j, = x
                weight_job(f"out2_{j}", ("out2", j), P,
                           chunk_terms(g1h, g1l, ready=(lambda k: s_yl.at("y2", k)) if j == 0 else None))
            elif stage in ("mlp1", "mlp2"):
                one = stage == "mlp1"
                groups = groups1 if one else groups2
                pe.wait_ge(*s_nl.at("ffn" if one else "mlp2", DC - 1))
                assert len(jobs) % 2 == 1 or True
                for key, by in jobs[-2:]:
                    pe.wait_ge(*by.at(*key))
                for gi, (f0, fn) in enumerate(groups):
                    w0 = W[f"gate{f0}" if one else f"up2_{f0}"]
                    n_up = 2 * fn if one else fn
                    last = gi == len(groups) - 1
                    p0 = len(jobs) % 2
                    b0 = s_big.loop(stage, "up", gi, total=n_up)
                    r0 = s_rel.base(stage, "up", gi)
                    with pe.Fori(0, n_up // 2, 1) as i:
                        for u in range(2):
                            pe.wait_ge(s_wlo.sem, i * 2 + (w0 + u + 1))
                            pe.wait_ge(s_rel.sem, i * 2 + (r0 + u - 1))
                            passes(big[(p0 + u) % 2], P, (w0 + u) % 2, chunk_terms(g2h, g2l)).then_inc(s_big.sem, 1)
                    for n in range(n_up):
                        s_big.known[("w", w0 + n)] = b0 + n + 1
                    jobs.extend([None] * n_up)
                    w1 = w0 + n_up
                    n_down = DC
                    b1 = s_big.loop(stage, "down", gi, total=n_down)
                    r1 = s_rel.base(stage, "down", gi)
                    a1 = s_mgl.base(stage, gi)
                    with pe.Fori(0, n_down // 2, 1) as i:
                        for u in range(2):
                            pe.wait_ge(s_wlo.sem, i * 2 + (w1 + u + 1))
                            pe.wait_ge(s_rel.sem, i * 2 + (r1 + u - 1))
                            ready = (lambda k: (s_mgl.sem, a1 + k + 1) if k >= fn - 2 else None) if u == 0 else (lambda k: None)
                            passes(big[(p0 + u) % 2], P, (w1 + u) % 2, chunk_terms(g1h, g1l, fn, ready=ready)).then_inc(s_big.sem, 1)
                    for n in range(n_down):
                        s_big.known[("w", w1 + n)] = b1 + n + 1
                        if last:
                            s_big.known[(stage, n)] = b1 + n + 1
                    jobs.extend([((stage, n), s_rel) if last else None for n in range(n_down)])
                    for n in range(n_down):
                        if last:
                            pair[(stage, n)] = (p0 + n) % 2
                    pair[(stage, "p0", gi)] = p0
            elif stage == "dnorm":
                which, h = x
                pe.wait_ge(*s_msq.at(which, h))
                sq = nb["y"]["sq"][0 if which == "dq" else 1]
                full_product(("dnorm", which, h), s_arel, [(blocks[:, :], sq[:, :])])
            elif stage == "donorm":
                h, = x
                pe.wait_ge(*s_msq.at("do", h))
                full_product(("donorm", h), s_arel, [(ones[:, :], nb["y"]["sq"][h % 2][:, :])])
            elif stage == "uqr":
                terms = lambda pr: [(2 * P * k + P * pr, clh[:, k, :], cll[:, k, :], s_nl.at("q_a", k)) for k in range(2)]
                for pr in range(2):
                    weight_job("uqr", ("uqr", pr), P, terms(pr), end=pr == 1)
            elif stage == "mh":
                h, = x
                q = [(P * k, clh[:, k, :], cll[:, k, :], None) for k in range(2)]
                kv = lambda n: [(P * (2 + n), clh[:, 2, :], cll[:, 2, :], s_nl.at("kv_a", 0))]
                weight_job(f"mh{h}", ("mh", h, "q"), P, q, end=False)
                weight_job(f"mh{h}", ("mh", h, "k"), P, kv(0), end=False)
                weight_job(f"mh{h}", ("mh", h, "v"), P, kv(1))
            elif stage == "mn1":
                which, h = x
                pe.wait_ge(*s_msq.at(which, h))
                r = HD * (h % 2)
                n = mnorms.index((which, h))
                rope_sq = sqr[h // 2 if which == "q" else 2]
                out = take(("mn", which, h), s_arel)
                for b in range(2):
                    c = slice(HALF * b, HALF * b + HALF)
                    pe.matmul(out[:, c], ones[:, :], sqn[n % 2][:, c], start=True, stop=False)
                    ins = pe.matmul(out[:, c], ones[r:r + HD, :], rope_sq[r:r + HD, c], start=False, stop=True)
                ins.then_inc(*s_big.mark("mn", which, h))
            elif stage == "yout":
                j, = x
                pe.wait_ge(*s_rel.at("mlp2", j))
                out = take(("yout", j), s_rel)
                for i in range(QT):
                    ins = pe.transpose(out[:, P * i:P * i + P], xres[:, j, P * i:P * i + P], ident[:, :])
                ins.then_inc(*s_big.mark("yout", j))

    @block.scalar
    def _(act):
        tn, pn, rn = [0], [0], [0]
        pt_log = []

        def split(w):
            if w >= NW:
                return
            act.wait_ge(*w_in_dma[w % 2].at(w))
            if w >= 2:
                act.wait_ge(*s_big.at("w", w - 2))
            act.activation(w_hi[w % 2][:, :], w_raw[w % 2][:, :], ACT.Copy).then_inc(*s_whi.mark(w))

        def norm(key, j, xj, ready, gain, dest, free=()):
            act.wait_ge(*ready)
            for f in free:
                act.wait_ge(*f)
            g = GAINS[gain][0] + j
            n = nb_of(key)
            if dest is not None:
                act.activation(dest, xj, ACT.Copy, scale=gains[:, g:g + 1]).then_inc(*s_nh.mark(key, j))
            if j >= 2:
                act.wait_ge(*s_ss.at(key, j - 2))
            act.activation(n["sq"][j % 2][:, :], xj, ACT.Square).then_inc(*s_sq.mark(key, j))

        def read_bank(key, dest, width, free=()):
            act.wait_ge(*s_tb.at(*key))
            for f in free:
                act.wait_ge(*f)
            src = tbank[tn[0] % 2][:, 0:width]
            if len(dest.shape) == 3:
                src = src.rearrange("p (i m) -> p i m", i=dest.shape[1])
            act.activation(dest, src, ACT.Copy).then_inc(*s_te.mark(*key))
            tn[0] += 1

        def root(key, mean, dest, free=()):
            act.wait_ge(*s_big.at(*key))
            for f in free:
                act.wait_ge(*f)
            act.activation(dest, big[pair[key]][:, :], ACT.Sqrt, scale=mean, bias=eps_c[:, :]).then_inc(*s_arel.mark(*key))

        act.wait_ge(*s_cst[1].at())
        act.wait_ge(*s_mm.at("ones"))
        split(0)
        for stage, *x in S:
            wname = {"rope": lambda: x[0], "lin": lambda: x[0], "kiwi": lambda: "kiwi", "kbvb": lambda: "kbvb",
                     "gate": lambda: f"ga{x[0]}" if x[0] < DC else f"gb{x[0] - DC}", "up": lambda: f"up{x[0]}",
                     "out": lambda: f"out{x[0]}", "out2": lambda: f"out2_{x[0]}", "uqr": lambda: "uqr",
                     "mh": lambda: f"mh{x[0]}", "krope": lambda: "kr"}.get(stage)
            if wname:
                split(W[wname()] + 1)
            if stage == "lam":
                act.wait_ge(*s_big.at("lam"))
                act.activation(lam_e[:, 0:2], big[pair[("lam",)]][:, 0:2], ACT.Exp).then_inc(*s_arel.mark("lam"))
            elif stage == "xin":
                j, = x
                norm("mix", j, xs[j % 2][:, :], s_rel.at("xin", j), "mix", g1h[:, j, :],
                     [s_bsp[0].at(2), s_bsp[1].at(3)] if j == 0 else [])
            elif stage == "ss":
                key, = x
                root(("ss", key), {"q_a": 1 / 256, "kv_a": 1 / 128}.get(key, 1 / D), root_of(key)[:, :],
                     [s_r.at("q_a")] if key == "kv_a" else [])
            elif stage == "wi_t":
                read_bank(("t", "wi", 0), wiT[:, :, :], 8 * QT)
            elif stage == "vb_t":
                read_bank(("t", "vb", 0), vbb[:, :, :], HD * QT, [s_ptu.at("end", a_steps[3][-1])])
            elif stage == "v_t":
                name, = x
                c = int(name[2])
                dest = {"v": vab[c % 2], "d": dvb[c % 2], "m": mvb[c]}[name[0]]
                old = {"v": a_steps, "d": d_steps}.get(name[0], {}).get(c - 2)
                for b in range(2):
                    read_bank(("t", name, b), dest[:, 4 * b:4 * b + 4, :], HALF,
                              [s_ptu.at("end", old[-1])] if old and b == 0 else [])
            elif stage == "idx":
                c, = x
                for hh in range(2):
                    for i in range(2, QT):
                        key = ("idx", c, hh, i)
                        act.wait_ge(*s_big.at(*key))
                        if rn[0] >= 2:
                            act.wait_ge(s_acc.sem, rn[0] - 1)
                        n = P * (i + 1)
                        act.activation(rel[rn[0] % 2][:, 0:n], big[pair[key]][:, 0:n], ACT.Relu).then_inc(*s_arel.mark(*key))
                        rn[0] += 1
            elif stage == "gate":
                j, = x
                name = f"ga{j}" if j < DC else f"gb{j - DC}"
                act.wait_ge(*s_rel.at(name))
                act.activation(gst[j % 2][:, :], gst[j % 2][:, :], ACT.Sigmoid).then_inc(*s_sg.mark(j))
            elif stage == "sc":
                s, = x
                st = step_of(s)
                n = nstep[s]
                for ti, i in enumerate(st["tiles"]):
                    for m in range(len(st["maps"])):
                        key = ("sc",) + s + (ti, m)
                        act.wait_ge(*s_rel.at(*key))
                        p = st["prob"][m][n % 2][:, ti, 0:keys(st, i)]
                        c = 4 * (n % 2) + 2 * ti + m
                        act.activation(p, p, ACT.Exp, scale=-1.0, bias=mn[:, c:c + 1],
                                       accum_out=sm[:, c:c + 1]).then_inc(*s_ex.mark(*key))
            elif stage == "pv":
                s, = x
                st = step_of(s)
                for t, group in enumerate(tgroups(st)):
                    width = group[-1][1] + group[-1][2]
                    read_bank((s, t), st["pt"][pn[0] % 3][:, 0:width], width,
                              [s_ptu.at(*pt_log[-3])] if len(pt_log) >= 3 else [])
                    pt_log.append((s, t))
                    pn[0] += 1
            elif stage in ("ysplit", "y2split"):
                two = stage == "y2split"
                for j in range(DC):
                    if two:
                        src = ym[:, j, :] if j < 4 else yd[:, j - 4, :]
                        act.wait_ge(*s_oe.at(m_steps[3][-1]))
                        dest = g1h
                    else:
                        src = ya[:, j, :] if j < 4 else yb[:, j - 4, :]
                        act.wait_ge(*s_oe.at(b_steps[3][-1]))
                        dest = g2h
                    act.activation(dest[:, j, :], src, ACT.Copy).then_inc(*s_yh.mark(*(("y2", j) if two else (j,))))
            elif stage == "up":
                j, = x
                act.wait_ge(*s_mg.at(j))
                act.activation(g1h[:, j, :], ta[:, :], ACT.Copy).then_inc(*s_mgh.mark("m", j))
            elif stage in ("out", "out2"):
                j, = x
                norm("ffn" if stage == "out" else "mlp2", j, xres[:, j, :], s_rel.at(stage, j),
                     "ffn" if stage == "out" else "mlp2", g2h[:, j, :])
            elif stage in ("mlp1", "mlp2"):
                one = stage == "mlp1"
                for gi, (f0, fn) in enumerate(groups1 if one else groups2):
                    last = gi == len(groups1 if one else groups2) - 1
                    n_up = 2 * fn if one else fn
                    w0 = W[f"gate{f0}" if one else f"up2_{f0}"]
                    b0, r0 = s_big.base(stage, "up", gi), s_rel.base(stage, "up", gi)
                    h0 = s_mgh.loop(stage, gi, total=fn)
                    g0 = s_sg.loop(stage, gi, total=fn) if one else 0
                    v0 = s_dv.base(stage, gi)
                    l0 = [w_in_dma[s].base("before", w0) for s in range(2)]
                    s_whi.count += n_up
                    with act.Fori(0, n_up // 2, 1) as i:
                        for u in range(2):
                            sl = (w0 + u + 1) % 2
                            act.wait_ge(w_in_dma[sl].sem, i * 16 + (l0[sl] + 16 * (1 + (u == 1))))
                            act.wait_ge(s_big.sem, i * 2 + (b0 + u))
                            act.activation(w_hi[sl][:, :], w_raw[sl][:, :], ACT.Copy).then_inc(s_whi.sem, 1)
                            if one and u == 0:
                                act.wait_ge(s_rel.sem, i * 2 + (r0 + 1))
                                act.activation(tsil[:, :], tg[:, :], ACT.Silu).then_inc(s_sg.sem, 1)
                            elif one:
                                act.wait_ge(s_rel.sem, i * 2 + (r0 + 2))
                                act.activation(g1h[:, i, :], tact[:, :], ACT.Copy).then_inc(s_mgh.sem, 1)
                            else:
                                act.wait_ge(s_dv.sem, i * 2 + (v0 + u + 1))
                                act.activation(g1h[:, i * 2 + u, :], tact[:, :], ACT.Copy).then_inc(s_mgh.sem, 1)
                    w1 = w0 + n_up
                    b1 = s_big.base(stage, "down", gi)
                    if last:
                        for j in range(DC):
                            split(w1 + j + 1)
                            if one:
                                norm("final", j, xres[:, j, :], s_rel.at("mlp1", j), "final", None)
                    else:
                        l1 = [w_in_dma[s].base("before", w1) for s in range(2)]
                        s_whi.count += DC
                        with act.Fori(0, DC // 2, 1) as i:
                            for u in range(2):
                                sl = (w0 + u + 1) % 2
                                act.wait_ge(w_in_dma[sl].sem, i * 16 + (l1[sl] + 16 * (1 + (u == 1))))
                                act.wait_ge(s_big.sem, i * 2 + (b1 + u))
                                act.activation(w_hi[sl][:, :], w_raw[sl][:, :], ACT.Copy).then_inc(s_whi.sem, 1)
            elif stage == "x1":
                j, = x
                norm("attn2", j, xres[:, j, :], s_hn.at("x1", j), "attn2", g2h[:, j, :])
            elif stage == "dnorm":
                which, h = x
                z = (dqb if which == "dq" else dkb)[h % 2]
                sq = nb["y"]["sq"][0 if which == "dq" else 1]
                act.wait_ge(*s_rel.at(f"{which}{h}"))
                if h:
                    act.wait_ge(*s_big.at("dnorm", which, h - 1))
                act.activation(sq[:, :], z[:, :], ACT.Square).then_inc(*s_msq.mark(which, h))
                prev = ("dq", h) if which == "dk" else ("dk", h - 1)
                root(("dnorm", which, h), 1 / HD, nb["y"]["rt"][:, :], [s_hn.at(*prev)] if prev[1] >= 0 else [])
            elif stage == "donorm":
                h, = x
                act.wait_ge(*s_oe.at(d_steps[h][-1]))
                if h >= 2:
                    act.wait_ge(*s_big.at("donorm", h - 2))
                act.activation(nb["y"]["sq"][h % 2][:, :], yd[:, h, :], ACT.Square).then_inc(*s_msq.mark("do", h))
                root(("donorm", h), 1 / P, nb["y"]["rt"][:, :], [s_hn.at("do", h - 1) if h else s_hn.at("dk", 3)])
            elif stage == "mn1":
                which, h = x
                n = mnorms.index((which, h))
                z = (mqn if which == "q" else mkn)[h]
                act.wait_ge(*s_rel.at("mh", h, which))
                if n >= 2:
                    act.wait_ge(*s_big.at("mn", *mnorms[n - 2]))
                if which == "q" and h % 2 == 0:
                    act.wait_ge(*s_rot.at("uqr", h // 2))
                    act.activation(sqr[h // 2][:, :], mqr[h // 2][:, :], ACT.Square)
                if which == "k" and h == 0:
                    act.wait_ge(*s_rot.at("kr"))
                    act.activation(sqr[2][:, :], krb[:, :], ACT.Square)
                act.activation(sqn[n % 2][:, :], z[:, :], ACT.Square).then_inc(*s_msq.mark(which, h))
            elif stage == "mn2":
                which, h = x
                n = mnorms.index((which, h))
                root(("mn", which, h), 1 / MLA_QK, mrt[:, :],
                     [s_hn.at(*(("m" + mnorms[n - 1][0], mnorms[n - 1][1])))] if n else [])
            if stage == "lin" and x[0] in ("cq0", "cq1", "ckv"):
                n = {"cq0": 0, "cq1": 1, "ckv": 2}[x[0]]
                norm("kv_a" if n == 2 else "q_a", n % 2, cqf[n][:, :], s_rel.at(x[0]), "kv_a" if n == 2 else "q_a",
                     clh[:, n, :], [s_ss.at("q_a", 0)] if n == 2 else [])

    @block.vector
    def _(dve):
        def step(ins, *key):
            ins.then_inc(*s_dv.mark(*key))
            dve.wait_ge(s_dv.sem, s_dv.count)

        rot_log = []
        on = [0]

        def rope(key, z, rows, cs, sn, reader=None):
            if rot_log:
                dve.wait_ge(*s_rot.at(*rot_log[-1]))
            dve.tensor_tensor(rot1[0:rows, :], z[0:rows, :], cs[0:rows, :], ALU.mult)
            for b in range(0, rows, HD):
                for d, e in ((b, b + 32), (b + 32, b)):
                    ins = dve.tensor_tensor(rot2[d:d + 32, :], z[e:e + 32, :], sn[e:e + 32, :], ALU.mult)
            rot_log.append(key)
            return ins

        def norm_lo(key, j, xj, gain, hi, lo):
            g = GAINS[gain][0] + j
            dve.wait_ge(*s_nh.at(key, j))
            dve.scalar_tensor_tensor(out=lo, in0=xj, scalar=gains[:, g:g + 1], in1=hi.bitcast(F32), op0=ALU.mult,
                                     op1=ALU.subtract).then_inc(*s_nl.mark(key, j))

        def scaled(key, dest, ps, r, *free):
            dve.wait_ge(*s_big.at(*key))
            for f in free:
                dve.wait_ge(*f)
            dve.tensor_tensor(dest, ps, r, ALU.mult).then_inc(*s_rel.mark(*key))

        dve.memset(ones[:, :], 1.0)
        dve.memset(eps_c[:, :], EPS).then_inc(*s_mm.mark("ones"))
        dve.wait_ge(*s_cst[0].at())
        dve.wait_ge(*s_cst[1].at())
        dve.wait_ge(*s_mm.at("ones"))
        g = GAINS["dout"][0]
        step(dve.tensor_scalar(gains[:, g:g + 1], gains[:, g:g + 1], 1.0 - LAM_INIT, None, ALU.mult), "gain")
        acc_seen = set()
        for stage, *x in S:
            if stage == "biasrow":
                h, = x
                if h:
                    dve.wait_ge(*s_big.at("br", h - 1, 1))
                dve.tensor_scalar(tabr[:, :], ones[0:32, :], tab[:, h:h + 1], 1.0 / ATTN_SCALE, ALU.mult,
                                  ALU.mult).then_inc(*s_mm.mark("tabr", h))
                for q in range(2):
                    dve.wait_ge(*s_big.at("br", h, q))
                    if h >= 2 and q == 0:
                        dve.wait_ge(*s_bsp[h % 2].at(h - 2))
                    dve.tensor_copy(brow[h % 2][:, T * q:T * q + T], big[pair[("br", h, q)]][:, :]).then_inc(*s_rel.mark("br", h, q))
            elif stage == "lam":
                dve.tensor_tensor(lam_v[:, 4:6], lam_v[:, 0:4:2], lam_v[:, 1:4:2], ALU.mult).then_inc(*s_mm.mark("lamp"))
                dve.wait_ge(*s_arel.at("lam"))
                dve.scalar_tensor_tensor(out=lam_e[:, 2:3], in0=lam_e[:, 1:2], scalar=LAM_INIT, in1=lam_e[:, 0:1],
                                         op0=ALU.subtract, op1=ALU.subtract).then_inc(*s_fin.mark("lam"))
            elif stage == "xin":
                j, = x
                dve.wait_ge(*s_big.at("xin", j))
                if j >= 2:
                    dve.wait_ge(*s_sp[j % 2].at("xin", j - 2))
                    dve.wait_ge(*s_sq.at("mix", j - 2))
                    dve.wait_ge(*s_nl.at("mix", j - 2))
                dve.tensor_copy(xs[j % 2][:, :], big[pair[("xin", j)]][:, :]).then_inc(*s_rel.mark("xin", j))
                norm_lo("mix", j, xs[j % 2][:, :], "mix", g1h[:, j, :], g1l[:, j, :])
            elif stage == "ss":
                key, = x
                dve.wait_ge(*s_arel.at("ss", key))
                dve.reciprocal(r_of(key)[:, :], root_of(key)[:, :]).then_inc(*s_r.mark(key))
                if key == "final":
                    dve.wait_ge(*s_r.at(key))
                else:
                    dve.wait_ge(*s_r.at(key))
            elif stage == "tables":
                dve.wait_ge(*s_tabl.at(x[0]))
                if x[0] == "b1":
                    for t in (cosr, sinr):
                        ins = dve.tensor_tensor(t[:, :], t[:, :], r_rep[:, :], ALU.mult)
                    step(ins, "tables")
                    late_rope()
            elif stage == "rope":
                name, = x
                if name == "qi0":
                    def late_rope():
                        dve.wait_ge(*s_big.at("qi0"))
                        rope(("qi0",), big[pair[("qi0",)]], P, cosr, sinr).then_inc(*s_rel.mark("qi0"))
                else:
                    dve.wait_ge(*s_big.at(name))
                    rope((name,), big[pair[(name,)]], P, cosr, sinr).then_inc(*s_rel.mark(name))
            elif stage == "kiwi":
                dve.wait_ge(*s_big.at("kiwi"))
                ps = big[pair[("kiwi",)]]
                rope(("kiwi",), ps, HD, cosr, sinr)
                dve.scalar_tensor_tensor(out=wif[HD:HD + 8, :], in0=ps[HD:HD + 8, :], scalar=IDX_SCALE,
                                         in1=r_rep[HD:HD + 8, :], op0=ALU.mult, op1=ALU.mult).then_inc(*s_rel.mark("kiwi"))
            elif stage == "kbvb":
                dve.wait_ge(*s_big.at("kbvb"))
                ps = big[pair[("kbvb",)]]
                rope(("kbvb",), ps, HD, cosr, sinr)
                dve.wait_ge(*s_tb.at("t", "va3", 1))
                dve.tensor_tensor(vf[HD:P, :], ps[HD:P, :], r_rep[HD:P, :], ALU.mult).then_inc(*s_rel.mark("kbvb"))
            elif stage == "lin":
                name, = x
                kind, c = name[:2], name[2:]
                free = []
                if kind == "va" and c != "0":
                    free = [s_tb.at("t", f"va{int(c) - 1}", 1)]
                if kind == "dv" and c != "0":
                    free = [s_tb.at("t", f"dv{int(c) - 1}", 1)]
                if kind in ("dq", "dk") and int(c) >= 2:
                    free = [s_big.at("sc", *d_steps[int(c) - 2][-1], 1, 1)]
                if name == "dv0":
                    def late_lin():
                        scaled(("dv0",), dvf[:, :], big[pair[("dv0",)]][:, :], r_rep[:, :],
                               s_sp[0].at("x1", DC - 2), s_sp[1].at("x1", DC - 1))
                else:
                    if name == "dq0":
                        late_lin()
                    scaled((name,), lin_dest[name][:, :], big[pair[(name,)]][:, :], r_rep[:, :], *free)
                if name in ("cq0", "cq1", "ckv"):
                    n = {"cq0": 0, "cq1": 1, "ckv": 2}[name]
                    key = "kv_a" if n == 2 else "q_a"
                    dve.wait_ge(*s_rel.at(name))
                    norm_lo(key, n % 2, cqf[n][:, :], key, clh[:, n, :], cll[:, n, :])
            elif stage == "krope":
                scaled(("kr",), krz[:, :], big[pair[("kr",)]][:, :], r_rep[:, :])
                dve.wait_ge(*s_rel.at("kr"))
                dve.wait_ge(*s_tabl.at("b2"))
                rope(("kr",), krz, P, cosr, sinr).then_inc(*s_dv.mark("kr"))
            elif stage == "uqr":
                for pr in range(2):
                    dve.wait_ge(*s_dv.at("kr" if pr == 0 else "uqr0"))
                    scaled(("uqr", pr), krz[:, :], big[pair[("uqr", pr)]][:, :], r_rep[:, :])
                    dve.wait_ge(*s_rel.at("uqr", pr))
                    rope(("uqr", pr), krz, P, cosr, sinr).then_inc(*s_dv.mark(f"uqr{pr}"))
            elif stage == "mh":
                h, = x
                if h:
                    vfree = [s_tb.at("t", f"mv{h - 1}", 1)]
                else:
                    vfree = []
                scaled(("mh", h, "q"), mqn[h][:, :], big[pair[("mh", h, "q")]][:, :], r_rep[:, :])
                scaled(("mh", h, "k"), mkn[h][:, :], big[pair[("mh", h, "k")]][:, :], rkv[:, :])
                scaled(("mh", h, "v"), mvf[:, :], big[pair[("mh", h, "v")]][:, :], rkv[:, :], *vfree)
            elif stage == "idx":
                c, = x
                dve.wait_ge(*s_te.at("t", "wi", 0))
                for hh in range(2):
                    for i in range(2, QT):
                        key = ("idx", c, hh, i)
                        h = 2 * c + hh
                        w = wiT[:, i, h:h + 1]
                        z = acc[:, acc_at[i]:acc_at[i + 1]]
                        r = rel[s_acc.count % 2][:, 0:P * (i + 1)]
                        dve.wait_ge(*s_arel.at(*key))
                        if h == 0:
                            ins = dve.tensor_scalar(z, r, w, None, ALU.mult)
                        else:
                            dve.wait_ge(*s_acc.at("idx", (h - 1) // 2, (h - 1) % 2, i))
                            ins = dve.scalar_tensor_tensor(out=z, in0=r, scalar=w, in1=z, op0=ALU.mult, op1=ALU.add)
                        ins.then_inc(*s_acc.mark(*key))
            elif stage == "fill":
                dve.wait_ge(*s_cst[2].at())
                dve.wait_ge(s_acc.sem, s_acc.count)
                dve.memset(acc[:, 0:acc_at[2]], 0.0).then_inc(*s_tk.mark("zero"))
                for i in range(2, QT):
                    z = acc[:, acc_at[i + 1] - P:acc_at[i + 1]]
                    dve.tensor_tensor(z, z, causal[:, :], ALU.add).then_inc(*s_tk.mark("fill", i))
                dve.wait_ge(s_tk.sem, s_tk.count)
                for i in range(2):
                    dve.tensor_copy(acc[:, acc_at[i + 1] - P:acc_at[i + 1]], causal[:, :]).then_inc(*s_tk.mark("fill", i))
                dve.wait_ge(s_tk.sem, s_tk.count)
            elif stage == "topk":
                for n in range(x[0], x[1]):
                    i, r = rounds[n]
                    z = acc[:, acc_at[i]:acc_at[i + 1]]
                    dve.max(m8[:, :], z).then_inc(*s_tk.mark("max", n))
                    dve.wait_ge(*s_tk.at("max", n))
                    dve.match_replace(z, m8[:, :], z, TAKEN).then_inc(*s_tk.mark("take", n))
                    dve.wait_ge(*s_tk.at("take", n))
            elif stage == "mask":
                for i in range(2, QT):
                    z = acc[:, acc_at[i]:acc_at[i + 1]]
                    dve.tensor_scalar(z, z, -3.2e38, MASKED, ALU.is_gt, ALU.mult).then_inc(*s_tk.mark("mask", i))
                dve.wait_ge(s_tk.sem, s_tk.count)
            elif stage == "gate":
                j, = x
                name = f"ga{j}" if j < DC else f"gb{j - DC}"
                scaled((name,), gst[j % 2][:, :], big[pair[(name,)]][:, :], r_rep[:, :],
                       *([s_gsp[j % 2].at(j - 2)] if j >= 2 else []))
            elif stage == "sc":
                s, = x
                st = step_of(s)
                n = nstep[s]
                maps = len(st["maps"])
                if n >= 2:
                    dve.wait_ge(*s_ptu.at("end", steps[n - 2]))
                if s[0] == "a" and n == 0:
                    dve.wait_ge(*s_cst[2].at())
                if s[0] == "d":
                    dve.wait_ge(*s_bl[s[1] % 2].at(s[1]))
                for ti, i in enumerate(st["tiles"]):
                    for m in range(maps):
                        key = ("sc",) + s + (ti, m)
                        dve.wait_ge(*s_big.at(*key))
                        nk = keys(st, i)
                        p = st["prob"][m][n % 2][:, ti, 0:nk]
                        c = 4 * (n % 2) + 2 * ti + m
                        ps = big[pair[key]][:, 0:nk]
                        if st["bias"] is None:
                            ins = dve.tensor_scalar(p, ps, -st["scale"], 3e38, ALU.mult, ALU.min, accum_out=mn[:, c:c + 1])
                        else:
                            ins = dve.tensor_tensor_reduce(p, ps, st["bias"](i), -st["scale"], 3e38, ALU.add, ALU.min,
                                                           mn[:, c:c + 1])
                        ins.then_inc(*s_rel.mark(*key))
                for ti, i in enumerate(st["tiles"]):
                    nk = keys(st, i)
                    c = 4 * (n % 2) + 2 * ti
                    p0 = st["prob"][0][n % 2][:, ti, 0:nk]
                    dve.wait_ge(*s_ex.at("sc", *s, ti, maps - 1))
                    step(dve.reciprocal(rc[:, c:c + maps], sm[:, c:c + maps]), "rc", s, ti)
                    if maps == 1:
                        dve.tensor_scalar(p0, p0, rc[:, c:c + 1], None, ALU.mult).then_inc(*s_nrm.mark(s, ti))
                    else:
                        p1 = st["prob"][1][n % 2][:, ti, 0:nk]
                        step(dve.tensor_scalar(rc[:, c + 1:c + 2], rc[:, c + 1:c + 2], lam_e[:, 2:3], None, ALU.mult), "rl", s, ti)
                        step(dve.tensor_scalar(p1, p1, rc[:, c + 1:c + 2], None, ALU.mult), "p1", s, ti)
                        dve.scalar_tensor_tensor(out=p0, in0=p0, scalar=rc[:, c:c + 1], in1=p1, op0=ALU.mult,
                                                 op1=ALU.add).then_inc(*s_nrm.mark(s, ti))
            elif stage == "pv":
                s, = x
                st = step_of(s)
                if st["last"]:
                    g = s[2]
                    dve.wait_ge(*s_ptu.at("end", s))
                    dve.tensor_copy(st["y"][:, 2 * P * g:2 * P * g + 2 * P], obank[on[0] % 2][:, 0:2 * P]).then_inc(*s_oe.mark(s))
                    on[0] += 1
            elif stage in ("ysplit", "y2split"):
                two = stage == "y2split"
                if two:
                    dve.wait_ge(*s_oe.at(m_steps[3][-1]))
                for j in range(DC):
                    if two:
                        src, hi, lo = (ym[:, j, :] if j < 4 else yd[:, j - 4, :]), g1h[:, j, :], g1l[:, j, :]
                    else:
                        src, hi, lo = (ya[:, j, :] if j < 4 else yb[:, j - 4, :]), g2h[:, j, :], g2l[:, j, :]
                    key = ("y2", j) if two else (j,)
                    dve.wait_ge(*s_yh.at(*key))
                    dve.tensor_tensor(lo, src, hi.bitcast(F32), ALU.subtract).then_inc(*s_yl.mark(*key))
            elif stage == "up":
                j, = x
                for n, t in enumerate((ta, tb)):
                    free = [s_mgl.at("m", j - 1)] if j and n == 0 else []
                    scaled(("up", j, "ab"[n]), t[:, :], big[pair[("up", j, "ab"[n])]][:, :], sgab[n][:, :],
                           s_gl[n].at(j), *free)
                dve.wait_ge(*s_rel.at("up", j, "b"))
                dve.tensor_tensor(ta[:, :], ta[:, :], tb[:, :], ALU.add).then_inc(*s_mg.mark(j))
                dve.wait_ge(*s_mg.at(j))
            elif stage in ("out", "out2"):
                j, = x
                key = "ffn" if stage == "out" else "mlp2"
                dve.wait_ge(*s_xres.at(stage))
                dve.wait_ge(*s_big.at(stage, j))
                dve.tensor_tensor(xres[:, j, :], big[pair[(stage, j)]][:, :], xres[:, j, :], ALU.add).then_inc(*s_rel.mark(stage, j))
                dve.wait_ge(*s_rel.at(stage, j))
                norm_lo(key, j, xres[:, j, :], key, g2h[:, j, :], g2l[:, j, :])
            elif stage in ("mlp1", "mlp2"):
                one = stage == "mlp1"
                for gi, (f0, fn) in enumerate(groups1 if one else groups2):
                    last = gi == len(groups1 if one else groups2) - 1
                    p0 = pair[(stage, "p0", gi)]
                    n_up = 2 * fn if one else fn
                    b0 = s_big.base(stage, "up", gi)
                    r0 = s_rel.loop(stage, "up", gi, total=n_up)
                    a0, g0, q0 = s_mgl.base(stage, gi), s_sg.base(stage, gi), s_rot.base(stage, gi)
                    if one:
                        with dve.Fori(0, fn, 1) as i:
                            dve.wait_ge(s_big.sem, i * 2 + (b0 + 1))
                            dve.wait_ge(s_sg.sem, i + g0)
                            dve.tensor_tensor(tg[:, :], big[p0][:, :], r_rep[:, :], ALU.mult).then_inc(s_rel.sem, 1)
                            dve.wait_ge(s_big.sem, i * 2 + (b0 + 2))
                            dve.wait_ge(s_rot.sem, i + (q0 + 1))
                            dve.wait_ge(s_mgl.sem, i + a0)
                            dve.tensor_tensor(tact[:, :], big[1 - p0][:, :], tsil[:, :], ALU.mult).then_inc(s_rel.sem, 1)
                    else:
                        v0 = s_dv.loop(stage, gi, total=n_up)
                        with dve.Fori(0, n_up // 2, 1) as i:
                            for u in range(2):
                                dve.wait_ge(s_big.sem, i * 2 + (b0 + u + 1))
                                dve.wait_ge(s_dv.sem, i * 2 + (v0 + u))
                                dve.tensor_tensor(tg[:, :], big[(p0 + u) % 2][:, :], r_rep[:, :], ALU.mult).then_inc(s_rel.sem, 1)
                                dve.wait_ge(s_rel.sem, i * 2 + (r0 + u + 1))
                                dve.wait_ge(s_mgl.sem, i * 2 + (a0 + u))
                                dve.scalar_tensor_tensor(out=tact[:, :], in0=tg[:, :], scalar=0.0, in1=tg[:, :],
                                                         op0=ALU.max, op1=ALU.mult).then_inc(s_dv.sem, 1)
                    b1 = s_big.base(stage, "down", gi)
                    if last:
                        s_rel.known[(stage, "down", gi)] = s_rel.count
                        for j in range(DC):
                            dve.wait_ge(*s_big.at(stage, j))
                            dve.tensor_tensor(xres[:, j, :], big[pair[(stage, j)]][:, :], xres[:, j, :],
                                              ALU.add).then_inc(*s_rel.mark(stage, j))
                    else:
                        r1 = s_rel.loop(stage, "down", gi, total=DC)
                        with dve.Fori(0, DC // 2, 1) as i:
                            for u in range(2):
                                dve.wait_ge(s_big.sem, i * 2 + (b1 + u + 1))
                                dve.tensor_tensor(xres[:, i * 2 + u, :], big[(p0 + u) % 2][:, :], xres[:, i * 2 + u, :],
                                                  ALU.add).then_inc(s_rel.sem, 1)
            elif stage == "x1":
                j, = x
                gcol = GAINS["final"][0] + j
                xj = xres[:, j, :]
                dve.wait_ge(*s_sq.at("final", j))
                dve.scalar_tensor_tensor(out=xj, in0=xj, scalar=gains[:, gcol:gcol + 1], in1=r_rep[:, :], op0=ALU.mult,
                                         op1=ALU.mult).then_inc(*s_hn.mark("x1", j))
                dve.wait_ge(*s_hn.at("x1", j))
                norm_lo("attn2", j, xj, "attn2", g2h[:, j, :], g2l[:, j, :])
            elif stage in ("dnorm", "donorm"):
                if stage == "dnorm":
                    which, h = x
                    key, gain, z = ("dnorm", which, h), which, (dqb if which == "dq" else dkb)[h % 2][:, :]
                    out = (which, h)
                else:
                    h, = x
                    key, gain, z, out = ("donorm", h), "dout", yd[:, h, :], ("do", h)
                rt = nb["y"]["rt"]
                dve.wait_ge(*s_arel.at(*key))
                step(dve.reciprocal(rt[:, :], rt[:, :]), "hr", *out)
                gcol = GAINS[gain][0]
                dve.scalar_tensor_tensor(out=z, in0=z, scalar=gains[:, gcol:gcol + 1], in1=rt[:, :], op0=ALU.mult,
                                         op1=ALU.mult).then_inc(*s_hn.mark(*out))
            elif stage == "mn2":
                which, h = x
                r = HD * (h % 2)
                dve.wait_ge(*s_arel.at("mn", which, h))
                step(dve.reciprocal(mrt[:, :], mrt[:, :]), "mr", which, h)
                z = (mqn if which == "q" else mkn)[h][:, :]
                g = GAINS[f"m{which}_n"][0]
                dve.scalar_tensor_tensor(out=z, in0=z, scalar=gains[:, g:g + 1], in1=mrt[:, :], op0=ALU.mult, op1=ALU.mult)
                g = GAINS[f"m{which}_r"][0]
                src = (mqr[h // 2] if which == "q" else krb)[r:r + HD, :]
                dest = (mqr if which == "q" else mkr)[h // 2][r:r + HD, :]
                dve.scalar_tensor_tensor(out=dest, in0=src, scalar=gains[r:r + HD, g:g + 1], in1=mrt[r:r + HD, :],
                                         op0=ALU.mult, op1=ALU.mult).then_inc(*s_hn.mark("m" + which, h))
            elif stage == "yout":
                j, = x
                dve.wait_ge(*s_big.at("yout", j))
                if j >= 2:
                    dve.wait_ge(*s_out[j % 2].at(j - 2))
                dve.tensor_copy(yst[j % 2][:, :, :].rearrange("p i m -> p (i m)"), big[pair[("yout", j)]][:, :]).then_inc(*s_rel.mark("yout", j))

    @block.gpsimd
    def _(pool):
        def split(w):
            if w >= NW:
                return
            s = w % 2
            pool.wait_ge(s_whi.sem, w + 1)
            pool.tensor_tensor(w_lo[s][:, :], w_raw[s][:, :], w_hi[s][:, :].bitcast(F32), ALU.subtract).then_inc(*s_wlo.mark(w))

        def add_squares(key, j):
            n = nb_of(key)
            pool.wait_ge(*s_sq.at(key, j))
            sq = n["sq"][j % 2][:, :]
            if j == 0:
                ins = pool.tensor_copy(ss_of(key)[:, :], sq)
            else:
                pool.wait_ge(*s_ss.at(key, j - 1))
                ins = pool.tensor_tensor(ss_of(key)[:, :], ss_of(key)[:, :], sq, ALU.add)
            ins.then_inc(*s_ss.mark(key, j))

        def rope_add(key, ready, dest, rows, free):
            pool.wait_ge(*ready)
            for f in free:
                pool.wait_ge(*f)
            pool.tensor_tensor(dest[0:rows, :], rot1[0:rows, :], rot2[0:rows, :], ALU.add).then_inc(*s_rot.mark(*key))

        split(0)
        for stage, *x in S:
            wname = {"rope": lambda: x[0], "lin": lambda: x[0], "kiwi": lambda: "kiwi", "kbvb": lambda: "kbvb",
                     "gate": lambda: f"ga{x[0]}" if x[0] < DC else f"gb{x[0] - DC}", "up": lambda: f"up{x[0]}",
                     "out": lambda: f"out{x[0]}", "out2": lambda: f"out2_{x[0]}", "uqr": lambda: "uqr",
                     "mh": lambda: f"mh{x[0]}", "krope": lambda: "kr"}.get(stage)
            if wname:
                split(W[wname()] + 1)
            if stage == "xin":
                add_squares("mix", x[0])
            elif stage == "rope":
                name, = x
                dest, free = rope_dest(name)
                rope_add((name,), s_rel.at(name), dest, P, [s_big.at(*k) if s == "big" else s_oe.at(*k[1:]) for s, k in free])
            elif stage == "kiwi":
                rope_add(("kiwi",), s_rel.at("kiwi"), kib, HD, [])
            elif stage == "kbvb":
                rope_add(("kbvb",), s_rel.at("kbvb"), kbb, HD, [s_oe.at(a_steps[3][-1])])
            elif stage == "krope":
                rope_add(("kr",), s_dv.at("kr"), krb, P, [])
            elif stage == "uqr":
                for pr in range(2):
                    rope_add(("uqr", pr), s_dv.at(f"uqr{pr}"), mqr[pr], P, [])
            elif stage == "up":
                j, = x
                pool.wait_ge(*s_mgh.at("m", j))
                pool.tensor_tensor(g1l[:, j, :], ta[:, :], g1h[:, j, :].bitcast(F32), ALU.subtract).then_inc(*s_mgl.mark("m", j))
            elif stage in ("out", "out2"):
                add_squares("ffn" if stage == "out" else "mlp2", x[0])
            elif stage == "x1":
                add_squares("attn2", x[0])
            elif stage == "lin" and x[0] in ("cq0", "cq1", "ckv"):
                n = {"cq0": 0, "cq1": 1, "ckv": 2}[x[0]]
                add_squares("kv_a" if n == 2 else "q_a", n % 2)
            elif stage in ("mlp1", "mlp2"):
                one = stage == "mlp1"
                for gi, (f0, fn) in enumerate(groups1 if one else groups2):
                    last = gi == len(groups1 if one else groups2) - 1
                    n_up = 2 * fn if one else fn
                    w0 = W[f"gate{f0}" if one else f"up2_{f0}"]
                    h0, g0 = s_mgh.base(stage, gi), s_sg.base(stage, gi)
                    s_mgl.loop(stage, gi, total=fn)
                    if one:
                        s_rot.loop(stage, gi, total=fn)
                    s_wlo.count += n_up
                    with pool.Fori(0, n_up // 2, 1) as i:
                        for u in range(2):
                            sl = (w0 + u + 1) % 2
                            pool.wait_ge(s_whi.sem, i * 2 + (w0 + u + 2))
                            pool.tensor_tensor(w_lo[sl][:, :], w_raw[sl][:, :], w_hi[sl][:, :].bitcast(F32),
                                               ALU.subtract).then_inc(s_wlo.sem, 1)
                            if one and u == 0:
                                pool.wait_ge(s_sg.sem, i + (g0 + 1))
                                pool.tensor_tensor(tsil[:, :], tsil[:, :], r_rep[:, :], ALU.mult).then_inc(s_rot.sem, 1)
                            elif one:
                                pool.wait_ge(s_mgh.sem, i + (h0 + 1))
                                pool.tensor_tensor(g1l[:, i, :], tact[:, :], g1h[:, i, :].bitcast(F32),
                                                   ALU.subtract).then_inc(s_mgl.sem, 1)
                            else:
                                pool.wait_ge(s_mgh.sem, i * 2 + (h0 + u + 1))
                                pool.tensor_tensor(g1l[:, i * 2 + u, :], tact[:, :], g1h[:, i * 2 + u, :].bitcast(F32),
                                                   ALU.subtract).then_inc(s_mgl.sem, 1)
                    w1 = w0 + n_up
                    if last:
                        for j in range(DC):
                            split(w1 + j + 1)
                            if one:
                                add_squares("final", j)
                    else:
                        s_wlo.count += DC
                        with pool.Fori(0, DC // 2, 1) as i:
                            for u in range(2):
                                sl = (w0 + u + 1) % 2
                                pool.wait_ge(s_whi.sem, i * 2 + (w1 + u + 2))
                                pool.tensor_tensor(w_lo[sl][:, :], w_raw[sl][:, :], w_hi[sl][:, :].bitcast(F32),
                                                   ALU.subtract).then_inc(s_wlo.sem, 1)

    @block.sync
    def _(sp):
        def load(w):
            if w >= NW:
                return
            if w >= 2:
                sp.wait_ge(s_wlo.sem, w - 1)
            w_in_dma[w % 2].known[("before", w)] = w_in_dma[w % 2].count
            for dst, src in chunks[w][1](w % 2):
                sp.dma_start(dst, src).then_inc(*w_in_dma[w % 2].mark(w, by=16))

        def column(name, col, rows, src, n=1):
            sp.dma_start(gains[rows[0]:rows[1], col:col + n], src, allow_slow_non_contiguous=True).then_inc(*s_cst[1].mark(by=16))

        def x_tile(j):
            sp.dma_start(xt[j % 2][:, :, :], a["x"][0].rearrange("(i p) d -> p i d", p=P)[:, :, P * j:P * j + P]).then_inc(
                *s_xl[j % 2].mark("xin", j, by=16))

        sp.dma_start(ident[:, :], a["ident"]).then_inc(*s_cst[0].mark(by=16))
        sp.dma_start(oh[:, :], a["onehot"]).then_inc(*s_cst[0].mark(by=16))
        sp.dma_start(tab[:, :], a["rel_bias_2"]).then_inc(*s_cst[0].mark(by=16))
        for n, v in enumerate(("lambda_q1_2", "lambda_k1_2", "lambda_q2_2", "lambda_k2_2")):
            sp.dma_start(lam_v[:, n:n + 1], a[v].rearrange("a d -> d a"), allow_slow_non_contiguous=True).then_inc(*s_cst[1].mark(by=16))
        for name, v in (("mix", "norm_mix"), ("ffn", "norm_ffn"), ("final", "norm_final"), ("attn2", "attn_norm_w_2"),
                        ("mlp2", "mlp_norm_w_2"), ("q_a", "q_a_norm_w_2"), ("kv_a", "kv_a_norm_w_2"), ("dout", "diff_out_norm_w_2")):
            vec = a[v] if len(a[v].shape) == 1 else a[v][0]
            column(name, GAINS[name][0], (0, P), vec.rearrange("(j p) -> p j", p=P), GAINS[name][1])
        for q, v in (("q", "mla_q_norm_w_2"), ("k", "mla_k_norm_w_2")):
            vec = a[v][0].rearrange("(p j) -> p j", j=1)
            column("", GAINS[f"m{q}_n"][0], (0, P), vec[0:P, :])
            for r in (0, HD):
                column("", GAINS[f"m{q}_r"][0], (r, r + HD), vec[P:P + HD, :])
            v = f"diff_{q}_norm_w_2"
            for r in (0, HD):
                column("", GAINS[f"d{q}"][0], (r, r + HD), a[v][0].rearrange("(p j) -> p j", j=1))
        x_tile(0)
        x_tile(1)
        load(0)
        load(1)
        for t, n in ((cosr, "cos_t"), (sinr, "sin_t")):
            sp.dma_start(t[:, :], a[n]).then_inc(*s_tabl.mark("b1", by=16))
        for t, n in ((abias, "abias"), (causal, "causal"), (blocks, "blocks")):
            sp.dma_start(t[:, :], a[n]).then_inc(*s_cst[2].mark(by=16))
        for stage, *x in S:
            wname = {"rope": lambda: x[0], "lin": lambda: x[0], "kiwi": lambda: "kiwi", "kbvb": lambda: "kbvb",
                     "gate": lambda: f"ga{x[0]}" if x[0] < DC else f"gb{x[0] - DC}", "up": lambda: f"up{x[0]}",
                     "out": lambda: f"out{x[0]}", "out2": lambda: f"out2_{x[0]}", "uqr": lambda: "uqr",
                     "mh": lambda: f"mh{x[0]}", "krope": lambda: "kr"}.get(stage)
            if wname:
                load(W[wname()] + 2)
            if stage == "biasrow":
                h, = x
                for q in range(2):
                    sp.wait_ge(*s_rel.at("br", h, q))
                sp.dma_start(b_spill[h].rearrange("(p m) -> p m", p=P), brow[h % 2][:, :]).then_inc(*s_bsp[h % 2].mark(h, by=16))
            elif stage == "xin":
                j, = x
                sp.wait_ge(*s_rel.at("xin", j))
                sp.dma_start(x_spill[j], xs[j % 2][:, :]).then_inc(*s_sp[j % 2].mark("xin", j, by=16))
                if j + 2 < DC:
                    sp.wait_ge(*s_big.at("xin", j))
                    x_tile(j + 2)
            elif stage in ("kiwi", "kbvb"):
                buf = kib if stage == "kiwi" else kbb
                sp.wait_ge(*s_rot.at(stage))
                sp.dma_start(buf[HD:P, :], buf[0:HD, :]).then_inc(*s_dup.mark(stage, by=16))
            elif stage == "gate":
                j, = x
                sp.wait_ge(*s_sg.at(j))
                sp.dma_start(g_spill[j], gst[j % 2][:, :]).then_inc(*s_gsp[j % 2].mark(j, by=16))
            elif stage == "ysplit":
                sp.wait_ge(*s_yl.at(DC - 1))
                for n in range(2):
                    sp.wait_ge(*s_gsp[n].at(2 * DC - 2 + n))
                    sp.wait_ge(*s_sp[n].at("xin", DC - 2 + n))
                for n in range(2):
                    sp.dma_start(sgab[n][:, :], g_spill[DC * n]).then_inc(*s_gl[n].mark(0, by=16))
                sp.dma_start(xres[:, :, :], x_spill.rearrange("j p t -> p j t")).then_inc(*s_xres.mark("out", by=16))
            elif stage == "up":
                j, = x
                if j + 1 < DC:
                    for n in range(2):
                        sp.wait_ge(*s_rel.at("up", j, "ab"[n]))
                        sp.dma_start(sgab[n][:, :], g_spill[DC * n + j + 1]).then_inc(*s_gl[n].mark(j + 1, by=16))
            elif stage in ("mlp1", "mlp2"):
                one = stage == "mlp1"
                for gi, (f0, fn) in enumerate(groups1 if one else groups2):
                    w0 = W[f"gate{f0}" if one else f"up2_{f0}"]
                    n_up = 2 * fn if one else fn
                    skip = 1 if gi == 0 else 0
                    for s in range(2):
                        w_in_dma[s].known[("before", w0)] = w_in_dma[s].count - (16 if gi == 0 else 0)
                    ups = (a["w_gate"][0], a["w_up"][0]) if one else (a["w_up_2"][0],) * 2
                    with sp.Fori(skip, n_up // 2, 1) as i:
                        for u in range(2):
                            sp.wait_ge(s_wlo.sem, i * 2 + (w0 + u - 1))
                            f = (i + f0) * P if one else (i * 2 + (f0 + u)) * P
                            src = ups[u].rearrange("(k p) m -> p k m", p=P)[:, :, bass.ds(f, P)]
                            sp.dma_start(raw((w0 + u) % 2, DC, P), src).then_inc(w_in_dma[(w0 + u) % 2].sem, 16)
                    for s in range(2):
                        w_in_dma[s].count += 16 * (n_up // 2 - skip)
                    w1 = w0 + n_up
                    for s in range(2):
                        w_in_dma[s].known[("before", w1)] = w_in_dma[s].count
                    down = a["w_down"][0] if one else a["w_down_2"][0]
                    with sp.Fori(0, DC // 2, 1) as i:
                        for u in range(2):
                            sp.wait_ge(s_wlo.sem, i * 2 + (w1 + u - 1))
                            src = down[P * f0:P * (f0 + fn), :].rearrange("(k p) m -> p k m", p=P)[:, :, bass.ds((i * 2 + u) * P, P)]
                            sp.dma_start(raw((w1 + u) % 2, fn, P), src).then_inc(w_in_dma[(w1 + u) % 2].sem, 16)
                    for n in range(DC):
                        s = (w1 + n) % 2
                        w_in_dma[s].known[(w1 + n,)] = w_in_dma[s].count + 16 * (n // 2 + 1)
                    for s in range(2):
                        w_in_dma[s].count += 16 * (DC // 2)
                w2 = W["down2_3_7" if not one else "down2_7"] + 1
                load(w2)
                load(w2 + 1)
            elif stage == "x1":
                j, = x
                sp.wait_ge(*s_hn.at("x1", j))
                sp.dma_start(x_spill[j], xres[:, j, :]).then_inc(*s_sp[j % 2].mark("x1", j, by=16))
            elif stage == "ss" and x[0] == "attn2":
                sp.wait_ge(*s_r.at("attn2"))
                for h in range(2):
                    load_bias(sp, h)
            elif stage == "pv" and x[0][0] == "d" and x[0][2] == 3 and x[0][1] < 2:
                h = x[0][1]
                sp.wait_ge(*s_rel.at("sc", *d_steps[h][-1], 1, 1))
                load_bias(sp, h + 2)
            elif stage == "tables" and x[0] == "b2":
                sp.wait_ge(*s_rel.at("sc", *d_steps[3][-1], 1, 1))
                for t, n in ((cosr, "cos_t"), (sinr, "sin_t")):
                    sp.dma_start(t[:, :], a[n]).then_inc(*s_tabl.mark("b2", by=16))
            elif stage == "y2split":
                sp.wait_ge(*s_yl.at("y2", DC - 1))
                for n in range(2):
                    sp.wait_ge(*s_sp[n].at("x1", DC - 2 + n))
                sp.dma_start(xres[:, :, :], x_spill.rearrange("j p t -> p j t")).then_inc(*s_xres.mark("out2", by=16))
            elif stage == "yout":
                j, = x
                sp.wait_ge(*s_rel.at("yout", j))
                sp.dma_start(a["out"][0].rearrange("(i p) d -> p i d", p=P)[:, :, P * j:P * j + P], yst[j % 2][:, :, :]).then_inc(
                    *s_out[j % 2].mark(j, by=16))
        for n in range(2):
            sp.wait_ge(*s_out[n].at(DC - 2 + n))


_INS = ["x", "norm_mix", "w_in", "w_up_a", "w_up_b", "w_out", "norm_ffn", "w_gate", "w_up", "w_down", "norm_final",
        "attn_norm_w_2", "w_in_2", "q_a_norm_w_2", "w_uq_2", "kv_a_norm_w_2", "w_ukv_2", "mla_q_norm_w_2",
        "mla_k_norm_w_2", "diff_q_norm_w_2", "diff_k_norm_w_2", "lambda_q1_2", "lambda_k1_2", "lambda_q2_2",
        "lambda_k2_2", "diff_out_norm_w_2", "w_out_2", "mlp_norm_w_2", "w_up_2", "w_down_2", "rel_bias_2"]


def kernel(**inputs):
    import concourse.bacc as _bacc
    from concourse.bass_utils import run_bass_kernel_spmd as _run

    arrays = {n: np.ascontiguousarray(inputs[n]) for n in _INS}
    arrays |= shape_constants()
    known = {}
    for _ in range(2):
        nc = _bacc.Bacc("TRN2", target_bir_lowering=False, num_devices=1)
        a = {n: nc.dram_tensor(f"in_{n}", v.shape, F32, kind="ExternalInput").ap() for n, v in arrays.items()}
        a["out"] = nc.dram_tensor("out_0", (1, T, D), F32, kind="ExternalOutput").ap()
        emit(nc, known, a)
    r = _run(nc, [{f"in_{n}": v for n, v in arrays.items()}], core_ids=[0])
    return r.results[0]["out_0"]
```

```python
from contextlib import ExitStack
import math

import numpy as np

import concourse.bass as bass
from concourse import mybir

F32 = mybir.dt.float32
F32R = mybir.dt.float32r
ACT = mybir.ActivationFunctionType
ALU = mybir.AluOpType
AX = mybir.AxisListType

P = 128
T = 1024
D = 1024
QT = T // P
DC = D // P
HALF = 512
CH = P * DC
HD = 64
TOPK = 256
D_FF = 2816
D_FF2 = 4096
EPS = 1e-6
ATTN_SCALE = HD ** -0.5
IDX_SCALE = (HD ** -0.5) * (8 ** -0.5)
MLA_QK = 192
MLA_SCALE = MLA_QK ** -0.5
LAM_INIT = 0.8 - 0.6 * math.exp(0.0)
MASKED = -1e30
UNREACHABLE = -3e38
TAKEN = -3.4e38
SPAN = 1920

QA, KA, VA, QB, KB, VB, QI, KI, WI, GA, GB = 0, 512, 1024, 1536, 2048, 2112, 2176, 2688, 2752, 2760, 3784
CQ, CKV, KR, DQ, DK, DV = 0, 256, 384, 448, 960, 1472

GAINS = {"mix": (0, 8), "ffn": (8, 8), "final": (16, 8), "attn2": (24, 8), "mlp2": (32, 8), "q_a": (40, 2),
         "kv_a": (42, 1), "mq_n": (43, 1), "mq_r": (44, 1), "mk_n": (45, 1), "mk_r": (46, 1), "dq": (47, 1),
         "dk": (48, 1), "dout": (49, 1), "both": (50, 8)}


def shape_constants():
    f = np.float32
    half = HD // 2
    inv = np.power(f(10000.0), (-np.arange(half, dtype=f) / f(half)).astype(f)).astype(f)
    ang = (np.arange(T, dtype=f)[:, None] * inv[None, :]).astype(f)
    cos, sin = np.cos(ang).astype(f).T, np.sin(ang).astype(f).T
    cos_t = np.concatenate([cos, cos, cos, cos], 0)
    sin_t = np.concatenate([-sin, sin, -sin, sin], 0)
    dist = np.arange(P)[:, None] + 896 - np.arange(T)[None, :]
    count = ((dist <= 128).astype(int) + ((dist % 4 == 0) & (dist <= 512)) + (dist % 16 == 0)) * (dist >= 0)
    abias = np.where(count > 0, np.log(np.maximum(count, 1)) / ATTN_SCALE, MASKED).astype(f)
    causal = np.where(np.arange(P)[None, :] > np.arange(P)[:, None], UNREACHABLE, 0.0).astype(f)
    rel = np.arange(2 * T) - (T - 1)
    n = np.abs(rel)
    large = 8 + (np.log(np.maximum(n, 1).astype(f) / f(8)) / f(math.log(128 / 8)) * f(8)).astype(np.int32)
    bucket = np.where(rel > 0, 16, 0) + np.where(n < 8, n, np.minimum(large, 15))
    onehot = (bucket[None, :] == np.arange(32)[:, None]).astype(f)
    blocks = np.kron(np.eye(2), np.ones((64, 64))).astype(f)
    return {"cos_t": cos_t, "sin_t": sin_t, "abias": abias, "causal": causal, "onehot": onehot,
            "ident": np.eye(P, dtype=f), "blocks": blocks}


class Signal:

    def __init__(self, sem, known):
        self.sem, self.known, self.count = sem, known, 0

    def mark(self, *key, by=1):
        self.count += by
        self.known[key] = self.count
        return self.sem, by

    def at(self, *key):
        return self.sem, self.known.get(key, 1) if self.known is not None else 1

    def loop(self, *key, total):
        self.known[key] = self.count
        self.count += total
        return self.count - total

    def base(self, *key):
        return self.known.get(key, 0)


def emit(nc, known, a):
    ctx = ExitStack()
    with ctx:
        _emit(nc, ctx, known, a)


def _emit(nc, ctx, known, a):
    base0 = (nc.sbuf_base + 63) // 64 * 64

    def at(name, offset, shape, dt=F32):
        return nc.alloc_sbuf_tensor_at(name, shape, dt, offset=base0 + offset)

    K = 1024
    G1, G2, WB, M0, X0, R0 = 0, 64 * K, 128 * K, 152 * K, 152 * K + 7424, 184 * K + 7424
    g1h, g1l = at("g1_hi", G1, [P, DC, T], F32R), at("g1_lo", G1 + 32 * K, [P, DC, T], F32R)
    g2h, g2l = at("g2_hi", G2, [P, DC, T], F32R), at("g2_lo", G2 + 32 * K, [P, DC, T], F32R)
    w_raw = [at(f"w_raw{s}", WB + 4 * K * s, [P, CH]) for s in range(2)]
    w_hi = [at(f"w_hi{s}", WB + 8 * K + 4 * K * s, [P, CH], F32R) for s in range(2)]
    w_lo = [at(f"w_lo{s}", WB + 16 * K + 4 * K * s, [P, CH], F32R) for s in range(2)]
    r_rep = at("r_rep", M0, [P, T])
    ident = at("ident_sb", M0 + 4096, [P, P])
    ones = at("ones_sb", M0 + 4608, [P, P])
    blocks = at("blocks_sb", M0 + 5120, [P, P])
    causal = at("causal_sb", M0 + 5632, [P, P])
    gains = at("gains", M0 + 6144, [P, 58])
    eps_c = at("eps_c", M0 + 6400, [P, 1])
    lam_v = at("lam_v", M0 + 6464, [HD, 8])
    lam_e = at("lam_e", M0 + 6528, [P, 4])
    mn = at("mn", M0 + 6592, [P, 8])
    sm = at("sm", M0 + 6656, [P, 8])
    rc = at("rc", M0 + 6720, [P, 8])
    m8 = at("m8", M0 + 6784, [P, 8])
    wiT = at("wiT", M0 + 6848, [P, QT, 8])
    tab = at("tab", M0 + 7104, [HD, 4])
    xres = at("x_res", X0, [P, DC, T])
    ya = at("y_a", X0, [P, 4, T])
    yb = at("y_b", X0 + 16 * K, [P, 4, T])
    cosr, sinr = at("cos_r", R0, [P, T]), at("sin_r", R0 + 4 * K, [P, T])
    rot1, rot2 = at("rot1", R0 + 8 * K, [P, T]), at("rot2", R0 + 12 * K, [P, T])
    qab = [at(f"qa{s}", G2 + 4 * K * s, [P, T]) for s in range(2)]
    kab = [at(f"ka{s}", G2 + 8 * K + 4 * K * s, [P, T]) for s in range(2)]
    vab = [at(f"va{s}", G2 + 16 * K + 4 * K * s, [P, QT, P]) for s in range(2)]
    kib = at("ki_b", G2 + 8 * K, [P, T])
    qbb = [at(f"qb{c}", G2 + 4 * K * c, [P, T]) for c in range(4)]
    kbb = at("kb_b", G2 + 16 * K, [P, T])
    vbb = at("vb_b", G2 + 20 * K, [P, QT, HD])
    prob = [at(f"prob{s}", G2 + 24 * K + 8 * K * s, [P, 2, T]) for s in range(2)]
    rel = [at(f"rel{s}", G2 + 24 * K + 4 * K * s, [P, T]) for s in range(2)]
    wif = at("wi_f", G2 + 32 * K, [P, T])
    pt = [at(f"pt{s}", G2 + 40 * K + 2 * K * s, [P, HALF]) for s in range(3)]
    acc_at = [sum(P * (j + 1) for j in range(i)) for i in range(QT + 1)]
    acc = at("idx_acc", G2 + 46 * K, [P, acc_at[QT]])
    xt = [at(f"xt{s}", G2 + 16 * K + 4 * K * s, [P, QT, P]) for s in range(DC)]
    xs = [at(f"xs{s}", G2 + 4 * K * s, [P, T]) for s in range(3)]
    gst_a = at("gst_a", X0 + 16 * K, [P, T])
    zb = at("rope_in", X0 + 20 * K, [P, T])
    gst_b = [at(f"gst_b{s}", R0 + 4 * K * s, [P, T]) for s in range(2)]
    abias = at("abias_sb", X0 + 24 * K, [P, T])
    vf = at("v_f", X0 + 28 * K, [P, T])
    oh = at("onehot_sb", G1, [HD, 2 * T])
    ohr = at("onehot_r", G1 + 8 * K, [HD, 2 * T], F32R)
    brow = [at(f"brow{s}", G1 + 16 * K + 8 * K * s, [P, 2 * T]) for s in range(2)]
    tabf, tabh = at("tab_full", G1 + 32 * K, [HD, 4 * P]), at("tab_hi", G1 + 34 * K, [HD, 4 * P], F32R)
    tabr = at("tab_parts", G1 + 36 * K, [HD, 4 * P], F32R)
    sgab = [at("sg_a", R0 + 8 * K, [P, T]), at("sg_b", R0 + 12 * K, [P, T])]
    ta, tb = at("t_a", R0, [P, T]), at("t_b", R0 + 4 * K, [P, T])
    NB = {"x": X0, "r": R0, "y": X0 + 16 * K}
    nb = {k: {"sq": [at(f"sq_{k}{s}", o + 4 * K * s, [P, T]) for s in range(2)],
              "ss": at(f"ss_{k}", o + 8 * K, [P, T]), "rt": at(f"rt_{k}", o + 12 * K, [P, T])} for k, o in NB.items()}
    nb["f"] = {"sq": [at(f"sq_f{s}", G1 + 24 * K + 4 * K * s, [P, T]) for s in range(2)],
               "ss": at("ss_f", G1 + 56 * K, [P, T]), "rt": at("rt_f", G1 + 60 * K, [P, T])}
    r_fin, dvraw = nb["f"]["rt"], at("dv_raw", G1 + 52 * K, [P, T])
    tg, tsil, tact = at("t_g", R0, [P, T]), at("t_silu", R0 + 4 * K, [P, T]), at("t_act", R0 + 8 * K, [P, T])
    dprob = [[at(f"dprob{s}{m}", G1 + 16 * K * s + 8 * K * m, [P, 2, T]) for m in range(2)] for s in range(2)]
    dqb = [at(f"dq{s}", G1 + 32 * K + 4 * K * s, [P, T]) for s in range(2)]
    dkb = [at(f"dk{s}", G1 + 40 * K + 4 * K * s, [P, T]) for s in range(2)]
    dvb = [at(f"dv{s}", G1 + 48 * K + 4 * K * s, [P, QT, P]) for s in range(2)]
    dpt = [at(f"dpt{s}", G1 + 56 * K + 2 * K * s, [P, HALF]) for s in range(3)]
    dbias = [at(f"dbias{s}", R0 + 7680 * s, [P, SPAN]) for s in range(2)]
    yd, ym = at("y_d", X0, [P, 4, T]), at("y_m", X0 + 16 * K, [P, 4, T])
    dvf = at("dv_f", X0 + 28 * K, [P, T])
    mprob = [at(f"mprob{s}", R0 + 8 * K * s, [P, 2, T]) for s in range(2)]
    rkv = at("r_kv", G1, [P, T])
    sqr = [at(f"sqr{s}", G1 + 4 * K + 4 * K * s, [P, T]) for s in range(3)]
    cqf = [at(f"cqf{s}", G1 + 16 * K + 4 * K * s, [P, T]) for s in range(3)]
    krb = at("kr_b", G1 + 28 * K, [P, T])
    clh = at("cl_hi", G1 + 32 * K, [P, 3, T], F32R)
    cll = at("cl_lo", G1 + 44 * K, [P, 3, T], F32R)
    mqn = [at(f"mqn{h}", G2 + 4 * K * h, [P, T]) for h in range(4)]
    mkn = [at(f"mkn{h}", G2 + 16 * K + 4 * K * h, [P, T]) for h in range(4)]
    mqr = [at(f"mqr{p}", G2 + 32 * K + 4 * K * p, [P, T]) for p in range(2)]
    mkr = [at(f"mkr{p}", G2 + 40 * K + 4 * K * p, [P, T]) for p in range(2)]
    mvb = [at(f"mv{h}", G2 + 48 * K + 4 * K * h, [P, QT, P]) for h in range(4)]
    sqn = [at(f"sqn{s}", G1 + 16 * K + 4 * K * s, [P, T]) for s in range(2)]
    mrt = at("mrt", G1 + 24 * K, [P, T])
    mvf = at("mv_f", X0 + 28 * K, [P, T])
    sskv = at("ss_kv", G1 + 60 * K, [P, T])
    krz = at("kr_z", G1 + 56 * K, [P, T])
    yst = [at(f"yst{s}", R0 + 4 * K * s, [P, QT, P]) for s in range(2)]

    big = [ctx.enter_context(nc.psum_tensor(f"big{s}", [P, T], F32)) for s in range(2)]
    tbank = [ctx.enter_context(nc.psum_tensor(f"tbank{s}", [P, HALF], F32)) for s in range(2)]
    obank = [ctx.enter_context(nc.psum_tensor(f"obank{s}", [P, HALF], F32)) for s in range(2)]

    def dram(name, shape):
        return nc.dram_tensor(name, shape, F32, kind="Internal").ap()

    x_spill = dram("x_spill", [DC, P, T])
    g_spill = dram("g_spill", [2 * DC, P, T])
    b_spill = dram("b_spill", [4, P * 2 * T])

    def sig(name):
        return Signal(ctx.enter_context(nc.semaphore(name)), known.setdefault(name, {}))

    w_in_dma = [sig(f"w_loaded{s}") for s in range(2)]
    s_whi, s_wlo = sig("w_hi_done"), sig("w_lo_done")
    s_big = sig("big_done")
    s_rel = sig("big_released")
    s_arel = sig("big_read_act")
    s_tb, s_te = sig("tbank_done"), sig("tbank_read")
    s_o, s_oe = sig("obank_done"), sig("obank_read")
    s_cst = [sig(f"const{n}") for n in range(4)]
    s_xl = [sig(f"x_loaded{s}") for s in range(DC)]
    s_xsp = [sig(f"x_spilled{s}") for s in range(3)]
    s_sp = [sig(f"spilled{s}") for s in range(2)]
    s_bsp = [sig(f"bias_spilled{s}") for s in range(2)]
    s_bl = [sig(f"bias_loaded{s}") for s in range(2)]
    s_gsp = [sig(f"gate_spilled{s}") for s in range(2)]
    s_gl = [sig(f"gate_loaded{s}") for s in range(2)]
    s_dup = sig("key_duplicated")
    s_tabl = sig("tables_loaded")
    s_out = [sig(f"out_stored{s}") for s in range(2)]
    s_nh, s_sq = sig("norm_hi"), sig("norm_square")
    s_nl = sig("norm_lo")
    s_ss = sig("squares_summed")
    s_r = sig("r_ready")
    s_dv = sig("dve_step")
    s_rot = sig("rope_added")
    s_swap, s_cos, s_sin = sig("halves_swapped"), sig("cosine_applied"), sig("sine_applied")
    s_tab = sig("tables_scaled")
    s_relu, s_acc = sig("relu_done"), sig("acc_done")
    s_tk = sig("topk_step")
    s_sc, s_ex, s_nrm = sig("scores_shifted"), sig("exp_done"), sig("probs_ready")
    s_gt, s_sg = sig("gate_scaled"), sig("gate_done")
    s_mg, s_mgh, s_mgl = sig("merged"), sig("merged_hi"), sig("merged_lo")
    s_yh, s_yl = sig("y_hi"), sig("y_lo")
    s_mm, s_msq = sig("max_prepared"), sig("head_squares")
    s_hn = sig("head_normed")
    s_ptu = sig("pt_used")
    s_xres, s_fin = sig("x_reloaded"), sig("lambda_ready")

    w_in, w_in2 = a["w_in"][0], a["w_in_2"][0]

    def cols(w, c0, n=P, k0=0, kn=None):
        kn = w.shape[0] if kn is None else kn
        return w[k0:k0 + kn, c0:c0 + n].rearrange("(k p) m -> p k m", p=P)

    def raw(s, k, m, o=0):
        return w_raw[s][:, o:o + k * m].rearrange("p (k m) -> p k m", k=k)

    pieces = {}

    def std(name, w, c0, k0=0, kn=None):
        kn_ = w.shape[0] if kn is None else kn
        pieces[name] = lambda s: [(raw(s, kn_ // P, P), cols(w, c0, P, k0, kn_))]

    def mixed(name, w, parts):
        pieces[name] = lambda s: [(raw(s, DC, P)[:, :, m0:m0 + n], cols(w, c0, n)) for m0, c0, n in parts]

    std("qi0", w_in, QI)
    std("qi1", w_in, QI + P)
    mixed("kiwi", w_in, [(0, KI, HD), (HD, WI, 8)])
    std("qi2", w_in, QI + 2 * P)
    std("qi3", w_in, QI + 3 * P)
    for c in range(4):
        std(f"va{c}", w_in, VA + P * c)
        std(f"qa{c}", w_in, QA + P * c)
        std(f"ka{c}", w_in, KA + P * c)
    for j in range(DC):
        std(f"ga{j}", w_in, GA + P * j)
    for j in range(DC):
        std(f"gb{j}", w_in, GB + P * j)
    mixed("kbvb", w_in, [(0, KB, HD), (HD, VB, HD)])
    for c in range(4):
        std(f"qb{c}", w_in, QB + P * c)
    for j in range(DC):
        pieces[f"up{j}"] = lambda s, j=j: [(raw(s, 4, P), cols(a["w_up_a"][0], P * j)),
                                           (raw(s, 4, P, 4 * P), cols(a["w_up_b"][0], P * j))]
    for j in range(DC):
        std(f"out{j}", a["w_out"][0], P * j)
    groups1 = [(0, 8), (8, 8), (16, 6)]
    groups2 = [(8 * n, 8) for n in range(4)]
    for n, (f0, fn) in enumerate(groups1):
        for f in range(fn):
            std(f"gate{f0 + f}", a["w_gate"][0], P * (f0 + f))
            std(f"upf{f0 + f}", a["w_up"][0], P * (f0 + f))
        for j in range(DC):
            std(f"down{n}_{j}", a["w_down"][0], P * j, P * f0, P * fn)
    for h in range(4):
        std(f"dv{h}", w_in2, DV + P * h)
        std(f"dq{h}", w_in2, DQ + P * h)
        std(f"dk{h}", w_in2, DK + P * h)
    std("cq0", w_in2, CQ)
    std("cq1", w_in2, CQ + P)
    std("ckv", w_in2, CKV)
    mixed("kr", w_in2, [(0, KR, HD), (HD, KR, HD)])
    uq = a["w_uq_2"][0]
    ukv = a["w_ukv_2"][0]
    pieces["uqr"] = lambda s: [(raw(s, 2, 4 * HD)[:, :, HD * h:HD * h + HD], cols(uq, MLA_QK * h + P, HD)) for h in range(4)]
    for h in range(4):
        pieces[f"mh{h}"] = lambda s, h=h: [(raw(s, 2, P), cols(uq, MLA_QK * h)),
                                           (raw(s, 2, P, 2 * P), ukv[:, 2 * P * h:2 * P * h + 2 * P].rearrange("p (k m) -> p k m", k=2))]
    for j in range(DC):
        std(f"out2_{j}", a["w_out_2"][0], P * j)
    for n, (f0, fn) in enumerate(groups2):
        for f in range(fn):
            std(f"up2_{f0 + f}", a["w_up_2"][0], P * (f0 + f))
        for j in range(DC):
            std(f"down2_{n}_{j}", a["w_down_2"][0], P * j, P * f0, P * fn)

    S = []
    add = lambda *x: S.append(x)
    for h in range(4):
        add("biasrow", h)
    for j in range(DC):
        add("xin", j)
    add("rope", "qi0")
    add("ss", "mix")
    add("tables", "b1")
    add("rope", "qi1")
    add("kiwi")
    add("lam")
    add("rope", "qi2")
    add("wi_t")
    add("idx", 0)
    add("rope", "qi3")
    add("idx", 1)
    add("lin", "va0")
    add("idx", 2)
    add("rope", "qa0")
    add("rope", "ka0")
    add("idx", 3)
    add("fill")
    rounds = [(i, r) for i in range(2, QT) for r in range(TOPK // 8)]
    cost = lambda i: 2 * (P * (i + 1) / 960.0 + 0.07)
    left = list(rounds)

    def topk(us):
        n0 = len(rounds) - len(left)
        t = 0.0
        while left and t + cost(left[0][0]) / 2 < us:
            t += cost(left.pop(0)[0])
        n1 = len(rounds) - len(left)
        if n1 > n0:
            add("topk", n0, n1)

    def topk_until(tile):
        n0 = len(rounds) - len(left)
        while left and left[0][0] < tile:
            left.pop(0)
        n1 = len(rounds) - len(left)
        if n1 > n0:
            add("topk", n0, n1)

    a_steps = {c: [("a", c, i, 0) for i in range(QT)] for c in range(4)}
    b_steps = [("b", c, i, 0) for i in range(QT) for c in range(4)]

    def pipeline(steps, filler={}, rest=0.0, before=None, carry=None):
        prev = carry
        for n, s in enumerate(steps):
            if before:
                before(s)
            add("sc", s)
            topk(rest * (s[2] + 1) / 2 + (FILL_TOPK if n in filler and filler[n][0][0] != "v_t" else 0.0) if rest else 0.0)
            add("nm", s)
            if prev:
                add("pv", prev)
            prev = s
            for f in filler.get(n, []):
                add(*f)
        return prev

    A_TOPK, B_TOPK, FILL_TOPK = 0.4, 2.0, 8.5
    add("v_t", "va0")
    carry = None
    gate = iter(range(16))
    for c in range(4):
        filler = {0: [("gate", next(gate))], 1: [("gate", next(gate))]}
        if c < 3:
            filler[2] = [("rope", f"qa{c + 1}")]
            filler[3] = [("rope", f"ka{c + 1}")]
            filler[5] = [("lin", f"va{c + 1}")]
            filler[6] = [("v_t", f"va{c + 1}")]
        carry = pipeline(a_steps[c], filler, A_TOPK, carry=carry)
    add("gate", next(gate))
    topk(FILL_TOPK)
    add("pv", carry)
    add("kbvb")
    topk(4.0)
    for c in range(4):
        add("rope", f"qb{c}")
        topk(8.0 if c < 3 else 2.0)
    add("vb_t")
    masked = set()

    def mask_for(s):
        i = s[2]
        if i not in masked:
            masked.add(i)
            if i >= 2:
                topk_until(i + 1)
                add("mask", i)

    filler = {n: [("gate", j)] for n, j in zip((1, 3, 5, 7, 9, 11, 13), gate)}
    carry = pipeline(b_steps, filler, B_TOPK, before=mask_for)
    add("pv", carry)
    add("ysplit")
    for j in range(DC):
        add("up", j)
    for j in range(DC):
        add("out", j)
    add("ss", "ffn")
    add("mlp1")
    d_steps = {h: [("d", h, g, 0) for g in range(4)] for h in range(4)}
    m_steps = {h: [("m", h, g, 0) for g in range(4)] for h in range(4)}
    add("lin", "dv0")
    add("ss", "final")
    add("ss", "attn2")
    add("lin", "dq0")
    for j in range(DC):
        add("x1", j)
    add("lin", "dk0")
    add("dnorm", "dq", 0)
    add("dnorm", "dk", 0)
    add("dv0")
    add("v_t", "dv0")
    carry = None
    for h in range(4):
        filler = {}
        if h == 3:
            filler[0] = [("donorm", h - 1)]
        if h < 3:
            filler[0] = [("lin", f"dv{h + 1}"), ("lin", f"dq{h + 1}")]
            filler[1] = [("v_t", f"dv{h + 1}")] + ([("donorm", h - 1)] if h else []) + [("lin", f"dk{h + 1}"), ("dnorm", "dq", h + 1)]
            filler[2] = [("dnorm", "dk", h + 1)]
        carry = pipeline(d_steps[h], filler, carry=carry)
    add("pv", carry)
    add("donorm", 3)
    add("lin", "cq0")
    add("tables", "b2")
    add("lin", "cq1")
    add("lin", "ckv")
    add("krope")
    add("ss", "q_a")
    add("ss", "kv_a")
    add("uqr")
    mnorms = [(q, h) for h in range(4) for q in "qk"]
    add("mh", 0)
    add("v_t", "mv0")
    add("mn1", "q", 0)
    add("mn1", "k", 0)
    add("mn2", "q", 0)
    add("mn2", "k", 0)
    add("mh", 1)
    add("v_t", "mv1")
    carry = None
    for h in range(4):
        filler = {}
        if h < 3:
            filler[0] = [("mn1", "q", h + 1), ("mn2", "q", h + 1)]
            filler[1] = [("mn1", "k", h + 1), ("mn2", "k", h + 1)]
            if h < 2:
                filler[2] = [("mh", h + 2), ("v_t", f"mv{h + 2}")]
        carry = pipeline(m_steps[h], filler, carry=carry)
    add("pv", carry)
    add("y2split")
    for j in range(DC):
        add("out2", j)
    add("ss", "mlp2")
    add("mlp2")
    for j in range(DC):
        add("yout", j)

    def chunk_of(stage, x):
        if stage in ("rope", "lin"):
            return x[0]
        if stage in ("kiwi", "kbvb", "uqr"):
            return stage
        if stage == "krope":
            return "kr"
        if stage == "gate":
            return f"ga{x[0]}" if x[0] < DC else f"gb{x[0] - DC}"
        if stage in ("up", "mh", "out"):
            return f"{stage}{x[0]}"
        return f"out2_{x[0]}" if stage == "out2" else None

    order = []
    for stage, *x in S:
        if chunk_of(stage, x):
            order.append(chunk_of(stage, x))
        elif stage in ("mlp1", "mlp2"):
            for n, (f0, fn) in enumerate(groups1 if stage == "mlp1" else groups2):
                for f in range(f0, f0 + fn):
                    order += [f"gate{f}", f"upf{f}"] if stage == "mlp1" else [f"up2_{f}"]
                order += [f"down{n}_{j}" if stage == "mlp1" else f"down2_{n}_{j}" for j in range(DC)]
    W = {name: w for w, name in enumerate(order)}
    NW = len(order)

    def step_of(s):
        kind, c, g, _ = s
        half = lambda z, m: z[HD * m:HD * m + HD, :]
        if kind in "ab":
            q, k = (qab[c % 2], kab[(c + 1) % 2]) if kind == "a" else (qbb[c], kbb)
            return dict(tiles=(g, g), causal=True, n_maps=1, maps=lambda lane: [[(half(q, lane), half(k, lane))]],
                        v=(lambda kt, lane: vab[c % 2][:, kt, HD * lane:HD * lane + HD]) if kind == "a" else (lambda kt, lane: vbb[:, kt, :]),
                        heads=True, prob=[prob], pt=pt, scale=ATTN_SCALE,
                        bias=(lambda i: abias[:, 896 - P * i:T]) if kind == "a" else (lambda i: acc[:, acc_at[i]:acc_at[i + 1]]),
                        y=(ya if kind == "a" else yb)[:, c, P * g:P * g + P])
        tiles, cols_ = (2 * g, 2 * g + 1), slice(2 * P * g, 2 * P * g + 2 * P)
        if kind == "d":
            return dict(tiles=tiles, causal=False, n_maps=2, maps=lambda lane: [[(half(dqb[c % 2], m), half(dkb[c % 2], m))] for m in range(2)],
                        v=lambda kt, lane: dvb[c % 2][:, kt, :], heads=False,
                        prob=[[dprob[0][0], dprob[1][0]], [dprob[0][1], dprob[1][1]]],
                        pt=dpt, scale=HD ** -0.5, bias=lambda i: dbias[c % 2][:, 896 - P * i:896 - P * i + T], y=yd[:, c, cols_])
        return dict(tiles=tiles, causal=False, n_maps=1,
                    maps=lambda lane: [[(mqn[c][:, :], mkn[c][:, :]), (half(mqr[c // 2], c % 2), half(mkr[c // 2], c % 2))]],
                    v=lambda kt, lane: mvb[c][:, kt, :], heads=False, prob=[mprob], pt=dpt, scale=MLA_SCALE, bias=None,
                    y=ym[:, c, cols_])

    steps = [x[1] for x in S if x[0] == "sc"]
    nstep = {s: n for n, s in enumerate(steps)}

    def keys(st, i):
        return P * (i + 1) if st["causal"] else T

    def tgroups(st):
        last = st["tiles"][1] if st["causal"] else QT - 1
        return [[k for k in (k0, k0 + 1) if k <= last] for k0 in range(0, last + 1, 2)]

    def rope_dest(name):
        kind = name[:2]
        if kind == "qi":
            c = int(name[2])
            return qab[c % 2], ([("big", ("idx", c - 2, 1, QT - 1))] if c >= 2 else [])
        if kind in ("qa", "ka"):
            c = int(name[2])
            buf = qab[c % 2] if kind == "qa" else kab[(c + 1) % 2]
            if c >= 2:
                return buf, [("big", ("sc",) + a_steps[c - 2][-1] + (1, 0))]
            if kind == "ka":
                return buf, [("big", ("idx", 3, 1, QT - 1))] if c else []
            return buf, [("big", ("idx", 2 + c % 2, 1, QT - 1))]
        if kind == "qb":
            return qbb[int(name[2])], [("o", ("o",) + a_steps[3][-1])]
        if name == "kr":
            return krb, []
        raise KeyError(name)

    lin_dest = {f"va{c}": vf for c in range(4)} | {f"dv{h}": dvf for h in range(4)}
    lin_dest |= {f"dq{h}": dqb[h % 2] for h in range(4)} | {f"dk{h}": dkb[h % 2] for h in range(4)}
    lin_dest |= {"cq0": cqf[0], "cq1": cqf[1], "ckv": cqf[2]}

    gates_in_b = {x[1] for x in S[S.index(("sc", b_steps[0])):] if x[0] == "gate"}

    def gst(j):
        return gst_b[j % 2] if j in gates_in_b else gst_a

    def nb_of(key):
        if key in ("q_a", "kv_a"):
            return nb["y"]
        if key == "attn2":
            return nb["f"]
        return nb["x" if key == "mix" else "r"]

    def ss_of(key):
        return sskv if key == "kv_a" else nb_of(key)["ss"]

    def root_of(key):
        return nb_of(key)["rt"]

    def r_of(key):
        return {"kv_a": rkv, "final": r_fin}.get(key, r_rep)

    def load_bias(sp, h):
        sp.wait_ge(*s_bsp[h % 2].at(h))
        rows = b_spill[h][127:127 + P * (2 * T - 1)].rearrange("(p m) -> p m", p=P)
        sp.dma_start(dbias[h % 2][:, :], rows[:, 0:SPAN]).then_inc(*s_bl[h % 2].mark(h, by=16))

    pair = {}

    block = ctx.enter_context(nc.Block())

    @block.tensor
    def _(pe):
        jobs = []
        tn, on, pn = [0], [0], [0]

        def take(key, by):
            n = len(jobs)
            if n >= 2:
                last, reader = jobs[n - 2]
                pe.wait_ge(*reader.at(*last))
            jobs.append((key, by))
            pair[key] = n % 2
            return big[n % 2]

        def passes(out, m, slot, terms):
            total = len(terms)
            for n, (col, hi, lo, ready) in enumerate(terms):
                if ready is not None:
                    pe.wait_ge(*ready)
                for q, (w, x) in enumerate(((w_hi, hi), (w_hi, lo), (w_lo, hi))):
                    for h in range(2):
                        ins = pe.matmul(out[0:m, HALF * h:HALF * h + HALF], w[slot][:, col:col + m],
                                        x[:, HALF * h:HALF * h + HALF], start=(n == 0 and q == 0),
                                        stop=(n == total - 1 and q == 2))
            return ins

        def weight_job(name, key, m, terms, by=s_rel, end=True):
            w = W[name]
            pe.wait_ge(s_wlo.sem, w + 1)
            out = take(key, by)
            passes(out, m, w % 2, terms).then_inc(*s_big.mark(*key))
            if end:
                s_big.known[("w", w)] = s_big.count

        def chunk_terms(xh, xl, n=DC, k0=0, ready=None, col=0):
            return [(col + P * k, xh[:, k0 + k, :], xl[:, k0 + k, :], ready(k) if ready else None) for k in range(n)]

        def full_product(key, by, terms):
            out = take(key, by)
            for h in range(2):
                for n, (w, x) in enumerate(terms):
                    ins = pe.matmul(out[:, HALF * h:HALF * h + HALF], w, x[:, HALF * h:HALF * h + HALF],
                                    start=n == 0, stop=n == len(terms) - 1)
            ins.then_inc(*s_big.mark(*key))

        def to_tokens(name, src, r0, m, ready, per_bank):
            pe.wait_ge(*ready)
            for b in range(QT // per_bank):
                if tn[0] >= 2:
                    pe.wait_ge(s_te.sem, tn[0] - 1)
                for q in range(per_bank):
                    i = per_bank * b + q
                    ins = pe.transpose(tbank[tn[0] % 2][:, m * q:m * q + m], src[r0:r0 + m, P * i:P * i + P],
                                       ident[r0:r0 + m, r0:r0 + m])
                ins.then_inc(*s_tb.mark("t", name, b))
                tn[0] += 1

        pe.wait_ge(*s_cst[0].at())
        pe.wait_ge(*s_mm.at("ones"))
        seen = set()

        def once(tag, *waits):
            if tag not in seen:
                seen.add(tag)
                for w in waits:
                    pe.wait_ge(*w)

        for stage, *x in S:
            if stage == "biasrow":
                h, = x
                pe.wait_ge(*s_mm.at("tabr"))
                for q in range(2):
                    out = take(("br", h, q), s_arel if q else s_rel)
                    for b in range(2):
                        ins = pe.matmul(out[:, HALF * b:HALF * b + HALF], tabr[:, P * h:P * h + P],
                                        ohr[:, T * q + HALF * b:T * q + HALF * b + HALF], start=True, stop=True)
                    ins.then_inc(*s_big.mark("br", h, q))
            elif stage == "lam":
                pe.wait_ge(*s_mm.at("lamp"))
                out = take(("lam",), s_arel)
                pe.matmul(out[:, 0:2], ones[0:HD, :], lam_v[:, 4:6], start=True, stop=True).then_inc(*s_big.mark("lam"))
            elif stage == "xin":
                j, = x
                pe.wait_ge(*s_xl[j].at("xin", j))
                out = take(("xin", j), s_rel)
                for i in range(QT):
                    ins = pe.transpose(out[:, P * i:P * i + P], xt[j][:, i, :], ident[:, :])
                ins.then_inc(*s_big.mark("xin", j))
            elif stage == "ss":
                key, = x
                n = {"q_a": 2, "kv_a": 1}.get(key, DC)
                pe.wait_ge(*s_ss.at(key, n - 1))
                full_product(("ss", key), s_rel if key == "attn2" else s_arel, [(ones[:, :], ss_of(key)[:, :])])
            elif stage in ("rope", "lin"):
                name, = x
                norm = "mix" if name[:2] in ("qi", "va", "qa", "ka", "qb") else "attn2"
                gh, gl = (g1h, g1l) if norm == "mix" else (g2h, g2l)
                first = name in ("qi0", "dv0")
                weight_job(name, (name,), P, chunk_terms(gh, gl, ready=(lambda k: s_nl.at(norm, k)) if first else None),
                           by=s_arel if stage == "rope" else s_rel)
            elif stage in ("kiwi", "kbvb"):
                weight_job(stage, (stage,), HD + 8 if stage == "kiwi" else P, chunk_terms(g1h, g1l), by=s_arel)
            elif stage == "krope":
                weight_job("kr", ("kr",), P, chunk_terms(g2h, g2l))
            elif stage == "wi_t":
                to_tokens("wi", wif, HD, 8, s_hn.at("kiwi"), 8)
            elif stage == "vb_t":
                to_tokens("vb", vf, HD, HD, s_hn.at("kbvb"), 8)
            elif stage == "v_t":
                name, = x
                src = vf if name[0] == "v" else (dvf if name[0] == "d" else mvf)
                ready = s_rel.at("mh", int(name[2]), "v") if name[0] == "m" else s_rel.at(name)
                if name == "dv0":
                    ready = s_hn.at("dv0")
                to_tokens(name, src, 0, P, ready, 4)
            elif stage == "idx":
                c, = x
                pe.wait_ge(*s_rot.at(f"qi{c}"))
                pe.wait_ge(*s_dup.at("kiwi"))
                for hh in range(2):
                    for i in range(2, QT):
                        key = ("idx", c, hh, i)
                        out = take(key, s_arel)
                        n1 = P * (i + 1)
                        o = HD * hh
                        for n0 in range(0, n1, HALF):
                            ne = min(n0 + HALF, n1)
                            ins = pe.matmul(out[:, n0:ne], qab[c % 2][o:o + HD, P * i:P * i + P], kib[o:o + HD, n0:ne],
                                            start=True, stop=True)
                        ins.then_inc(*s_big.mark(*key))
            elif stage == "gate":
                j, = x
                name = f"ga{j}" if j < DC else f"gb{j - DC}"
                weight_job(name, (name,), P, chunk_terms(g1h, g1l))
            elif stage == "sc":
                s, = x
                st = step_of(s)
                kind, c = s[0], s[1]
                once(("q", kind, c), *{
                    "a": lambda: (s_rot.at(f"qa{c}"), s_rot.at(f"ka{c}")),
                    "b": lambda: (s_rot.at(f"qb{c}"), s_dup.at("kbvb")),
                    "d": lambda: (s_hn.at("dq", c), s_hn.at("dk", c)),
                    "m": lambda: (s_hn.at("mq", c), s_hn.at("mk", c)),
                }[kind]())
                for ti, i in enumerate(st["tiles"]):
                    for m, parts in enumerate(st["maps"](ti)):
                        key = ("sc",) + s + (ti, m)
                        out = take(key, s_rel)
                        n1 = keys(st, i)
                        for n0 in range(0, n1, HALF):
                            ne = min(n0 + HALF, n1)
                            for q, (qa, ka) in enumerate(parts):
                                ins = pe.matmul(out[:, n0:ne], qa[:, P * i:P * i + P], ka[:, n0:ne], start=q == 0,
                                                stop=q == len(parts) - 1)
                        ins.then_inc(*s_big.mark(*key))
            elif stage == "pv":
                s, = x
                st = step_of(s)
                kind, c = s[0], s[1]
                once(("v", kind, c), s_te.at("t", {"a": f"va{c}", "b": "vb", "d": f"dv{c}", "m": f"mv{c}"}[kind],
                                             0 if kind == "b" else 1))
                groups = tgroups(st)
                n = nstep[s]
                last_kt = groups[-1][-1]

                def transposed(t):
                    if t == 0:
                        for ti in range(2):
                            pe.wait_ge(*s_nrm.at(s, ti))
                    if tn[0] >= 2:
                        pe.wait_ge(s_te.sem, tn[0] - 1)
                    for n_, kt in enumerate(groups[t]):
                        for ti in range(2):
                            o = P * (2 * n_ + ti)
                            ins = pe.transpose(tbank[tn[0] % 2][:, o:o + P], st["prob"][0][n % 2][:, ti, P * kt:P * kt + P],
                                               ident[:, :])
                    ins.then_inc(*s_tb.mark(s, t))
                    tn[0] += 1

                def product(t):
                    if t == 0 and on[0] >= 2:
                        pe.wait_ge(s_oe.sem, on[0] - 1)
                    pe.wait_ge(*s_te.at(s, t))
                    out, p = obank[on[0] % 2], st["pt"][pn[0] % 3]
                    for n_, kt in enumerate(groups[t]):
                        c = 2 * P * n_
                        if st["heads"]:
                            for ti in range(2):
                                ins = pe.matmul(obank[(on[0] + ti) % 2][HD * ti:HD * ti + HD, 0:P], st["v"](kt, ti), p[:, c + P * ti:c + P * ti + P],
                                                start=kt == 0, stop=kt == last_kt)
                        else:
                            ins = pe.matmul(out[:, 0:2 * P], st["v"](kt, 0), p[:, c:c + 2 * P], start=kt == 0, stop=kt == last_kt)
                    ins.then_inc(*s_ptu.mark(s, t))
                    pn[0] += 1

                for t in range(len(groups)):
                    transposed(t)
                    if t:
                        product(t - 1)
                product(len(groups) - 1)
                s_ptu.known[("end", s)] = s_ptu.count
                on[0] += 1
            elif stage == "up":
                j, = x
                for half, part in enumerate("ab"):
                    weight_job(f"up{j}", ("up", j, part), P,
                               chunk_terms(g2h, g2l, 4, 4 * half, (lambda k: s_yl.at(4 * half + k)) if j == 0 else None,
                                           HALF * half), end=part == "b")
            elif stage == "out":
                j, = x
                weight_job(f"out{j}", ("out", j), P,
                           chunk_terms(g1h, g1l, ready=(lambda k: s_mgl.at("m", k)) if j == 0 else None))
            elif stage == "out2":
                j, = x
                weight_job(f"out2_{j}", ("out2", j), P,
                           chunk_terms(g1h, g1l, ready=(lambda k: s_yl.at("y2", k)) if j == 0 else None))
            elif stage in ("mlp1", "mlp2"):
                one = stage == "mlp1"
                groups = groups1 if one else groups2
                pe.wait_ge(*s_nl.at("ffn" if one else "mlp2", DC - 1))
                assert len(jobs) % 2 == 1 or True
                for key, by in jobs[-2:]:
                    pe.wait_ge(*by.at(*key))
                for gi, (f0, fn) in enumerate(groups):
                    w0 = W[f"gate{f0}" if one else f"up2_{f0}"]
                    n_up = 2 * fn if one else fn
                    last = gi == len(groups) - 1
                    p0 = len(jobs) % 2
                    b0 = s_big.loop(stage, "up", gi, total=n_up)
                    r0 = s_rel.base(stage, "up", gi)
                    with pe.Fori(0, n_up // 2, 1) as i:
                        for u in range(2):
                            pe.wait_ge(s_wlo.sem, i * 2 + (w0 + u + 1))
                            pe.wait_ge(s_rel.sem, i * 2 + (r0 + u - 1))
                            passes(big[(p0 + u) % 2], P, (w0 + u) % 2, chunk_terms(g2h, g2l)).then_inc(s_big.sem, 1)
                    for n in range(n_up):
                        s_big.known[("w", w0 + n)] = b0 + n + 1
                    jobs.extend([None] * n_up)
                    w1 = w0 + n_up
                    n_down = DC
                    b1 = s_big.loop(stage, "down", gi, total=n_down)
                    r1 = s_rel.base(stage, "down", gi)
                    a1 = s_mgl.base(stage, gi)
                    with pe.Fori(0, n_down // 2, 1) as i:
                        for u in range(2):
                            pe.wait_ge(s_wlo.sem, i * 2 + (w1 + u + 1))
                            pe.wait_ge(s_rel.sem, i * 2 + (r1 + u - 1))
                            ready = (lambda k: (s_mgl.sem, a1 + k + 1) if k >= fn - 2 else None) if u == 0 else (lambda k: None)
                            passes(big[(p0 + u) % 2], P, (w1 + u) % 2, chunk_terms(g1h, g1l, fn, ready=ready)).then_inc(s_big.sem, 1)
                    for n in range(n_down):
                        s_big.known[("w", w1 + n)] = b1 + n + 1
                        if last:
                            s_big.known[(stage, n)] = b1 + n + 1
                    jobs.extend([((stage, n), s_rel) if last else None for n in range(n_down)])
                    for n in range(n_down):
                        if last:
                            pair[(stage, n)] = (p0 + n) % 2
                    pair[(stage, "p0", gi)] = p0
            elif stage == "dnorm":
                which, h = x
                pe.wait_ge(*s_msq.at(which, h))
                sq = nb["y"]["sq"][0 if which == "dq" else 1]
                full_product(("dnorm", which, h), s_arel, [(blocks[:, :], sq[:, :])])
            elif stage == "donorm":
                h, = x
                pe.wait_ge(*s_msq.at("do", h))
                full_product(("donorm", h), s_arel, [(ones[:, :], nb["y"]["ss"][:, :])])
            elif stage == "uqr":
                terms = lambda pr: [(2 * P * k + P * pr, clh[:, k, :], cll[:, k, :], s_nl.at("q_a", k)) for k in range(2)]
                for pr in range(2):
                    weight_job("uqr", ("uqr", pr), P, terms(pr), end=pr == 1)
            elif stage == "mh":
                h, = x
                q = [(P * k, clh[:, k, :], cll[:, k, :], None) for k in range(2)]
                kv = lambda n: [(P * (2 + n), clh[:, 2, :], cll[:, 2, :], s_nl.at("kv_a", 0))]
                weight_job(f"mh{h}", ("mh", h, "q"), P, q, end=False)
                weight_job(f"mh{h}", ("mh", h, "k"), P, kv(0), end=False)
                weight_job(f"mh{h}", ("mh", h, "v"), P, kv(1))
            elif stage == "mn1":
                which, h = x
                pe.wait_ge(*s_mm.at("mn", which, h))
                full_product(("mn", which, h), s_arel, [(ones[:, :], sqn[mnorms.index((which, h)) % 2][:, :])])
            elif stage == "yout":
                j, = x
                pe.wait_ge(*s_rel.at("mlp2", j))
                out = take(("yout", j), s_rel)
                for i in range(QT):
                    ins = pe.transpose(out[:, P * i:P * i + P], xres[:, j, P * i:P * i + P], ident[:, :])
                ins.then_inc(*s_big.mark("yout", j))

    @block.scalar
    def _(act):
        tn, pn, rn = [0], [0], [0]
        pt_log = []

        def split(w):
            if w >= NW:
                return
            act.wait_ge(*w_in_dma[w % 2].at(w))
            if w >= 2:
                act.wait_ge(*s_big.at("w", w - 2))
            act.activation(w_hi[w % 2][:, :], w_raw[w % 2][:, :], ACT.Copy).then_inc(*s_whi.mark(w))

        def norm(key, j, xj, ready, gain, dest, free=(), scale=1.0):
            act.wait_ge(*ready)
            for f in free:
                act.wait_ge(*f)
            g = GAINS[gain][0] + j
            n = nb_of(key)
            if dest is not None:
                act.activation(dest, xj, ACT.Copy, scale=gains[:, g:g + 1]).then_inc(*s_nh.mark(key, j))
            if j >= 2:
                act.wait_ge(*s_ss.at(key, j - 2))
            act.activation(n["sq"][j % 2][:, :], xj, ACT.Square, scale=scale).then_inc(*s_sq.mark(key, j))

        def read_bank(key, dest, width, free=()):
            act.wait_ge(*s_tb.at(*key))
            for f in free:
                act.wait_ge(*f)
            src = tbank[tn[0] % 2][:, 0:width]
            if len(dest.shape) == 3:
                src = src.rearrange("p (i m) -> p i m", i=dest.shape[1])
            act.activation(dest, src, ACT.Copy).then_inc(*s_te.mark(*key))
            tn[0] += 1

        def root(key, mean, dest, free=(), final=None):
            final = dest if final is None else final
            if rt_log:
                act.wait_ge(*s_r.at(*rt_log[-1]))
            rt_log.append(key)
            act.wait_ge(*s_big.at(*key))
            for f in free:
                act.wait_ge(*f)
            act.activation(dest, big[pair[key]][:, :], ACT.Ln, scale=mean, bias=eps_c[:, :]).then_inc(*s_arel.mark(*key))
            act.wait_ge(*s_arel.at(*key))
            act.activation(final, dest, ACT.Exp, scale=-0.5).then_inc(*s_r.mark(*key))

        def exp_ln_tables():
            act.preload_act_table_set("natural_log_exp_and_others")

        swap_log, rt_log = [], []

        def take_out(key, rows):
            act.wait_ge(*s_big.at(*key))
            if swap_log:
                act.wait_ge(*s_swap.at(*swap_log[-1]))
                act.wait_ge(*(s_hn if swap_log[-1] in (("kiwi",), ("kbvb",)) else s_cos).at(*swap_log[-1]))
            act.activation(zb[0:rows, :], big[pair[key]][0:rows, :], ACT.Copy).then_inc(*s_arel.mark(*key))
            swap_log.append(key)

        exps = []

        def exp_next():
            if exps:
                key, p, c = exps.pop(0)
                act.wait_ge(*s_rel.at(*key))
                act.activation(p, p, ACT.Exp, scale=-1.0, bias=mn[:, c:c + 1], accum_out=sm[:, c:c + 1]).then_inc(*s_ex.mark(*key))

        act.wait_ge(*s_mm.at("ones"))
        split(0)
        for stage, *x in S:
            while exps and (stage not in ("pv", "nm", "topk", "mask") or (stage == "pv" and exps[0][0][1:5] == x[0])):
                exp_next()
            if chunk_of(stage, x):
                split(W[chunk_of(stage, x)] + 1)
            if stage in ("biasrow", "out", "ss") and (stage, x[0]) in (("biasrow", 0), ("out", 0), ("ss", "final")):
                exp_ln_tables()
            if stage == "rope":
                take_out((x[0],), P)
            elif stage in ("kiwi", "kbvb"):
                take_out((stage,), HD + 8 if stage == "kiwi" else P)
            if stage == "biasrow":
                h, = x
                act.wait_ge(*s_big.at("br", h, 1))
                if h >= 2:
                    act.wait_ge(*s_bsp[h % 2].at(h - 2))
                act.activation(brow[h % 2][:, T:2 * T], big[pair[("br", h, 1)]][:, :], ACT.Copy).then_inc(*s_arel.mark("br", h, 1))
            elif stage == "lam":
                act.wait_ge(*s_big.at("lam"))
                act.activation(lam_e[:, 0:2], big[pair[("lam",)]][:, 0:2], ACT.Exp).then_inc(*s_arel.mark("lam"))
            elif stage == "xin":
                j, = x
                if j == 0:
                    act.wait_ge(*s_cst[1].at())
                norm("mix", j, xs[j % 3][:, :], s_rel.at("xin", j), "mix", g1h[:, j, :],
                     [s_bsp[0].at(2), s_bsp[1].at(3)] if j == 0 else [])
            elif stage == "ss" and x[0] == "attn2":
                t, u = nb["r"]["sq"]
                act.wait_ge(*s_rel.at("ss", "attn2"))
                act.activation(u[:, :], t[:, :], ACT.Ln, scale=1 / D, bias=eps_c[:, :]).then_inc(*s_arel.mark("ln", "attn2"))
                act.wait_ge(*s_arel.at("ln", "attn2"))
                act.activation(u[:, :], u[:, :], ACT.Exp, scale=-0.5).then_inc(*s_r.mark("ss", "attn2"))
            elif stage == "ss":
                key, = x
                root(("ss", key), {"q_a": 1 / 256, "kv_a": 1 / 128}.get(key, 1 / D), root_of(key)[:, :],
                     [s_rel.at("kr")] if key == "q_a" else [], final=r_of(key)[:, :])
            elif stage == "wi_t":
                read_bank(("t", "wi", 0), wiT[:, :, :], 8 * QT)
            elif stage == "vb_t":
                read_bank(("t", "vb", 0), vbb[:, :, :], HD * QT, [s_ptu.at("end", a_steps[3][-1])])
            elif stage == "v_t":
                name, = x
                c = int(name[2])
                dest = {"v": vab[c % 2], "d": dvb[c % 2], "m": mvb[c]}[name[0]]
                old = {"v": a_steps, "d": d_steps}.get(name[0], {}).get(c - 2)
                for b in range(2):
                    read_bank(("t", name, b), dest[:, 4 * b:4 * b + 4, :], HALF,
                              [s_ptu.at("end", old[-1])] if old and b == 0 else [])
            elif stage == "idx":
                c, = x
                for hh in range(2):
                    for i in range(2, QT):
                        key = ("idx", c, hh, i)
                        act.wait_ge(*s_big.at(*key))
                        if rn[0] >= 2:
                            act.wait_ge(s_acc.sem, rn[0] - 1)
                        n = P * (i + 1)
                        act.activation(rel[rn[0] % 2][:, 0:n], big[pair[key]][:, 0:n], ACT.Relu).then_inc(*s_arel.mark(*key))
                        rn[0] += 1
            elif stage == "sc":
                s, = x
                st = step_of(s)
                n = nstep[s]
                for ti, i in enumerate(st["tiles"]):
                    for m in range(st["n_maps"]):
                        key = ("sc",) + s + (ti, m)
                        p = st["prob"][m][n % 2][:, ti, 0:keys(st, i)]
                        exps.append((key, p, 4 * (n % 2) + 2 * ti + m))
            elif stage == "pv":
                s, = x
                st = step_of(s)
                for t, group in enumerate(tgroups(st)):
                    if t >= 2:
                        exp_next()
                    width = 2 * P * len(group)
                    read_bank((s, t), st["pt"][pn[0] % 3][:, 0:width], width,
                              [s_ptu.at(*pt_log[-3])] if len(pt_log) >= 3 else [])
                    pt_log.append((s, t))
                    pn[0] += 1
            elif stage in ("ysplit", "y2split"):
                two = stage == "y2split"
                for j in range(DC):
                    if two:
                        src = ym[:, j, :] if j < 4 else yd[:, j - 4, :]
                        act.wait_ge(*s_oe.at(m_steps[3][-1]))
                        dest = g1h
                    else:
                        src = ya[:, j, :] if j < 4 else yb[:, j - 4, :]
                        act.wait_ge(*s_oe.at(b_steps[-1]))
                        dest = g2h
                    act.activation(dest[:, j, :], src, ACT.Copy).then_inc(*s_yh.mark(*(("y2", j) if two else (j,))))
            elif stage == "up":
                j, = x
                for n in range(2):
                    act.wait_ge(*s_gl[n].at(j))
                    act.activation(sgab[n][:, :], sgab[n][:, :], ACT.Sigmoid).then_inc(*s_sg.mark(j, n))
                act.wait_ge(*s_mg.at(j))
                act.activation(g1h[:, j, :], ta[:, :], ACT.Copy).then_inc(*s_mgh.mark("m", j))
            elif stage in ("out", "out2"):
                j, = x
                norm("ffn" if stage == "out" else "mlp2", j, xres[:, j, :], s_rel.at(stage, j),
                     "ffn" if stage == "out" else "mlp2", g2h[:, j, :])
            elif stage in ("mlp1", "mlp2"):
                one = stage == "mlp1"
                if one:
                    act.preload_act_table(ACT.Silu)
                for gi, (f0, fn) in enumerate(groups1 if one else groups2):
                    last = gi == len(groups1 if one else groups2) - 1
                    n_up = 2 * fn if one else fn
                    w0 = W[f"gate{f0}" if one else f"up2_{f0}"]
                    b0, r0 = s_big.base(stage, "up", gi), s_rel.base(stage, "up", gi)
                    h0 = s_mgh.loop(stage, gi, total=fn)
                    g0 = s_sg.loop(stage, gi, total=fn) if one else 0
                    v0 = s_dv.base(stage, gi)
                    l0 = [w_in_dma[s].base("before", w0) for s in range(2)]
                    s_whi.count += n_up
                    with act.Fori(0, n_up // 2, 1) as i:
                        for u in range(2):
                            sl = (w0 + u + 1) % 2
                            act.wait_ge(w_in_dma[sl].sem, i * 16 + (l0[sl] + 16 * (1 + (u == 1))))
                            act.wait_ge(s_big.sem, i * 2 + (b0 + u))
                            act.activation(w_hi[sl][:, :], w_raw[sl][:, :], ACT.Copy).then_inc(s_whi.sem, 1)
                            if one and u == 0:
                                act.wait_ge(s_rel.sem, i * 2 + (r0 + 1))
                                act.activation(tsil[:, :], tg[:, :], ACT.Silu).then_inc(s_sg.sem, 1)
                            elif one:
                                act.wait_ge(s_rel.sem, i * 2 + (r0 + 2))
                                act.activation(g1h[:, i, :], tact[:, :], ACT.Copy).then_inc(s_mgh.sem, 1)
                            else:
                                act.wait_ge(s_dv.sem, i * 2 + (v0 + u + 1))
                                act.activation(g1h[:, i * 2 + u, :], tact[:, :], ACT.Copy).then_inc(s_mgh.sem, 1)
                    w1 = w0 + n_up
                    b1 = s_big.base(stage, "down", gi)
                    if last:
                        for j in range(DC):
                            split(w1 + j + 1)
                            if one:
                                norm("final", j, xres[:, j, :], s_rel.at("mlp1", j), "final", None)
                                g = GAINS["final"][0] + j
                                norm("attn2", j, xres[:, j, :], s_rel.at("mlp1", j), "both", g2h[:, j, :],
                                     scale=gains[:, g:g + 1])
                    else:
                        l1 = [w_in_dma[s].base("before", w1) for s in range(2)]
                        s_whi.count += DC
                        with act.Fori(0, DC // 2, 1) as i:
                            for u in range(2):
                                sl = (w0 + u + 1) % 2
                                act.wait_ge(w_in_dma[sl].sem, i * 16 + (l1[sl] + 16 * (1 + (u == 1))))
                                act.wait_ge(s_big.sem, i * 2 + (b1 + u))
                                act.activation(w_hi[sl][:, :], w_raw[sl][:, :], ACT.Copy).then_inc(s_whi.sem, 1)
            elif stage == "dnorm":
                which, h = x
                z = (dqb if which == "dq" else dkb)[h % 2]
                sq = nb["y"]["sq"][0 if which == "dq" else 1]
                act.wait_ge(*s_rel.at(f"{which}{h}"))
                if h:
                    act.wait_ge(*s_big.at("dnorm", which, h - 1))
                else:
                    for n in range(2):
                        act.wait_ge(*s_sp[n].at("x1", DC - 2 + n))
                act.activation(sq[:, :], z[:, :], ACT.Square).then_inc(*s_msq.mark(which, h))
                prev = ("dq", h) if which == "dk" else (("do", h - 2) if h >= 2 else ("dk", h - 1))
                root(("dnorm", which, h), 1 / HD, nb["y"]["rt"][:, :], [s_hn.at(*prev)] if prev[1] >= 0 else [])
            elif stage == "donorm":
                h, = x
                act.wait_ge(*s_oe.at(d_steps[h][-1]))
                if h < 2:
                    act.wait_ge(*s_tb.at("t", f"dv{h + 2}", 1))
                if h:
                    act.wait_ge(*s_big.at("donorm", h - 1))
                act.activation(nb["y"]["ss"][:, :], yd[:, h, :], ACT.Square).then_inc(*s_msq.mark("do", h))
                root(("donorm", h), 1 / P, nb["y"]["rt"][:, :], [s_hn.at("dk", h + 1) if h < 3 else s_hn.at("do", 2)])
            elif stage == "mn1":
                which, h = x
                n = mnorms.index((which, h))
                z = (mqn if which == "q" else mkn)[h]
                act.wait_ge(*s_rel.at("mh", h, which))
                if n >= 2:
                    act.wait_ge(*s_big.at("mn", *mnorms[n - 2]))
                if which == "q" and h % 2 == 0:
                    act.wait_ge(*s_rot.at("uqr", h // 2))
                    act.activation(sqr[h // 2][:, :], mqr[h // 2][:, :], ACT.Square)
                if which == "k" and h == 0:
                    act.wait_ge(*s_rot.at("kr"))
                    act.activation(sqr[2][:, :], krb[:, :], ACT.Square)
                act.activation(sqn[n % 2][:, :], z[:, :], ACT.Square).then_inc(*s_msq.mark(which, h))
            elif stage == "mn2":
                which, h = x
                n = mnorms.index((which, h))
                root(("mn", which, h), 1 / MLA_QK, mrt[:, :],
                     [s_hn.at(*(("m" + mnorms[n - 1][0], mnorms[n - 1][1])))] if n else [])
            if stage == "lin" and x[0] in ("cq0", "cq1", "ckv"):
                n = {"cq0": 0, "cq1": 1, "ckv": 2}[x[0]]
                norm("kv_a" if n == 2 else "q_a", n % 2, cqf[n][:, :], s_rel.at(x[0]), "kv_a" if n == 2 else "q_a",
                     clh[:, n, :], [s_ss.at("q_a", 0)] if n == 2 else [])

    @block.vector
    def _(dve):
        def step(ins, *key):
            ins.then_inc(*s_dv.mark(*key))
            dve.wait_ge(s_dv.sem, s_dv.count)

        rot_log = []
        on = [0]

        def rope(key, z, rows, ready):
            if rot_log:
                dve.wait_ge(*s_rot.at(*rot_log[-1]))
            dve.wait_ge(*ready)
            rot_log.append(key)
            dve.tensor_tensor(rot1[0:rows, :], z[0:rows, :], cosr[0:rows, :], ALU.mult).then_inc(*s_cos.mark(*key))

        def norm_lo(key, j, xj, gain, hi, lo):
            g = GAINS[gain][0] + j
            dve.wait_ge(*s_nh.at(key, j))
            dve.scalar_tensor_tensor(out=lo, in0=xj, scalar=gains[:, g:g + 1], in1=hi.bitcast(F32), op0=ALU.mult,
                                     op1=ALU.subtract).then_inc(*s_nl.mark(key, j))

        def scaled(key, dest, ps, r, *free):
            dve.wait_ge(*s_big.at(*key))
            for f in free:
                dve.wait_ge(*f)
            dve.tensor_tensor(dest, ps, r, ALU.mult).then_inc(*s_rel.mark(*key))

        dve.memset(ones[:, :], 1.0)
        dve.memset(eps_c[:, :], EPS).then_inc(*s_mm.mark("ones"))
        dve.wait_ge(*s_cst[0].at())
        dve.wait_ge(*s_mm.at("ones"))
        acc_seen = set()
        for stage, *x in S:
            if stage == "biasrow":
                h, = x
                if h == 0:
                    dve.tensor_copy(ohr[:, :], oh[:, :])
                    for n in range(4):
                        ins = dve.tensor_scalar(tabf[:, P * n:P * n + P], ones[0:HD, :], tab[:, n:n + 1], 1.0 / ATTN_SCALE, ALU.mult, ALU.mult)
                    step(ins, "tf")
                    step(dve.tensor_copy(tabh[:, :], tabf[:, :]), "th")
                    dve.tensor_copy(tabr[0:32, :], tabf[0:32, :])
                    dve.tensor_tensor(tabr[32:HD, :], tabf[32:HD, :], tabh[32:HD, :].bitcast(F32),
                                      ALU.subtract).then_inc(*s_mm.mark("tabr"))
                dve.wait_ge(*s_big.at("br", h, 0))
                if h >= 2:
                    dve.wait_ge(*s_bsp[h % 2].at(h - 2))
                dve.tensor_copy(brow[h % 2][:, 0:T], big[pair[("br", h, 0)]][:, :]).then_inc(*s_rel.mark("br", h, 0))
            elif stage == "lam":
                dve.wait_ge(*s_cst[3].at())
                g = GAINS["dout"][0]
                step(dve.tensor_scalar(gains[:, g:g + 1], gains[:, g:g + 1], 1.0 - LAM_INIT, None, ALU.mult), "gain")
                g, ga, gb = (GAINS[n][0] for n in ("both", "final", "attn2"))
                step(dve.tensor_tensor(gains[:, g:g + DC], gains[:, ga:ga + DC], gains[:, gb:gb + DC], ALU.mult), "gains")
                dve.tensor_tensor(lam_v[:, 4:6], lam_v[:, 0:4:2], lam_v[:, 1:4:2], ALU.mult).then_inc(*s_mm.mark("lamp"))
                dve.wait_ge(*s_arel.at("lam"))
                dve.scalar_tensor_tensor(out=lam_e[:, 2:3], in0=lam_e[:, 1:2], scalar=LAM_INIT, in1=lam_e[:, 0:1],
                                         op0=ALU.subtract, op1=ALU.subtract).then_inc(*s_fin.mark("lam"))
            elif stage == "xin":
                j, = x
                if j == 0:
                    dve.wait_ge(*s_cst[1].at())
                dve.wait_ge(*s_big.at("xin", j))
                if j >= 3:
                    dve.wait_ge(*s_xsp[(j - 3) % 3].at("xin", j - 3))
                    dve.wait_ge(*s_sq.at("mix", j - 3))
                    dve.wait_ge(*s_nl.at("mix", j - 3))
                dve.tensor_copy(xs[j % 3][:, :], big[pair[("xin", j)]][:, :]).then_inc(*s_rel.mark("xin", j))
                for i in ([j - 1] if j else []) + ([j] if j == DC - 1 else []):
                    norm_lo("mix", i, xs[i % 3][:, :], "mix", g1h[:, i, :], g1l[:, i, :])
            elif stage == "ss":
                key, = x
                t, u = nb["r"]["sq"]
                if key == "final":
                    dve.wait_ge(*s_r.at("ss", key))
                    step(dve.tensor_tensor(t[:, :], r_fin[:, :], r_fin[:, :], ALU.mult), "r_fin squared")
                elif key == "attn2":
                    dve.wait_ge(*s_big.at("ss", key))
                    dve.tensor_tensor(t[:, :], big[pair[("ss", key)]][:, :], t[:, :], ALU.mult).then_inc(*s_rel.mark("ss", key))
                    dve.wait_ge(*s_r.at("ss", key))
                    step(dve.tensor_tensor(r_rep[:, :], r_fin[:, :], u[:, :], ALU.mult), "r of both")
                else:
                    dve.wait_ge(*s_r.at("ss", key))
            elif stage == "tables":
                dve.wait_ge(*s_tabl.at(x[0]))
                if x[0] == "b1":
                    for t in (cosr, sinr):
                        ins = dve.tensor_tensor(t[:, :], t[:, :], r_rep[:, :], ALU.mult)
                    step(ins, "tables")
                    rope(("qi0",), zb, P, s_arel.at("qi0"))
            elif stage == "rope":
                name, = x
                if name != "qi0":
                    rope((name,), zb, P, s_arel.at(name))
            elif stage == "kiwi":
                rope(("kiwi",), zb, HD, s_arel.at("kiwi"))
                dve.scalar_tensor_tensor(out=wif[HD:HD + 8, :], in0=zb[HD:HD + 8, :], scalar=IDX_SCALE,
                                         in1=r_rep[HD:HD + 8, :], op0=ALU.mult, op1=ALU.mult).then_inc(*s_hn.mark("kiwi"))
            elif stage == "kbvb":
                rope(("kbvb",), zb, HD, s_arel.at("kbvb"))
                dve.wait_ge(*s_tb.at("t", "va3", 1))
                dve.tensor_tensor(vf[HD:P, :], zb[HD:P, :], r_rep[HD:P, :], ALU.mult).then_inc(*s_hn.mark("kbvb"))
            elif stage == "lin":
                name, = x
                kind, c = name[:2], name[2:]
                free = []
                if kind == "va" and c != "0":
                    free = [s_tb.at("t", f"va{int(c) - 1}", 1)]
                if kind == "dv" and c != "0":
                    free = [s_tb.at("t", f"dv{int(c) - 1}", 1), s_hn.at("dk", int(c) - 1)]
                if kind in ("dq", "dk") and int(c) >= 2:
                    free = [s_big.at("sc", *d_steps[int(c) - 2][-1], 1, 1)]
                if name == "dv0":
                    dve.wait_ge(*s_big.at("dv0"))
                    dve.tensor_copy(dvraw[:, :], big[pair[("dv0",)]][:, :]).then_inc(*s_rel.mark("dv0"))
                else:
                    scaled((name,), lin_dest[name][:, :], big[pair[(name,)]][:, :], r_rep[:, :], *free)
                if name in ("cq0", "cq1", "ckv"):
                    n = {"cq0": 0, "cq1": 1, "ckv": 2}[name]
                    key = "kv_a" if n == 2 else "q_a"
                    dve.wait_ge(*s_rel.at(name))
                    norm_lo(key, n % 2, cqf[n][:, :], key, clh[:, n, :], cll[:, n, :])
            elif stage == "dv0":
                for n in range(2):
                    dve.wait_ge(*s_sp[n].at("x1", DC - 2 + n))
                dve.wait_ge(*s_rel.at("dv0"))
                dve.wait_ge(*s_hn.at("dk", 0))
                dve.tensor_tensor(dvf[:, :], dvraw[:, :], r_rep[:, :], ALU.mult).then_inc(*s_hn.mark("dv0"))
            elif stage == "krope":
                scaled(("kr",), krz[:, :], big[pair[("kr",)]][:, :], r_rep[:, :])
                dve.wait_ge(*s_rel.at("kr"))
                dve.wait_ge(*s_tabl.at("b2"))
                rope(("kr",), krz, P, s_rel.at("kr"))
            elif stage == "uqr":
                for pr in range(2):
                    last = ("kr",) if pr == 0 else ("uqr", 0)
                    dve.wait_ge(*s_swap.at(*last))
                    dve.wait_ge(*s_cos.at(*last))
                    scaled(("uqr", pr), krz[:, :], big[pair[("uqr", pr)]][:, :], r_rep[:, :])
                    dve.wait_ge(*s_rel.at("uqr", pr))
                    rope(("uqr", pr), krz, P, s_rel.at("uqr", pr))
            elif stage == "mh":
                h, = x
                if h:
                    vfree = [s_tb.at("t", f"mv{h - 1}", 1)]
                else:
                    vfree = []
                scaled(("mh", h, "q"), mqn[h][:, :], big[pair[("mh", h, "q")]][:, :], r_rep[:, :])
                scaled(("mh", h, "k"), mkn[h][:, :], big[pair[("mh", h, "k")]][:, :], rkv[:, :])
                scaled(("mh", h, "v"), mvf[:, :], big[pair[("mh", h, "v")]][:, :], rkv[:, :], *vfree)
            elif stage == "idx":
                c, = x
                dve.wait_ge(*s_te.at("t", "wi", 0))
                for hh in range(2):
                    for i in range(2, QT):
                        key = ("idx", c, hh, i)
                        h = 2 * c + hh
                        w = wiT[:, i, h:h + 1]
                        z = acc[:, acc_at[i]:acc_at[i + 1]]
                        r = rel[s_acc.count % 2][:, 0:P * (i + 1)]
                        dve.wait_ge(*s_arel.at(*key))
                        if h == 0:
                            ins = dve.tensor_scalar(z, r, w, None, ALU.mult)
                        else:
                            dve.wait_ge(*s_acc.at("idx", (h - 1) // 2, (h - 1) % 2, i))
                            ins = dve.scalar_tensor_tensor(out=z, in0=r, scalar=w, in1=z, op0=ALU.mult, op1=ALU.add)
                        ins.then_inc(*s_acc.mark(*key))
            elif stage == "fill":
                dve.wait_ge(*s_cst[2].at())
                dve.wait_ge(s_acc.sem, s_acc.count)
                dve.memset(acc[:, 0:acc_at[2]], 0.0).then_inc(*s_tk.mark("zero"))
                for i in range(2, QT):
                    z = acc[:, acc_at[i + 1] - P:acc_at[i + 1]]
                    dve.tensor_tensor(z, z, causal[:, :], ALU.add).then_inc(*s_tk.mark("fill", i))
                dve.wait_ge(s_tk.sem, s_tk.count)
                for i in range(2):
                    dve.tensor_copy(acc[:, acc_at[i + 1] - P:acc_at[i + 1]], causal[:, :]).then_inc(*s_tk.mark("fill", i))
                dve.wait_ge(s_tk.sem, s_tk.count)
            elif stage == "topk":
                for n in range(x[0], x[1]):
                    i, r = rounds[n]
                    z = acc[:, acc_at[i]:acc_at[i + 1]]
                    dve.max(m8[:, :], z).then_inc(*s_tk.mark("max", n))
                    dve.wait_ge(*s_tk.at("max", n))
                    dve.match_replace(z, m8[:, :], z, TAKEN).then_inc(*s_tk.mark("take", n))
                    dve.wait_ge(*s_tk.at("take", n))
            elif stage == "mask":
                for i in x:
                    z = acc[:, acc_at[i]:acc_at[i + 1]]
                    dve.tensor_scalar(z, z, -3.2e38, MASKED, ALU.is_gt, ALU.mult).then_inc(*s_tk.mark("mask", i))
                dve.wait_ge(s_tk.sem, s_tk.count)
            elif stage == "gate":
                j, = x
                name = f"ga{j}" if j < DC else f"gb{j - DC}"
                scaled((name,), gst(j)[:, :], big[pair[(name,)]][:, :], r_rep[:, :],
                       *([s_gsp[(j - 1) % 2].at(j - 1)] if j else []), *([s_rot.at("qb3")] if j in gates_in_b else []))
            elif stage == "sc":
                s, = x
                st = step_of(s)
                n = nstep[s]
                maps = st["n_maps"]
                if n >= 2:
                    dve.wait_ge(*s_ptu.at("end", steps[n - 2]))
                if s[0] == "a" and n == 0:
                    dve.wait_ge(*s_cst[2].at())
                if s[0] == "d":
                    dve.wait_ge(*s_bl[s[1] % 2].at(s[1]))
                for ti, i in enumerate(st["tiles"]):
                    for m in range(maps):
                        key = ("sc",) + s + (ti, m)
                        dve.wait_ge(*s_big.at(*key))
                        nk = keys(st, i)
                        p = st["prob"][m][n % 2][:, ti, 0:nk]
                        c = 4 * (n % 2) + 2 * ti + m
                        ps = big[pair[key]][:, 0:nk]
                        if st["bias"] is None:
                            ins = dve.tensor_scalar(p, ps, -st["scale"], 3e38, ALU.mult, ALU.min, accum_out=mn[:, c:c + 1])
                        else:
                            ins = dve.tensor_tensor_reduce(p, ps, st["bias"](i), -st["scale"], 3e38, ALU.add, ALU.min,
                                                           mn[:, c:c + 1])
                        ins.then_inc(*s_rel.mark(*key))
            elif stage == "nm":
                s, = x
                st = step_of(s)
                n = nstep[s]
                maps = st["n_maps"]
                for ti, i in enumerate(st["tiles"]):
                    nk = keys(st, i)
                    c = 4 * (n % 2) + 2 * ti
                    p0 = st["prob"][0][n % 2][:, ti, 0:nk]
                    dve.wait_ge(*s_ex.at("sc", *s, ti, maps - 1))
                    step(dve.reciprocal(rc[:, c:c + maps], sm[:, c:c + maps]), "rc", s, ti)
                    if maps == 1:
                        dve.tensor_scalar(p0, p0, rc[:, c:c + 1], None, ALU.mult).then_inc(*s_nrm.mark(s, ti))
                    else:
                        p1 = st["prob"][1][n % 2][:, ti, 0:nk]
                        step(dve.tensor_scalar(rc[:, c + 1:c + 2], rc[:, c + 1:c + 2], lam_e[:, 2:3], None, ALU.mult), "rl", s, ti)
                        step(dve.tensor_scalar(p1, p1, rc[:, c + 1:c + 2], None, ALU.mult), "p1", s, ti)
                        dve.scalar_tensor_tensor(out=p0, in0=p0, scalar=rc[:, c:c + 1], in1=p1, op0=ALU.mult,
                                                 op1=ALU.add).then_inc(*s_nrm.mark(s, ti))
            elif stage == "pv":
                s, = x
                st = step_of(s)
                dve.wait_ge(*s_ptu.at("end", s))
                if st["heads"]:
                    for ti in range(2):
                        r = slice(HD * ti, HD * ti + HD)
                        ins = dve.tensor_copy(st["y"][r, :], obank[(on[0] + ti) % 2][r, 0:P])
                    ins.then_inc(*s_oe.mark(s))
                else:
                    dve.tensor_copy(st["y"], obank[on[0] % 2][:, 0:2 * P]).then_inc(*s_oe.mark(s))
                on[0] += 1
            elif stage in ("ysplit", "y2split"):
                two = stage == "y2split"
                if two:
                    dve.wait_ge(*s_oe.at(m_steps[3][-1]))
                for j in range(DC):
                    if two:
                        src, hi, lo = (ym[:, j, :] if j < 4 else yd[:, j - 4, :]), g1h[:, j, :], g1l[:, j, :]
                    else:
                        src, hi, lo = (ya[:, j, :] if j < 4 else yb[:, j - 4, :]), g2h[:, j, :], g2l[:, j, :]
                    key = ("y2", j) if two else (j,)
                    dve.wait_ge(*s_yh.at(*key))
                    dve.tensor_tensor(lo, src, hi.bitcast(F32), ALU.subtract).then_inc(*s_yl.mark(*key))
            elif stage == "up":
                j, = x
                for n, t in enumerate((ta, tb)):
                    free = [s_mgl.at("m", j - 1)] if j and n == 0 else []
                    scaled(("up", j, "ab"[n]), t[:, :], big[pair[("up", j, "ab"[n])]][:, :], sgab[n][:, :],
                           s_sg.at(j, n), *free)
                dve.wait_ge(*s_rel.at("up", j, "b"))
                dve.tensor_tensor(ta[:, :], ta[:, :], tb[:, :], ALU.add).then_inc(*s_mg.mark(j))
                dve.wait_ge(*s_mg.at(j))
            elif stage in ("out", "out2"):
                j, = x
                key = "ffn" if stage == "out" else "mlp2"
                dve.wait_ge(*s_xres.at(stage))
                dve.wait_ge(*s_big.at(stage, j))
                dve.tensor_tensor(xres[:, j, :], big[pair[(stage, j)]][:, :], xres[:, j, :], ALU.add).then_inc(*s_rel.mark(stage, j))
                dve.wait_ge(*s_rel.at(stage, j))
                norm_lo(key, j, xres[:, j, :], key, g2h[:, j, :], g2l[:, j, :])
            elif stage in ("mlp1", "mlp2"):
                one = stage == "mlp1"
                for gi, (f0, fn) in enumerate(groups1 if one else groups2):
                    last = gi == len(groups1 if one else groups2) - 1
                    p0 = pair[(stage, "p0", gi)]
                    n_up = 2 * fn if one else fn
                    b0 = s_big.base(stage, "up", gi)
                    r0 = s_rel.loop(stage, "up", gi, total=n_up)
                    a0, g0, q0 = s_mgl.base(stage, gi), s_sg.base(stage, gi), s_rot.base(stage, gi)
                    if one:
                        with dve.Fori(0, fn, 1) as i:
                            dve.wait_ge(s_big.sem, i * 2 + (b0 + 1))
                            dve.wait_ge(s_sg.sem, i + g0)
                            dve.tensor_tensor(tg[:, :], big[p0][:, :], r_rep[:, :], ALU.mult).then_inc(s_rel.sem, 1)
                            dve.wait_ge(s_big.sem, i * 2 + (b0 + 2))
                            dve.wait_ge(s_rot.sem, i + (q0 + 1))
                            dve.wait_ge(s_mgl.sem, i + a0)
                            dve.tensor_tensor(tact[:, :], big[1 - p0][:, :], tsil[:, :], ALU.mult).then_inc(s_rel.sem, 1)
                    else:
                        v0 = s_dv.loop(stage, gi, total=n_up)
                        with dve.Fori(0, n_up // 2, 1) as i:
                            for u in range(2):
                                dve.wait_ge(s_big.sem, i * 2 + (b0 + u + 1))
                                dve.wait_ge(s_dv.sem, i * 2 + (v0 + u))
                                dve.tensor_tensor(tg[:, :], big[(p0 + u) % 2][:, :], r_rep[:, :], ALU.mult).then_inc(s_rel.sem, 1)
                                dve.wait_ge(s_rel.sem, i * 2 + (r0 + u + 1))
                                dve.wait_ge(s_mgl.sem, i * 2 + (a0 + u))
                                dve.scalar_tensor_tensor(out=tact[:, :], in0=tg[:, :], scalar=0.0, in1=tg[:, :],
                                                         op0=ALU.max, op1=ALU.mult).then_inc(s_dv.sem, 1)
                    b1 = s_big.base(stage, "down", gi)
                    if last:
                        s_rel.known[(stage, "down", gi)] = s_rel.count
                        for j in range(DC):
                            dve.wait_ge(*s_big.at(stage, j))
                            dve.tensor_tensor(xres[:, j, :], big[pair[(stage, j)]][:, :], xres[:, j, :],
                                              ALU.add).then_inc(*s_rel.mark(stage, j))
                            if one:
                                dve.wait_ge(*s_rel.at(stage, j))
                                norm_lo("attn2", j, xres[:, j, :], "both", g2h[:, j, :], g2l[:, j, :])
                    else:
                        r1 = s_rel.loop(stage, "down", gi, total=DC)
                        with dve.Fori(0, DC // 2, 1) as i:
                            for u in range(2):
                                dve.wait_ge(s_big.sem, i * 2 + (b1 + u + 1))
                                dve.tensor_tensor(xres[:, i * 2 + u, :], big[(p0 + u) % 2][:, :], xres[:, i * 2 + u, :],
                                                  ALU.add).then_inc(s_rel.sem, 1)
            elif stage == "x1":
                j, = x
                gcol = GAINS["final"][0] + j
                xj = xres[:, j, :]
                dve.wait_ge(*s_sq.at("attn2", j))
                dve.scalar_tensor_tensor(out=xj, in0=xj, scalar=gains[:, gcol:gcol + 1], in1=r_fin[:, :], op0=ALU.mult,
                                         op1=ALU.mult).then_inc(*s_hn.mark("x1", j))
            elif stage in ("dnorm", "donorm"):
                if stage == "dnorm":
                    which, h = x
                    key, gain, z = ("dnorm", which, h), which, (dqb if which == "dq" else dkb)[h % 2][:, :]
                    out = (which, h)
                else:
                    h, = x
                    key, gain, z, out = ("donorm", h), "dout", yd[:, h, :], ("do", h)
                rt = nb["y"]["rt"]
                dve.wait_ge(*s_r.at(*key))
                gcol = GAINS[gain][0]
                dve.scalar_tensor_tensor(out=z, in0=z, scalar=gains[:, gcol:gcol + 1], in1=rt[:, :], op0=ALU.mult,
                                         op1=ALU.mult).then_inc(*s_hn.mark(*out))
            elif stage == "mn1":
                which, h = x
                r = slice(HD * (h % 2), HD * (h % 2) + HD)
                z, rope_sq = sqn[mnorms.index((which, h)) % 2], sqr[h // 2 if which == "q" else 2]
                dve.wait_ge(*s_msq.at(which, h))
                dve.tensor_tensor(z[r, :], z[r, :], rope_sq[r, :], ALU.add).then_inc(*s_mm.mark("mn", which, h))
            elif stage == "mn2":
                which, h = x
                r = HD * (h % 2)
                dve.wait_ge(*s_r.at("mn", which, h))
                z = (mqn if which == "q" else mkn)[h][:, :]
                g = GAINS[f"m{which}_n"][0]
                dve.scalar_tensor_tensor(out=z, in0=z, scalar=gains[:, g:g + 1], in1=mrt[:, :], op0=ALU.mult, op1=ALU.mult)
                g = GAINS[f"m{which}_r"][0]
                src = (mqr[h // 2] if which == "q" else krb)[r:r + HD, :]
                dest = (mqr if which == "q" else mkr)[h // 2][r:r + HD, :]
                dve.scalar_tensor_tensor(out=dest, in0=src, scalar=gains[r:r + HD, g:g + 1], in1=mrt[r:r + HD, :],
                                         op0=ALU.mult, op1=ALU.mult).then_inc(*s_hn.mark("m" + which, h))
            elif stage == "yout":
                j, = x
                dve.wait_ge(*s_big.at("yout", j))
                if j >= 2:
                    dve.wait_ge(*s_out[j % 2].at(j - 2))
                dve.tensor_copy(yst[j % 2][:, :, :].rearrange("p i m -> p (i m)"), big[pair[("yout", j)]][:, :]).then_inc(*s_rel.mark("yout", j))

    @block.gpsimd
    def _(pool):
        def split(w):
            if w >= NW:
                return
            s = w % 2
            pool.wait_ge(s_whi.sem, w + 1)
            pool.tensor_tensor(w_lo[s][:, :], w_raw[s][:, :], w_hi[s][:, :].bitcast(F32), ALU.subtract).then_inc(*s_wlo.mark(w))

        def add_squares(key, j):
            n = nb_of(key)
            pool.wait_ge(*s_sq.at(key, j))
            sq = n["sq"][j % 2][:, :]
            if j == 0:
                ins = pool.tensor_copy(ss_of(key)[:, :], sq)
            else:
                pool.wait_ge(*s_ss.at(key, j - 1))
                ins = pool.tensor_tensor(ss_of(key)[:, :], ss_of(key)[:, :], sq, ALU.add)
            ins.then_inc(*s_ss.mark(key, j))

        def rope_add(key, dest, rows, free):
            pool.wait_ge(*s_swap.at(*key))
            pool.wait_ge(*s_cos.at(*key))
            pool.tensor_tensor(rot2[0:rows, :], rot2[0:rows, :], sinr[0:rows, :], ALU.mult).then_inc(*s_sin.mark(*key))
            pool.wait_ge(*s_sin.at(*key))
            for f in free:
                pool.wait_ge(*f)
            pool.tensor_tensor(dest[0:rows, :], rot1[0:rows, :], rot2[0:rows, :], ALU.add).then_inc(*s_rot.mark(*key))

        split(0)
        for stage, *x in S:
            if chunk_of(stage, x):
                split(W[chunk_of(stage, x)] + 1)
            if stage == "xin":
                add_squares("mix", x[0])
            elif stage == "rope":
                name, = x
                dest, free = rope_dest(name)
                rope_add((name,), dest, P, [s_big.at(*k) if s == "big" else s_oe.at(*k[1:]) for s, k in free])
            elif stage == "kiwi":
                rope_add(("kiwi",), kib, HD, [])
            elif stage == "kbvb":
                rope_add(("kbvb",), kbb, HD, [s_oe.at(a_steps[3][-1])])
            elif stage == "krope":
                rope_add(("kr",), krb, P, [])
            elif stage == "uqr":
                for pr in range(2):
                    rope_add(("uqr", pr), mqr[pr], P, [])
            elif stage == "up":
                j, = x
                pool.wait_ge(*s_mgh.at("m", j))
                pool.tensor_tensor(g1l[:, j, :], ta[:, :], g1h[:, j, :].bitcast(F32), ALU.subtract).then_inc(*s_mgl.mark("m", j))
            elif stage in ("out", "out2"):
                add_squares("ffn" if stage == "out" else "mlp2", x[0])
            elif stage == "lin" and x[0] in ("cq0", "cq1", "ckv"):
                n = {"cq0": 0, "cq1": 1, "ckv": 2}[x[0]]
                add_squares("kv_a" if n == 2 else "q_a", n % 2)
            elif stage in ("mlp1", "mlp2"):
                one = stage == "mlp1"
                for gi, (f0, fn) in enumerate(groups1 if one else groups2):
                    last = gi == len(groups1 if one else groups2) - 1
                    n_up = 2 * fn if one else fn
                    w0 = W[f"gate{f0}" if one else f"up2_{f0}"]
                    h0, g0 = s_mgh.base(stage, gi), s_sg.base(stage, gi)
                    s_mgl.loop(stage, gi, total=fn)
                    if one:
                        s_rot.loop(stage, gi, total=fn)
                    s_wlo.count += n_up
                    with pool.Fori(0, n_up // 2, 1) as i:
                        for u in range(2):
                            sl = (w0 + u + 1) % 2
                            pool.wait_ge(s_whi.sem, i * 2 + (w0 + u + 2))
                            pool.tensor_tensor(w_lo[sl][:, :], w_raw[sl][:, :], w_hi[sl][:, :].bitcast(F32),
                                               ALU.subtract).then_inc(s_wlo.sem, 1)
                            if one and u == 0:
                                pool.wait_ge(s_sg.sem, i + (g0 + 1))
                                pool.tensor_tensor(tsil[:, :], tsil[:, :], r_rep[:, :], ALU.mult).then_inc(s_rot.sem, 1)
                            elif one:
                                pool.wait_ge(s_mgh.sem, i + (h0 + 1))
                                pool.tensor_tensor(g1l[:, i, :], tact[:, :], g1h[:, i, :].bitcast(F32),
                                                   ALU.subtract).then_inc(s_mgl.sem, 1)
                            else:
                                pool.wait_ge(s_mgh.sem, i * 2 + (h0 + u + 1))
                                pool.tensor_tensor(g1l[:, i * 2 + u, :], tact[:, :], g1h[:, i * 2 + u, :].bitcast(F32),
                                                   ALU.subtract).then_inc(s_mgl.sem, 1)
                    w1 = w0 + n_up
                    if last:
                        for j in range(DC):
                            split(w1 + j + 1)
                            if one:
                                add_squares("final", j)
                                add_squares("attn2", j)
                    else:
                        s_wlo.count += DC
                        with pool.Fori(0, DC // 2, 1) as i:
                            for u in range(2):
                                sl = (w0 + u + 1) % 2
                                pool.wait_ge(s_whi.sem, i * 2 + (w1 + u + 2))
                                pool.tensor_tensor(w_lo[sl][:, :], w_raw[sl][:, :], w_hi[sl][:, :].bitcast(F32),
                                                   ALU.subtract).then_inc(s_wlo.sem, 1)

    @block.sync
    def _(sp):
        def load(w):
            if w >= NW:
                return
            if w >= 2:
                sp.wait_ge(s_wlo.sem, w - 1)
            w_in_dma[w % 2].known[("before", w)] = w_in_dma[w % 2].count
            for dst, src in pieces[order[w]](w % 2):
                sp.dma_start(dst, src).then_inc(*w_in_dma[w % 2].mark(w, by=16))

        def column(name, col, rows, src, n=1, done=s_cst[3]):
            sp.dma_start(gains[rows[0]:rows[1], col:col + n], src, allow_slow_non_contiguous=True).then_inc(*done.mark(by=16))

        swap_log = []

        def swap(key, z, rows, ready):
            sp.wait_ge(*ready)
            if swap_log:
                sp.wait_ge(*s_rot.at(*swap_log[-1]))
            for b in range(0, rows, 32):
                e = b + 32 if b % HD == 0 else b - 32
                sp.dma_start(rot2[b:b + 32, :], z[e:e + 32, :]).then_inc(*s_swap.mark(*key, by=16))
            swap_log.append(key)

        def x_tile(j):
            sp.dma_start(xt[j][:, :, :], a["x"][0].rearrange("(i p) d -> p i d", p=P)[:, :, P * j:P * j + P]).then_inc(
                *s_xl[j].mark("xin", j, by=16))

        sp.dma_start(ident[:, :], a["ident"]).then_inc(*s_cst[0].mark(by=16))
        for r in (0, 32):
            sp.dma_start(oh[r:r + 32, :], a["onehot"]).then_inc(*s_cst[0].mark(by=16))
            sp.dma_start(tab[r:r + 32, :], a["rel_bias_2"]).then_inc(*s_cst[0].mark(by=16))
        column("mix", GAINS["mix"][0], (0, P), a["norm_mix"][0].rearrange("(j p) -> p j", p=P), DC, s_cst[1])
        for j in range(DC):
            x_tile(j)
        load(0)
        load(1)
        for n, v in enumerate(("lambda_q1_2", "lambda_k1_2", "lambda_q2_2", "lambda_k2_2")):
            sp.dma_start(lam_v[:, n:n + 1], a[v].rearrange("a d -> d a"), allow_slow_non_contiguous=True).then_inc(*s_cst[3].mark(by=16))
        for name, v in (("ffn", "norm_ffn"), ("final", "norm_final"), ("attn2", "attn_norm_w_2"),
                        ("mlp2", "mlp_norm_w_2"), ("q_a", "q_a_norm_w_2"), ("kv_a", "kv_a_norm_w_2"), ("dout", "diff_out_norm_w_2")):
            vec = a[v] if len(a[v].shape) == 1 else a[v][0]
            column(name, GAINS[name][0], (0, P), vec.rearrange("(j p) -> p j", p=P), GAINS[name][1])
        for q, v in (("q", "mla_q_norm_w_2"), ("k", "mla_k_norm_w_2")):
            vec = a[v][0].rearrange("(p j) -> p j", j=1)
            column("", GAINS[f"m{q}_n"][0], (0, P), vec[0:P, :])
            for r in (0, HD):
                column("", GAINS[f"m{q}_r"][0], (r, r + HD), vec[P:P + HD, :])
            v = f"diff_{q}_norm_w_2"
            for r in (0, HD):
                column("", GAINS[f"d{q}"][0], (r, r + HD), a[v][0].rearrange("(p j) -> p j", j=1))
        for t, n in ((cosr, "cos_t"), (sinr, "sin_t")):
            sp.dma_start(t[:, :], a[n]).then_inc(*s_tabl.mark("b1", by=16))
        for t, n in ((abias, "abias"), (causal, "causal"), (blocks, "blocks")):
            sp.dma_start(t[:, :], a[n]).then_inc(*s_cst[2].mark(by=16))
        for stage, *x in S:
            if chunk_of(stage, x):
                load(W[chunk_of(stage, x)] + 2)
            if stage == "rope":
                swap((x[0],), zb, P, s_arel.at(x[0]))
            elif stage in ("kiwi", "kbvb"):
                swap((stage,), zb, HD, s_arel.at(stage))
            elif stage == "krope":
                swap(("kr",), krz, P, s_rel.at("kr"))
            elif stage == "uqr":
                for pr in range(2):
                    swap(("uqr", pr), krz, P, s_rel.at("uqr", pr))
            if stage == "biasrow":
                h, = x
                sp.wait_ge(*s_rel.at("br", h, 0))
                sp.wait_ge(*s_arel.at("br", h, 1))
                sp.dma_start(b_spill[h].rearrange("(p m) -> p m", p=P), brow[h % 2][:, :]).then_inc(*s_bsp[h % 2].mark(h, by=16))
            elif stage == "xin":
                j, = x
                sp.wait_ge(*s_rel.at("xin", j))
                sp.dma_start(x_spill[j], xs[j % 3][:, :]).then_inc(*s_xsp[j % 3].mark("xin", j, by=16))
            elif stage in ("kiwi", "kbvb"):
                buf = kib if stage == "kiwi" else kbb
                sp.wait_ge(*s_rot.at(stage))
                sp.dma_start(buf[HD:P, :], buf[0:HD, :]).then_inc(*s_dup.mark(stage, by=16))
            elif stage == "gate":
                j, = x
                sp.wait_ge(*s_rel.at(chunk_of(stage, x)))
                sp.dma_start(g_spill[j], gst(j)[:, :]).then_inc(*s_gsp[j % 2].mark(j, by=16))
            elif stage == "ysplit":
                sp.wait_ge(*s_yl.at(DC - 1))
                for n in range(3):
                    sp.wait_ge(*s_xsp[(DC - 3 + n) % 3].at("xin", DC - 3 + n))
                for n in range(2):
                    sp.wait_ge(*s_gsp[n].at(2 * DC - 2 + n))
                for n in range(2):
                    sp.dma_start(sgab[n][:, :], g_spill[DC * n]).then_inc(*s_gl[n].mark(0, by=16))
                sp.dma_start(xres[:, :, :], x_spill.rearrange("j p t -> p j t")).then_inc(*s_xres.mark("out", by=16))
            elif stage == "up":
                j, = x
                if j + 1 < DC:
                    for n in range(2):
                        sp.wait_ge(*s_rel.at("up", j, "ab"[n]))
                        sp.dma_start(sgab[n][:, :], g_spill[DC * n + j + 1]).then_inc(*s_gl[n].mark(j + 1, by=16))
            elif stage in ("mlp1", "mlp2"):
                one = stage == "mlp1"
                for gi, (f0, fn) in enumerate(groups1 if one else groups2):
                    w0 = W[f"gate{f0}" if one else f"up2_{f0}"]
                    n_up = 2 * fn if one else fn
                    skip = 1 if gi == 0 else 0
                    for s in range(2):
                        w_in_dma[s].known[("before", w0)] = w_in_dma[s].count - (16 if gi == 0 else 0)
                    ups = (a["w_gate"][0], a["w_up"][0]) if one else (a["w_up_2"][0],) * 2
                    with sp.Fori(skip, n_up // 2, 1) as i:
                        for u in range(2):
                            sp.wait_ge(s_wlo.sem, i * 2 + (w0 + u - 1))
                            f = (i + f0) * P if one else (i * 2 + (f0 + u)) * P
                            src = ups[u].rearrange("(k p) m -> p k m", p=P)[:, :, bass.ds(f, P)]
                            sp.dma_start(raw((w0 + u) % 2, DC, P), src).then_inc(w_in_dma[(w0 + u) % 2].sem, 16)
                    for s in range(2):
                        w_in_dma[s].count += 16 * (n_up // 2 - skip)
                    w1 = w0 + n_up
                    for s in range(2):
                        w_in_dma[s].known[("before", w1)] = w_in_dma[s].count
                    down = a["w_down"][0] if one else a["w_down_2"][0]
                    with sp.Fori(0, DC // 2, 1) as i:
                        for u in range(2):
                            sp.wait_ge(s_wlo.sem, i * 2 + (w1 + u - 1))
                            src = down[P * f0:P * (f0 + fn), :].rearrange("(k p) m -> p k m", p=P)[:, :, bass.ds((i * 2 + u) * P, P)]
                            sp.dma_start(raw((w1 + u) % 2, fn, P), src).then_inc(w_in_dma[(w1 + u) % 2].sem, 16)
                    for n in range(DC):
                        s = (w1 + n) % 2
                        w_in_dma[s].known[(w1 + n,)] = w_in_dma[s].count + 16 * (n // 2 + 1)
                    for s in range(2):
                        w_in_dma[s].count += 16 * (DC // 2)
                w2 = w1 + DC
                load(w2)
                load(w2 + 1)
            elif stage == "x1":
                j, = x
                sp.wait_ge(*s_hn.at("x1", j))
                sp.dma_start(x_spill[j], xres[:, j, :]).then_inc(*s_sp[j % 2].mark("x1", j, by=16))
            elif stage == "ss" and x[0] == "attn2":
                sp.wait_ge(*s_dv.at("r of both"))
                for h in range(2):
                    load_bias(sp, h)
            elif stage == "pv" and x[0][0] == "d" and x[0][2] == 3 and x[0][1] < 2:
                h = x[0][1]
                sp.wait_ge(*s_rel.at("sc", *d_steps[h][-1], 1, 1))
                load_bias(sp, h + 2)
            elif stage == "tables" and x[0] == "b2":
                sp.wait_ge(*s_rel.at("sc", *d_steps[3][-1], 1, 1))
                for t, n in ((cosr, "cos_t"), (sinr, "sin_t")):
                    sp.dma_start(t[:, :], a[n]).then_inc(*s_tabl.mark("b2", by=16))
            elif stage == "y2split":
                sp.wait_ge(*s_yl.at("y2", DC - 1))
                for n in range(2):
                    sp.wait_ge(*s_sp[n].at("x1", DC - 2 + n))
                sp.dma_start(xres[:, :, :], x_spill.rearrange("j p t -> p j t")).then_inc(*s_xres.mark("out2", by=16))
            elif stage == "yout":
                j, = x
                sp.wait_ge(*s_rel.at("yout", j))
                sp.dma_start(a["out"][0].rearrange("(i p) d -> p i d", p=P)[:, :, P * j:P * j + P], yst[j % 2][:, :, :]).then_inc(
                    *s_out[j % 2].mark(j, by=16))
        for n in range(2):
            sp.wait_ge(*s_out[n].at(DC - 2 + n))


_INS = ["x", "norm_mix", "w_in", "w_up_a", "w_up_b", "w_out", "norm_ffn", "w_gate", "w_up", "w_down", "norm_final",
        "attn_norm_w_2", "w_in_2", "q_a_norm_w_2", "w_uq_2", "kv_a_norm_w_2", "w_ukv_2", "mla_q_norm_w_2",
        "mla_k_norm_w_2", "diff_q_norm_w_2", "diff_k_norm_w_2", "lambda_q1_2", "lambda_k1_2", "lambda_q2_2",
        "lambda_k2_2", "diff_out_norm_w_2", "w_out_2", "mlp_norm_w_2", "w_up_2", "w_down_2", "rel_bias_2"]


def kernel(**inputs):
    import concourse.bacc as _bacc
    from concourse.bass_utils import run_bass_kernel_spmd as _run

    arrays = {n: np.ascontiguousarray(inputs[n]) for n in _INS}
    arrays |= shape_constants()
    known = {}
    for _ in range(2):
        nc = _bacc.Bacc("TRN2", target_bir_lowering=False, num_devices=1)
        a = {n: nc.dram_tensor(f"in_{n}", v.shape, F32, kind="ExternalInput").ap() for n, v in arrays.items()}
        a["out"] = nc.dram_tensor("out_0", (1, T, D), F32, kind="ExternalOutput").ap()
        emit(nc, known, a)
    r = _run(nc, [{f"in_{n}": v for n, v in arrays.items()}], core_ids=[0])
    return r.results[0]["out_0"]
```
